# Optimizing a Trainium2 kernel written in Bass

```python
import jax, jax.numpy as jnp
from jax import lax
import numpy as np

D_MODEL = 1024
BATCH = 1
SEQ = 512
DEPTH = 2
DEC_BATCH = 1
DEC_SEQ = 32
PAST_LEN = 1024

CHUNK = 64
EPS = 1e-6
GDN_HEADS = 4
GDN_DK = 128
GDN_DV = 128
CONV_WIDTH = 4
GDN_QKV = 2 * GDN_HEADS * GDN_DK + GDN_HEADS * GDN_DV
HGRN_HEADS = 4
HGRN_DK = 64
HGRN_DV = 64
HGRN_KW = HGRN_HEADS * HGRN_DK
MLA_HEADS = 4
Q_LORA = 256
KV_LORA = 128
QK_NOPE = 64
QK_ROPE = 32
V_HEAD = 64
ROPE_THETA = 10000.0
Q_BLOCK = 128
MIX_A = GDN_HEADS * GDN_DV
MIX_B = HGRN_HEADS * HGRN_DV
MIX_C = MLA_HEADS * V_HEAD
MIX_WIDTH = MIX_A + MIX_B + MIX_C
IN_SIZES = (GDN_QKV, MIX_A, GDN_HEADS, GDN_HEADS, HGRN_KW, MIX_B, HGRN_KW, MIX_B, Q_LORA, KV_LORA, QK_ROPE)
P_IN = GDN_QKV + MIX_A + 2 * GDN_HEADS + 2 * HGRN_KW + 2 * MIX_B + Q_LORA + KV_LORA + QK_ROPE
PEER_HEADS = 8
N_KEYS = 128
N_EXPERTS = N_KEYS * N_KEYS
PEER_DKEY = 256
PEER_TOPK = 16
TOKEN_BLOCK = 128

kernel_name = "hybrid_gdn_hgrn2_mla_peer_stream_step"

F32 = jnp.float32

def _offsets(sizes):
    out, acc = [], 0
    for s in sizes[:-1]:
        acc += s
        out.append(acc)
    return out

def rms_norm(x, g):
    xf = x.astype(F32)
    y = xf * lax.rsqrt(jnp.mean(xf * xf, axis=-1, keepdims=True) + EPS)
    return (y * g.astype(F32)).astype(x.dtype)

def l2_norm(x):
    xf = x.astype(F32)
    return (xf * lax.rsqrt(jnp.sum(xf * xf, axis=-1, keepdims=True) + EPS)).astype(x.dtype)

def rope(x, pos):
    half = QK_ROPE // 2
    inv = ROPE_THETA ** (-jnp.arange(half, dtype=F32) / half)
    ang = pos.astype(F32)[:, None] * inv[None, :]
    shp = (ang.shape[0],) + (1,) * (x.ndim - 3) + (half,)
    cos, sin = jnp.cos(ang).reshape(shp), jnp.sin(ang).reshape(shp)
    xf = x.astype(F32)
    x1, x2 = xf[..., :half], xf[..., half:]
    return jnp.concatenate([x1 * cos - x2 * sin, x1 * sin + x2 * cos], axis=-1).astype(x.dtype)

def causal_conv(x, buf, w):
    L = x.shape[1]
    xp = jnp.concatenate([buf.astype(x.dtype), x], axis=1)
    y = xp[:, 0:L] * w[0]
    for j in range(1, CONV_WIDTH):
        y = y + xp[:, j:j + L] * w[j]
    return y, xp[:, -(CONV_WIDTH - 1):]

def _to_chunks(t, n):
    B, L = t.shape[0], t.shape[1]
    pad = n * CHUNK - L
    t = jnp.pad(t, [(0, 0), (0, pad)] + [(0, 0)] * (t.ndim - 2))
    t = t.reshape((B, n, CHUNK) + t.shape[2:])
    perm = (1, 0, 3, 2) + tuple(range(4, t.ndim))
    return t.transpose(perm)

def _from_chunks(o, L):
    n, B, H, C, d = o.shape
    return o.transpose(1, 0, 3, 2, 4).reshape(B, n * C, H, d)[:, :L]

def gated_delta_chunked(q, k, v, g, beta, s0):
    L = q.shape[1]
    n = -(-L // CHUNK)
    qc = _to_chunks(q.astype(F32) * (GDN_DK ** -0.5), n)
    kc = _to_chunks(k.astype(F32), n)
    vc = _to_chunks(v.astype(F32), n)
    gc = jnp.cumsum(_to_chunks(g.astype(F32)[..., None], n)[..., 0], axis=-1)
    bc = _to_chunks(beta.astype(F32)[..., None], n)[..., 0]
    tri = jnp.tril(jnp.ones((CHUNK, CHUNK), bool))
    strict = jnp.tril(jnp.ones((CHUNK, CHUNK), bool), -1)
    diff = gc[..., :, None] - gc[..., None, :]
    decay = jnp.where(tri, jnp.exp(jnp.where(tri, diff, 0.0)), 0.0)
    kb = kc * bc[..., None]
    a_mat = jnp.where(strict, jnp.einsum('nbhtd,nbhsd->nbhts', kb, kc) * decay, 0.0)
    eye = jnp.eye(CHUNK, dtype=F32)
    t_inv = lax.linalg.triangular_solve(a_mat + eye, jnp.broadcast_to(eye, a_mat.shape),
                                        left_side=True, lower=True, unit_diagonal=True)
    u = jnp.einsum('nbhts,nbhsd->nbhtd', t_inv, vc * bc[..., None])
    w = jnp.einsum('nbhts,nbhsd->nbhtd', t_inv, kb * jnp.exp(gc)[..., None])

    def step(S, inp):
        q_i, k_i, u_i, w_i, g_i, dec_i = inp
        v_new = u_i - jnp.einsum('bhtd,bhde->bhte', w_i, S)
        o_inter = jnp.einsum('bhtd,bhde->bhte', q_i * jnp.exp(g_i)[..., None], S)
        attn = jnp.einsum('bhtd,bhsd->bhts', q_i, k_i) * dec_i
        o = o_inter + jnp.einsum('bhts,bhse->bhte', attn, v_new)
        g_last = g_i[..., -1]
        S = S * jnp.exp(g_last)[..., None, None] + jnp.einsum(
            'bhtd,bhte->bhde', k_i * jnp.exp(g_last[..., None] - g_i)[..., None], v_new)
        return S, o

    S, o = lax.scan(step, s0.astype(F32), (qc, kc, u, w, gc, decay))
    return _from_chunks(o, L), S

def hgrn2_chunked(q, k, v, log_f, s0):
    L = q.shape[1]
    n = -(-L // CHUNK)
    qc, kc, vc, fc = (_to_chunks(t.astype(F32), n) for t in (q, k, v, log_f))
    tri = jnp.tril(jnp.ones((CHUNK, CHUNK), bool))[:, :, None]

    def step(S, inp):
        q_i, k_i, v_i, lf = inp
        b = jnp.cumsum(lf, axis=2)
        dec = jnp.exp(jnp.where(tri, b[:, :, :, None, :] - b[:, :, None, :, :], -jnp.inf))
        attn = jnp.einsum('bhtd,bhtsd,bhsd->bhts', q_i, dec, k_i)
        o = jnp.einsum('bhts,bhse->bhte', attn, v_i) + jnp.einsum(
            'bhtd,bhde->bhte', q_i * jnp.exp(b), S)
        b_last = b[:, :, -1]
        S = jnp.exp(b_last)[..., None] * S + jnp.einsum(
            'bhtd,bhte->bhde', k_i * jnp.exp(b_last[:, :, None] - b), v_i)
        return S, o

    S, o = lax.scan(step, s0.astype(F32), (qc, kc, vc, fc))
    return _from_chunks(o, L), S

def chunk_causal_attention(q_nope, q_pe, k_nope, k_pe, v, q_pos, k_pos):
    B, Lq, H, _ = q_nope.shape
    qb = min(Q_BLOCK, Lq)
    nb = Lq // qb
    scale = (QK_NOPE + QK_ROPE) ** -0.5
    k_chunk = k_pos // CHUNK

    def block(args):
        qn, qp, qpos = args
        s = (jnp.einsum('bqhd,bkhd->bhqk', qn, k_nope)
             + jnp.einsum('bqhd,bkd->bhqk', qp, k_pe)).astype(F32) * scale
        mask = k_chunk[None, :] <= (qpos // CHUNK)[:, None]
        p = jax.nn.softmax(jnp.where(mask, s, -jnp.inf), axis=-1).astype(v.dtype)
        return jnp.einsum('bhqk,bkhd->bqhd', p, v)

    qn_b = q_nope.reshape(B, nb, qb, H, QK_NOPE).transpose(1, 0, 2, 3, 4)
    qp_b = q_pe.reshape(B, nb, qb, H, QK_ROPE).transpose(1, 0, 2, 3, 4)
    out = lax.map(block, (qn_b, qp_b, q_pos.reshape(nb, qb)))
    return out.transpose(1, 0, 2, 3, 4).reshape(B, Lq, H, V_HEAD)

def peer(x, w_query, sub_keys, expert_u, expert_v):
    B, L, D = x.shape
    T = B * L
    nb = -(-T // TOKEN_BLOCK)
    t = jnp.pad(x.reshape(T, D), ((0, nb * TOKEN_BLOCK - T), (0, 0))).reshape(nb, TOKEN_BLOCK, D)

    def block(xb):
        q = (xb @ w_query).reshape(TOKEN_BLOCK, PEER_HEADS, 2, PEER_DKEY // 2)
        s = jnp.einsum('thpd,hpnd->thpn', q, sub_keys).astype(F32)
        s_top, i_top = lax.top_k(s, PEER_TOPK)
        cand = s_top[:, :, 0, :, None] + s_top[:, :, 1, None, :]
        cidx = i_top[:, :, 0, :, None] * N_KEYS + i_top[:, :, 1, None, :]
        best, sel = lax.top_k(cand.reshape(TOKEN_BLOCK, PEER_HEADS, PEER_TOPK * PEER_TOPK), PEER_TOPK)
        eidx = jnp.take_along_axis(cidx.reshape(TOKEN_BLOCK, PEER_HEADS, -1), sel, axis=-1)
        gate = jax.nn.softmax(best, axis=-1).reshape(TOKEN_BLOCK, PEER_HEADS * PEER_TOPK)
        eidx = eidx.reshape(TOKEN_BLOCK, PEER_HEADS * PEER_TOPK)
        act = jax.nn.gelu(jnp.einsum('td,ted->te', xb, expert_u[eidx]), approximate=False)
        return jnp.einsum('te,ted->td', gate.astype(xb.dtype) * act, expert_v[eidx])

    y = lax.map(block, t).reshape(nb * TOKEN_BLOCK, D)[:T]
    return y.reshape(B, L, D)

def trunk_layer(x, pos, past_pos, past_ckv, past_kpe, gdn_s0, conv_buf, hgrn_s0, lb, p):
    B, L, _ = x.shape
    h = rms_norm(x, p['norm_mix'])
    (a_qkv, a_z, a_beta, a_alpha, b_f, b_i, b_q, b_g,
     c_qa, c_kva, c_kpe) = jnp.split(h @ p['w_in'], _offsets(IN_SIZES), axis=-1)

    conv, new_conv = causal_conv(a_qkv, conv_buf, p['conv_w'])
    conv = jax.nn.silu(conv)
    aq, ak, av = jnp.split(conv, [GDN_HEADS * GDN_DK, 2 * GDN_HEADS * GDN_DK], axis=-1)
    aq = l2_norm(aq.reshape(B, L, GDN_HEADS, GDN_DK))
    ak = l2_norm(ak.reshape(B, L, GDN_HEADS, GDN_DK))
    av = av.reshape(B, L, GDN_HEADS, GDN_DV)
    beta = jax.nn.sigmoid(a_beta.astype(F32))
    g = -jnp.exp(p['gdn_a_log'].astype(F32)) * jax.nn.softplus(a_alpha.astype(F32) + p['gdn_dt_bias'].astype(F32))
    o_a, new_gdn = gated_delta_chunked(aq, ak, av, g, beta, gdn_s0)
    o_a = rms_norm(o_a.astype(x.dtype), p['gdn_norm']) * jax.nn.silu(a_z.reshape(B, L, GDN_HEADS, GDN_DV))

    zf = b_f.astype(F32).reshape(B, L, HGRN_HEADS, HGRN_DK)
    lbh = lb.reshape(HGRN_HEADS, HGRN_DK)
    log_f = jnp.logaddexp(jnp.log(lbh), jnp.log1p(-lbh) + jax.nn.log_sigmoid(zf))
    k_b = (1.0 - lbh) * jax.nn.sigmoid(-zf)
    q_b = jax.nn.silu(b_q).reshape(B, L, HGRN_HEADS, HGRN_DK)
    o_b, new_hgrn = hgrn2_chunked(q_b, k_b, b_i.reshape(B, L, HGRN_HEADS, HGRN_DV), log_f, hgrn_s0)
    o_b = rms_norm(o_b.astype(x.dtype), p['hgrn_norm']) * jax.nn.silu(b_g.reshape(B, L, HGRN_HEADS, HGRN_DV))

    qc = (rms_norm(c_qa, p['mla_q_a_norm']) @ p['mla_w_q_b']).reshape(B, L, MLA_HEADS, QK_NOPE + QK_ROPE)
    q_nope = rms_norm(qc[..., :QK_NOPE], p['mla_q_norm_nope'])
    q_pe = rope(rms_norm(qc[..., QK_NOPE:], p['mla_q_norm_rope']), pos)
    ckv = rms_norm(c_kva, p['mla_kv_a_norm'])
    kpe = rope(rms_norm(c_kpe, p['mla_k_norm_rope']), pos)
    all_ckv = jnp.concatenate([past_ckv.astype(x.dtype), ckv], axis=1)
    all_kpe = jnp.concatenate([past_kpe.astype(x.dtype), kpe], axis=1)
    k_pos = jnp.concatenate([past_pos, pos])
    kv = (all_ckv @ p['mla_w_kv_b']).reshape(B, all_ckv.shape[1], MLA_HEADS, QK_NOPE + V_HEAD)
    k_nope = rms_norm(kv[..., :QK_NOPE], p['mla_k_norm_nope'])
    o_c = chunk_causal_attention(q_nope, q_pe, k_nope, all_kpe, kv[..., QK_NOPE:], pos, k_pos)

    mixed = jnp.concatenate([o_a.reshape(B, L, MIX_A), o_b.reshape(B, L, MIX_B),
                             o_c.reshape(B, L, MIX_C)], axis=-1) @ p['w_out']
    x = x + mixed
    x = x + peer(rms_norm(x, p['norm_ffn']), p['peer_w_query'], p['peer_sub_keys'],
                 p['peer_expert_u'], p['peer_expert_v'])
    return x, new_gdn, new_conv, new_hgrn, ckv, kpe

def setup_inputs(seed: int = 0) -> dict:
    key = jax.random.key(seed)
    ks = jax.random.split(key, 32)

    def nrm(k, shape, s):
        return jax.random.normal(k, shape, F32) * s

    def gain(k, shape):
        return 1.0 + 0.01 * jax.random.normal(k, shape, F32)

    return {
        'x_prompt': nrm(ks[0], (BATCH, SEQ, D_MODEL), 1.0),
        'x_sample': nrm(ks[1], (DEC_BATCH, DEC_SEQ, D_MODEL), 1.0),
        'state_gdn': nrm(ks[2], (DEPTH, DEC_BATCH, GDN_HEADS, GDN_DK, GDN_DV), 0.5),
        'state_gdn_conv': nrm(ks[3], (DEPTH, DEC_BATCH, CONV_WIDTH - 1, GDN_QKV), 1.0),
        'state_hgrn': nrm(ks[4], (DEPTH, DEC_BATCH, HGRN_HEADS, HGRN_DK, HGRN_DV), 0.5),
        'cache_mla_ckv': nrm(ks[5], (DEPTH, DEC_BATCH, PAST_LEN, KV_LORA), 1.0),
        'cache_mla_kpe': nrm(ks[6], (DEPTH, DEC_BATCH, PAST_LEN, QK_ROPE), 1.0),
        'norm_mix': gain(ks[7], (DEPTH, D_MODEL)),
        'w_in': nrm(ks[8], (DEPTH, D_MODEL, P_IN), D_MODEL ** -0.5),
        'conv_w': nrm(ks[9], (DEPTH, CONV_WIDTH, GDN_QKV), 0.5),
        'gdn_a_log': jnp.log(jax.random.uniform(ks[10], (DEPTH, GDN_HEADS), F32, 1.0, 16.0)),
        'gdn_dt_bias': nrm(ks[11], (DEPTH, GDN_HEADS), 0.1),
        'gdn_norm': gain(ks[12], (DEPTH, GDN_DV)),
        'hgrn_lower_bounds': nrm(ks[13], (DEPTH, HGRN_KW), 0.1),
        'hgrn_norm': gain(ks[14], (DEPTH, HGRN_DV)),
        'mla_q_a_norm': gain(ks[15], (DEPTH, Q_LORA)),
        'mla_w_q_b': nrm(ks[16], (DEPTH, Q_LORA, MLA_HEADS * (QK_NOPE + QK_ROPE)), Q_LORA ** -0.5),
        'mla_kv_a_norm': gain(ks[17], (DEPTH, KV_LORA)),
        'mla_w_kv_b': nrm(ks[18], (DEPTH, KV_LORA, MLA_HEADS * (QK_NOPE + V_HEAD)), KV_LORA ** -0.5),
        'mla_q_norm_nope': gain(ks[19], (DEPTH, QK_NOPE)),
        'mla_q_norm_rope': gain(ks[20], (DEPTH, QK_ROPE)),
        'mla_k_norm_nope': gain(ks[21], (DEPTH, QK_NOPE)),
        'mla_k_norm_rope': gain(ks[22], (DEPTH, QK_ROPE)),
        'w_out': nrm(ks[23], (DEPTH, MIX_WIDTH, D_MODEL), MIX_WIDTH ** -0.5),
        'norm_ffn': gain(ks[24], (DEPTH, D_MODEL)),
        'peer_w_query': nrm(ks[25], (DEPTH, D_MODEL, PEER_HEADS * PEER_DKEY), D_MODEL ** -0.5),
        'peer_sub_keys': nrm(ks[26], (DEPTH, PEER_HEADS, 2, N_KEYS, PEER_DKEY // 2), (PEER_DKEY // 2) ** -0.5),
        'peer_expert_u': nrm(ks[27], (DEPTH, N_EXPERTS, D_MODEL), D_MODEL ** -0.5),
        'peer_expert_v': nrm(ks[28], (DEPTH, N_EXPERTS, D_MODEL), 0.25),
    }

def reference(x_prompt, x_sample, state_gdn, state_gdn_conv, state_hgrn, cache_mla_ckv, cache_mla_kpe,
              norm_mix, w_in, conv_w, gdn_a_log, gdn_dt_bias, gdn_norm, hgrn_lower_bounds, hgrn_norm,
              mla_q_a_norm, mla_w_q_b, mla_kv_a_norm, mla_w_kv_b, mla_q_norm_nope, mla_q_norm_rope,
              mla_k_norm_nope, mla_k_norm_rope, w_out, norm_ffn, peer_w_query, peer_sub_keys,
              peer_expert_u, peer_expert_v):
    dt = x_prompt.dtype
    Bp, Lp = x_prompt.shape[0], x_prompt.shape[1]
    Ls = x_sample.shape[1]
    past_len = cache_mla_ckv.shape[2]
    pos_p = jnp.arange(Lp, dtype=jnp.int32)
    pos_s = past_len + jnp.arange(Ls, dtype=jnp.int32)
    past_pos_s = jnp.arange(past_len, dtype=jnp.int32)
    past_pos_p = jnp.zeros((0,), jnp.int32)
    lb_all = jnp.cumsum(jax.nn.softmax(hgrn_lower_bounds.astype(F32), axis=0), axis=0)
    lb_all = lb_all - lb_all[0:1]

    yp, ys = x_prompt, x_sample
    pg, pc, ph, pk, pr = [], [], [], [], []
    sg, sc, sh, sk, sr = [], [], [], [], []
    for l in range(DEPTH):
        p = {'norm_mix': norm_mix[l], 'w_in': w_in[l], 'conv_w': conv_w[l], 'gdn_a_log': gdn_a_log[l],
             'gdn_dt_bias': gdn_dt_bias[l], 'gdn_norm': gdn_norm[l], 'hgrn_norm': hgrn_norm[l],
             'mla_q_a_norm': mla_q_a_norm[l], 'mla_w_q_b': mla_w_q_b[l], 'mla_kv_a_norm': mla_kv_a_norm[l],
             'mla_w_kv_b': mla_w_kv_b[l], 'mla_q_norm_nope': mla_q_norm_nope[l],
             'mla_q_norm_rope': mla_q_norm_rope[l], 'mla_k_norm_nope': mla_k_norm_nope[l],
             'mla_k_norm_rope': mla_k_norm_rope[l], 'w_out': w_out[l], 'norm_ffn': norm_ffn[l],
             'peer_w_query': peer_w_query[l], 'peer_sub_keys': peer_sub_keys[l],
             'peer_expert_u': peer_expert_u[l], 'peer_expert_v': peer_expert_v[l]}
        yp, g_p, c_p, h_p, k_p, r_p = trunk_layer(
            yp, pos_p, past_pos_p,
            jnp.zeros((Bp, 0, KV_LORA), dt), jnp.zeros((Bp, 0, QK_ROPE), dt),
            jnp.zeros((Bp, GDN_HEADS, GDN_DK, GDN_DV), F32), jnp.zeros((Bp, CONV_WIDTH - 1, GDN_QKV), dt),
            jnp.zeros((Bp, HGRN_HEADS, HGRN_DK, HGRN_DV), F32), lb_all[l], p)
        ys, g_s, c_s, h_s, k_s, r_s = trunk_layer(
            ys, pos_s, past_pos_s, cache_mla_ckv[l], cache_mla_kpe[l],
            state_gdn[l], state_gdn_conv[l], state_hgrn[l], lb_all[l], p)
        pg.append(g_p.astype(dt)); pc.append(c_p.astype(dt)); ph.append(h_p.astype(dt))
        pk.append(k_p.astype(dt)); pr.append(r_p.astype(dt))
        sg.append(g_s.astype(dt)); sc.append(c_s.astype(dt)); sh.append(h_s.astype(dt))
        sk.append(k_s.astype(dt)); sr.append(r_s.astype(dt))

    return (yp, ys,
            jnp.stack(pg), jnp.stack(pc), jnp.stack(ph), jnp.stack(pk), jnp.stack(pr),
            jnp.stack(sg), jnp.stack(sc), jnp.stack(sh), jnp.stack(sk), jnp.stack(sr))


_drawn_inputs = setup_inputs


def setup_inputs(seed=0):
    import zlib

    import numpy as np

    out = dict(_drawn_inputs(seed))
    spreads = {}
    factors = {'norm_mix': 2.705,
     'gdn_dt_bias': 3.588,
     'gdn_norm': 12.356,
     'hgrn_norm': 13.384,
     'mla_q_a_norm': 8.0,
     'mla_kv_a_norm': 5.828,
     'mla_q_norm_nope': 8.0,
     'mla_q_norm_rope': 24.689,
     'mla_k_norm_nope': 8.0,
     'mla_k_norm_rope': 20.073,
     'norm_ffn': 14.325,
     'state_hgrn': 2.879}
    for name, (base, spread) in spreads.items():
        noise = np.random.default_rng([zlib.crc32(name.encode()), seed]).standard_normal(out[name].shape)
        drawn = base * np.exp(spread * noise) if base else spread * noise
        out[name] = __import__('jax').numpy.asarray(drawn.astype(out[name].dtype))
    for name, factor in factors.items():
        out[name] = (out[name] * factor).astype(out[name].dtype)
    return out
```

```python
from contextlib import ExitStack

import numpy as np

import concourse.bass as bass
from concourse import mybir

ALU = mybir.AluOpType
ACT = mybir.ActivationFunctionType
AX = mybir.AxisListType
F32 = mybir.dt.float32
U32 = mybir.dt.uint32

P = 128
DEPTH, D, SEQ, DEC, PAST = 2, 1024, 512, 32, 1024
NT = SEQ // P + 1
TP = NT * P
TV = SEQ + DEC
KC = D // P
EPS = 1e-6
C = 64
GH = 4
QKV = 1536
NJ = QKV // P
PIN = 3496
VALS = 50
EH = 8
EXPERTS = 16384
SCALE = 96 ** -0.5
GROUPS = (4 * P + DEC) // 4

W_Z, W_BA, W_BF, W_BI, W_BQ, W_BG, W_C = 1536, 2048, 2056, 2312, 2568, 2824, 3080
T_Z, T_V, T_G, T_C, T_BA, TM = 0, 512, 768, 1024, 1440, 1448
CH_COLS = [j * P for j in range(NJ)] + [W_BF, W_BF + P, W_BQ, W_BQ + P]
TM_GROUPS = [(W_Z, 512, T_Z, 0), (W_BI, 256, T_V, 4096), (W_BG, 256, T_G, 6144), (W_C, 416, T_C, 0),
             (W_BA, 8, T_BA, 8192)]
MIX_COLS = [0, 128, 256, 384, 768, 896, 1024, 1152]
PAIR_ROWS = [(0, 1, 16), (1, 1, 8), (2, 1, 5), (3, 1, 4), (4, 1, 3), (5, 3, 2), (8, 8, 1)]


def constants():
    s, t = np.arange(P)[:, None], np.arange(P)[None, :]
    same = (s // C) == (t // C)
    parts = {
        "ident": s == t, "ones": np.ones((P, P)), "upto": same & (s <= t), "after": same & (s > t),
        "chunk0": (s < C) & (t >= 0), "chunk1": (s >= C) & (t >= 0), "diagonal": same,
    }
    for b in (1, 2, 4, 8, 16, 32):
        parts[f"half{b}"] = (s // (2 * b) == t // (2 * b)) & (s % (2 * b) < b) & (t % (2 * b) >= b)
    parts["half1t"] = parts["half1"].T
    parts["carry"] = (np.arange(TP)[None, :] % C != 0) & (s >= 0)
    inv = (np.float32(10000.0) ** (-np.arange(16, dtype=np.float32) / np.float32(16))).astype(np.float32)
    pos = np.arange(P)[:, None] + P * np.arange(NT)[None, :]
    pos[:, NT - 1] = PAST + np.arange(P)
    ang = (pos.astype(np.float32)[:, :, None] * inv).astype(np.float32)
    parts["cos"], parts["sin"] = np.cos(ang).reshape(P, -1), np.sin(ang).reshape(P, -1)
    valid = np.ones((P, NT))
    valid[DEC:, NT - 1] = 0
    parts["valid"] = valid
    parts["eps"] = np.full((P, 1), EPS)
    parts["early"] = (t < C) & (s >= 0)
    parts["late"] = np.where(t >= C, -1e30, 0.0) * (s >= 0)
    parts["fold"] = s % DEC == np.arange(DEC)[None, :]
    parts["iota"] = np.arange(VALS)[None, :] * np.ones((P, 1))
    at, off = {}, 0
    for k, v in parts.items():
        at[k] = (off, v.shape[1])
        off += v.shape[1]
    return np.concatenate([v.astype(np.float32) for v in parts.values()], axis=1), at


class Count:

    def __init__(self):
        self.n = 0

    def up(self):
        self.n += 1
        return 1


def build(nc, i, o, at, ncols):
    with ExitStack() as ctx:
        def sb(name, cols, dt=F32):
            return ctx.enter_context(nc.sbuf_tensor(name, [P, cols], dt))

        sems = []

        def sem(name, cleared=True):
            s = ctx.enter_context(nc.semaphore(name))
            if cleared:
                sems.append(s)
            return s

        ps = ctx.enter_context(nc.psum_tensor("ps", [P, 8, 512], F32))
        x = sb("x", NT * D)[:, :].rearrange("p (t d) -> p t d", t=NT)
        region_h = sb("region_h", 5120)
        region_t = sb("region_t", NT * TM)
        region_c = sb("region_c", 8192)
        region_w = sb("region_w", 3072)
        arena = sb("arena", 12288)
        cst = sb("cst", ncols)
        gain = sb("gain", D)
        region_v = sb("region_v", 2304)
        raw = [sb(f"raw{k}", 550) for k in range(2)]
        small = sb("small", 1500)

        used = [0]

        def piece(n):
            used[0] += n
            assert used[0] <= 1500
            return small[:, used[0] - n:used[0]]

        def const(name):
            a, n = at[name]
            return cst[:, a:a + n]

        ident, ones, upto = const("ident"), const("ones"), const("upto")
        hT = region_h[:, :].rearrange("p (c t) -> p c t", c=KC)
        tm = region_t[:, :].rearrange("p (t n) -> p t n", t=NT)
        xb = region_t[:, 0:NT * D].rearrange("p (t n) -> p t n", t=NT)
        conv = region_c[:, 0:NJ * TP].rearrange("p (j t) -> p j t", j=NJ)
        wcol = [region_w[:, k * D:(k + 1) * D] for k in range(3)]
        zf = arena[:, 9728:11008]
        qh = arena[:, 11008:12288]
        conv_y = [arena[:, 8256 + k * 547:8256 + (k + 1) * 547] for k in range(2)]

        sumsq, rs = piece(NT), piece(NT)
        wh = piece(NJ * 7).rearrange("p (j w) -> p j w", j=NJ)
        tails = piece(NJ * 6).rearrange("p (j w) -> p j w", j=NJ)
        lb_rows = piece(4).rearrange("p (l r) -> p l r", l=2)
        lb_all = piece(12).rearrange("p (l r) -> p l r", l=2)
        lb = piece(6)
        lb_t = piece(8)
        gdn_par = piece(8)
        gdn_gain, hgrn_gain = piece(128), piece(64)
        lora_gain = piece(416)
        knope_gain, qnope_gain, qrope_gain = piece(64), piece(64), piece(32)
        ebase = piece(1)
        gate_n = NT * GH
        beta, gg, gcs, egc, begc, erest = (piece(gate_n) for _ in range(6))
        egl = piece(2 * gate_n)
        gt = piece(gate_n)
        ebl = piece(20)
        ss = piece(16)
        sr = piece(16)
        mx, nm, sume, rsum = piece(4), piece(4), piece(4), piece(4)

        shared = [ctx.enter_context(nc.semaphore(f"shared{k}")) for k in range(64)]

        def named(text):
            names = text.split()
            assert len(names) <= len(shared)
            return type("Phase", (), dict(zip(names, shared)))

        start_loaded = ctx.enter_context(nc.semaphore("start_loaded"))
        start_set = ctx.enter_context(nc.semaphore("start_set"))
        met = ctx.enter_context(nc.semaphore("phase_met"))
        start_act = ctx.enter_context(nc.semaphore("start_act"))
        layer_arrive = ctx.enter_context(nc.semaphore("layer_arrive"))
        layer_cleared = ctx.enter_context(nc.semaphore("layer_cleared"))
        u_loaded = [ctx.enter_context(nc.semaphore(f"u_loaded{k}")) for k in range(4)]
        v_loaded = [ctx.enter_context(nc.semaphore(f"v_loaded{k}")) for k in range(4)]
        passed = ctx.enter_context(nc.semaphore("passed"))
        turn = ctx.enter_context(nc.semaphore("turn"))
        y_out = ctx.enter_context(nc.semaphore("y_out"))

        def meet(eng, k):
            if eng.engine == nc.sync.engine:
                eng.wait_ge(met, 5 * k - 1)
                for s in shared:
                    eng.sem_clear(s)
                eng.sem_inc(met, 1)
            else:
                eng.drain().then_inc(met, 1)
            eng.wait_ge(met, 5 * k)
            eng.sem_inc(passed, 1)

        def next_layer(eng, l):
            if eng.engine == nc.sync.engine:
                eng.wait_ge(layer_arrive, l * 4 + 4)
                eng.sem_inc(turn, 1)
                eng.sem_clear(met)
                eng.sem_clear(turn)
                eng.sem_inc(layer_cleared, 1)
            else:
                eng.sem_inc(layer_arrive, 1)
                eng.wait_ge(layer_cleared, l + 1)
                eng.sem_inc(passed, 1)

        def tok(t):
            return slice(t * P, (t + 1) * P)

        def half(c):
            return slice(c * C, (c + 1) * C)

        def heads(ap, m=P):
            return ap.unsqueeze(2).to_broadcast([ap.shape[0], ap.shape[1], m])

        def per_head(ap, h=GH):
            return ap.unsqueeze(1).to_broadcast([ap.shape[0], h, ap.shape[1]])

        def span(region, start, cols):
            return region[:, start:start + cols]

        zeros = piece(P)
        sr2 = piece(16)
        B, E, QE, KE = (span(arena, k * 1280, 1280) for k in range(4))
        hattn = span(arena, 5120, 2560).rearrange("p (t h s) -> p t h s", t=NT, h=4)
        hs = span(arena, 7680, 256).rearrange("p (r e) -> p r e", r=2)
        hs_init = span(arena, 7936, 256)
        hs_out = span(arena, 8192, 512).rearrange("p (k r e) -> p k r e", k=2, r=2)
        hds = span(arena, 8704, 256)
        kdt = span(region_v, 0, 512).rearrange("p (k n) -> p k n", k=2)
        hosq = span(region_v, 512, 256)
        hgg = span(region_v, 768, 256)
        (DT, EG, QG, AT, GD, A, ATF, AM0, AM1, X, XT, Y, VB, KB, KD, NW, VN, S, OSQ, ZG, ug, gs_init) = (
            span(arena, k * 512, 512) for k in range(22))
        AM = [AM0, AM1]
        gs_out = span(region_v, 0, 1024).rearrange("p (k n) -> p k n", k=2)
        gsq = [span(region_v, 1024, 544), span(region_v, 1024 + 544, 544)]
        grs = [span(region_w, 0, 544), span(region_w, 544, 544)]
        wqb = span(arena, 0, 768).rearrange("p (c n) -> p c n", c=2)
        wkvb = span(arena, 768, 512)
        past_c = span(arena, 1280, 1024).rearrange("p (t n) -> p t n", t=8)
        past_k = span(arena, 2304, 256).rearrange("p (t n) -> p t n", t=8)
        qaT = span(arena, 2560, 256)
        ckvT = span(arena, 2816, 128)
        K = span(arena, 2944, 384).rearrange("p (h n) -> p h n", h=4)
        Qh = span(arena, 3328, 384).rearrange("p (h n) -> p h n", h=4)
        QT = span(arena, 3712, 512).rearrange("p (h n) -> p h n", h=4)
        pr = span(arena, 4224, 1056)
        pT = span(arena, 5280, 1152)
        csq = span(arena, 6432, 2080).rearrange("p (t n) -> p t n", t=NT)
        rot = span(arena, 8512, 320)
        ksq = span(arena, 8832, 256)
        qsq = span(arena, 9088, 384)
        KTp = span(region_w, 0, 2048).rearrange("p (h n) -> p h n", h=4)
        Vp = span(region_w, 2048, 1024).rearrange("p (t n) -> p t n", t=4)
        KTs = span(region_h, 0, 4 * 1056).rearrange("p (h n) -> p h n", h=4)
        Vs = span(region_v, 0, 2304).rearrange("p (t n) -> p t n", t=9)
        kv_tiles = ([(tm[:, t, T_C + 256:T_C + 384], P, tm[:, t, T_C + 384:T_C + 416]) for t in range(4)]
                    + [(past_c[:, t, :], P, past_k[:, t, :]) for t in range(8)]
                    + [(tm[0:DEC, 4, T_C + 256:T_C + 384], DEC, tm[0:DEC, 4, T_C + 384:T_C + 416])])
        w_out_sb = [span(arena, k * 4096, 4096).rearrange("p (c n) -> p c n", c=KC) for k in range(2)]
        mT = [span(region_c, k * 1024, 1024) for k in range(2)]
        keys = span(arena, 0, 2048).rearrange("p (j n) -> p j n", j=16)
        keysT = span(arena, 2048, 2048).rearrange("p (j n) -> p j n", j=16)
        qT = [span(arena, 4096, 544), span(arena, 4640, 544)]
        top = span(arena, 5184, 1280).rearrange("p (t h s a) -> p t h s a", t=NT, h=EH, s=2)
        top_i = span(arena, 6464, 1280).bitcast(U32).rearrange("p (t h s a) -> p t h s a", t=NT, h=EH, s=2)
        top_f = span(arena, 7744, 1280).rearrange("p (t h s a) -> p t h s a", t=NT, h=EH, s=2)
        work = [span(arena, 9024, 128), span(arena, 9152, 128)]
        pairs, pairs_left = span(arena, 0, VALS), span(arena, 64, VALS)
        best = span(arena, 128, 16)
        sel = span(arena, 144, 16).bitcast(U32)
        sel_f, expert = span(arena, 160, 16), span(arena, 176, 16)
        onehot = span(arena, 192, 16 * VALS).rearrange("p (a n) -> p a n", a=16)
        eid_s = span(arena, 1024, DEC).bitcast(U32)
        gate_s = span(arena, 1024 + DEC, DEC)
        xs = gain[:, :]
        cand = span(arena, 9280, EH * VALS)
        cidx = span(arena, 9680, EH * VALS)
        eid = span(arena, 10464, NT * P).bitcast(U32)
        gate = span(arena, 11104, NT * P)
        diag = [span(arena, 11744 + k * P, P) for k in range(4)]
        dots = span(region_v, 0, NT * P)
        wts = span(region_v, 640, NT * P)
        act = span(region_v, 1280, P)
        uidx = [span(region_v, 1408 + 8 * k, 4).bitcast(U32) for k in range(2)]
        vidx = [span(region_v, 1412 + 8 * k, 4).bitcast(U32) for k in range(2)]
        gsum = span(region_v, 1424, EH)
        ring = [span(region_c, k * D, D) for k in range(8)]

        project = named("gain_ready sumsq_ready rs_ready xb_ready h_banks h_copy_v h_copy_a params_ready rows_ready wcol_used "
                        "wc0 wc1 wc2 tm_used wt0 wt1 wt2 wt3 wt4 wh_bank wh_ready col_bank col_read tm_bank tm_read_a tm_read_v "
                        "tails_in tail_bank tail_ready tail_out raw_ready y_ready silu_done v_done a_done zero_set")
        project.wcol_ready = [project.wc0, project.wc1, project.wc2]
        project.wtm_ready = [project.wt0, project.wt1, project.wt2, project.wt3, project.wt4]
        hgrn = named("init_zero init_ready s_saved state_out qe_ready ke_ready lev_bank lev_read decayed kd_bank kd_ready o_scaled "
                     "s_ready o_bank ds_bank v_done a_done e1 lsig nlsig k_ready bprime ad lf scanned diff ediff eb ed mult_ready "
                     "osq oss ors gg_ready ebl_ready p_done o_done")
        gdn = named("init_ready s_saved state_out square_ready sum_bank sum_read gate_ready gates_bank gates_ready qk_ready ug_ready "
                    "row_bank gram_bank kv_bank gd_ready gdt_bank a_ready at_bank kv_read am_ready x_ready y_ready y_bank xx_bank "
                    "t_ready w_bank w_ready qg_ready s_ready vn_bank vn_ready ds_bank o_bank o_scaled v_done a_done norm_ready "
                    "soft gexp_ready eg_ready diff_ready edt_ready dtm_ready atf_ready osq oss ors zg_ready bexp alpha nega o_done")
        mla = named("loads latent_ready latent_out ckvT_ready ckvT_bank k_ready v_ready kv_bank kT_ready kT_bank qaT_ready qaT_bank "
                    "q_ready q_bank qT_ready qT_bank p_ready s_bank pT_ready pT_bank o_ready o_bank pn_ready v_done a_done "
                    "csq css crs ksq kss krs qsq qss qrs nm psum_ready")
        outp = named("w0 w1 copy_v copy_a t_banks x_ready o_bank")
        outp.w_ready = [outp.w0, outp.w1]
        peer = named("gain_ready sumsq_ready rs_ready xb_ready h_banks h_copy_v h_copy_a wcol_used wc0 wc1 wc2 keys_loaded "
                     "keys_bank keys_ready q_ready s_bank top_done q_bank acc_read diag_ready v_free acc_bank u_free "
                     "v_done a_done idx_ready pair_ready pair_used eid_ready dots_ready act_ready wts_ready diag_free bests gexp "
                     "p_done pe_done ids_u ids_v spread_x spread_e spread_g gate_done sel_step turn_v")
        peer.wcol_ready = [peer.wc0, peer.wc1, peer.wc2]
        peer.u_loaded, peer.v_loaded = u_loaded, v_loaded
        block = ctx.enter_context(nc.Block())
        def norm_loads(sp, q, l, weights):
            sp.dma_start(gain[:, :], weights[bass.ds(l, 1), :].to_broadcast([P, D])).then_inc(q.gain_ready, 16)

        def project_loads(sp, l):
            q = project
            norm_loads(sp, q, l, i.norm_mix)
            sp.dma_start(region_v[0:4, 0:QKV], i.conv_w[bass.ds(l, 1), :, :].rearrange("o w n -> (o w) n")).then_inc(q.rows_ready, 16)
            sp.dma_start(region_v[4:7, 0:QKV], i.state_gdn_conv[bass.ds(l, 1), 0, :, :].rearrange("o w n -> (o w) n")).then_inc(q.rows_ready, 16)
            small_loads = [
                (gdn_par[:, 0:4], i.gdn_a_log, GH), (gdn_par[:, 4:8], i.gdn_dt_bias, GH), (gdn_gain, i.gdn_norm, P),
                (hgrn_gain, i.hgrn_norm, C), (lora_gain[:, 0:256], i.mla_q_a_norm, 256),
                (lora_gain[:, 256:384], i.mla_kv_a_norm, 128), (lora_gain[:, 384:416], i.mla_k_norm_rope, 32),
                (knope_gain, i.mla_k_norm_nope, C), (qnope_gain, i.mla_q_norm_nope, C), (qrope_gain, i.mla_q_norm_rope, 32)]
            for dst, src, m in small_loads:
                sp.dma_start(dst, src[bass.ds(l, 1), :].to_broadcast([P, m])).then_inc(q.params_ready, 16)
            for j, col in enumerate(CH_COLS):
                if j >= 3:
                    sp.wait_ge(q.wcol_used, j - 2)
                sp.dma_start(wcol[j % 3].rearrange("p (c n) -> p c n", c=KC),
                             i.w_in[bass.ds(l, 1), :, col:col + P].rearrange("o (c p) n -> p (o c) n", p=P)).then_inc(q.wcol_ready[j % 3], 16)
            for g, (col, m, _, at_) in enumerate(TM_GROUPS):
                if g == 3:
                    sp.wait_ge(q.tm_used, 1)
                sp.dma_start(arena[:, at_:at_ + KC * m].rearrange("p (c n) -> p c n", c=KC),
                             i.w_in[bass.ds(l, 1), :, col:col + m].rearrange("o (c p) n -> p (o c) n", p=P)).then_inc(q.wtm_ready[g], 16)
            sp.wait_ge(q.tail_ready, 1)
            sp.dma_start(o.p_conv[bass.ds(l, 1), 0, :, :].rearrange("o w n -> (o w) n"), region_v[0:3, 0:QKV]).then_inc(q.tail_out, 16)
            sp.dma_start(o.s_conv[bass.ds(l, 1), 0, :, :].rearrange("o w n -> (o w) n"), region_v[3:6, 0:QKV]).then_inc(q.tail_out, 16)
            sp.wait_ge(q.params_ready, 16 * len(small_loads))
            sp.wait_ge(q.tail_out, 32)

        def hgrn_loads(sp, l):
            q = hgrn
            sp.wait_ge(q.init_zero, 1)
            for h in range(4):
                sp.dma_start(hs_init[half(h % 2), h // 2 * P + h % 2 * C:h // 2 * P + h % 2 * C + C],
                             i.state_hgrn[bass.ds(l, 1), 0, h, :, :].rearrange("o a b -> (o a) b")).then_inc(q.init_ready, 16)
            for k, (dst, at_) in enumerate(((o.p_hgrn, 1), (o.s_hgrn, 2))):
                sp.wait_ge(q.s_saved, at_)
                for h in range(4):
                    sp.dma_start(dst[bass.ds(l, 1), 0, h, :, :].rearrange("o a b -> (o a) b"),
                                 hs_out[half(h % 2), k, h // 2, h % 2 * C:h % 2 * C + C]).then_inc(q.state_out, 16)
            sp.wait_ge(q.state_out, 8 * 16)

        def gdn_loads(sp, l):
            q = gdn
            sp.dma_start(gs_init[:, :].rearrange("p (h e) -> p h e", h=GH),
                         i.state_gdn[bass.ds(l, 1), 0, :, :, :].rearrange("o h a b -> a (o h) b")).then_inc(q.init_ready, 16)
            for k, dst in enumerate((o.p_gdn, o.s_gdn)):
                sp.wait_ge(q.s_saved, k + 1)
                sp.dma_start(dst[bass.ds(l, 1), 0, :, :, :].rearrange("o h a b -> a (o h) b"),
                             gs_out[:, k, :].rearrange("p (h e) -> p h e", h=GH)).then_inc(q.state_out, 16)
            sp.wait_ge(q.state_out, 32)

        def mla_loads(sp, l):
            q = mla
            sp.dma_start(wqb[:, :, :], i.mla_w_q_b[bass.ds(l, 1), :, :].rearrange("o (c p) n -> p (o c) n", p=P)).then_inc(q.loads, 16)
            sp.dma_start(wkvb, i.mla_w_kv_b[bass.ds(l, 1), :, :].rearrange("o p n -> p (o n)")).then_inc(q.loads, 16)
            sp.dma_start(past_c[:, :, :], i.cache_mla_ckv[bass.ds(l, 1), 0, :, :].rearrange("o (t p) n -> p (o t) n", p=P)).then_inc(q.loads, 16)
            sp.dma_start(past_k[:, :, :], i.cache_mla_kpe[bass.ds(l, 1), 0, :, :].rearrange("o (t p) n -> p (o t) n", p=P)).then_inc(q.loads, 16)
            sp.wait_ge(q.latent_ready, 1)
            sp.dma_start(o.p_ckv[bass.ds(l, 1), 0, :, :].rearrange("o (t p) n -> p (o t) n", p=P), tm[:, 0:4, T_C + 256:T_C + 384]).then_inc(q.latent_out, 16)
            sp.dma_start(o.p_kpe[bass.ds(l, 1), 0, :, :].rearrange("o (t p) n -> p (o t) n", p=P), tm[:, 0:4, T_C + 384:T_C + 416]).then_inc(q.latent_out, 16)
            sp.dma_start(o.s_ckv[bass.ds(l, 1), 0, :, :].rearrange("o p n -> p (o n)"), tm[0:DEC, 4, T_C + 256:T_C + 384]).then_inc(q.latent_out, 16)
            sp.dma_start(o.s_kpe[bass.ds(l, 1), 0, :, :].rearrange("o p n -> p (o n)"), tm[0:DEC, 4, T_C + 384:T_C + 416]).then_inc(q.latent_out, 16)
            sp.wait_ge(q.latent_out, 64)

        def out_loads(sp, l):
            q = outp
            for k in range(2):
                sp.dma_start(w_out_sb[k], i.w_out[bass.ds(l, 1), :, k * 512:(k + 1) * 512].rearrange("o (c p) n -> p (o c) n", p=P)).then_inc(q.w_ready[k], 16)

        def peer_loads(sp, l):
            q = peer
            norm_loads(sp, q, l, i.norm_ffn)
            for k in range(2):
                sp.dma_start(keys[:, 8 * k:8 * k + 8, :], i.peer_sub_keys[bass.ds(l, 1), 4 * k:4 * k + 4, :, :, :].rearrange("o h s n d -> n (o h s) d")).then_inc(q.keys_loaded, 16)
            for j in range(16):
                if j >= 3:
                    sp.wait_ge(q.wcol_used, j - 2)
                sp.dma_start(wcol[j % 3].rearrange("p (c n) -> p c n", c=KC),
                             i.peer_w_query[bass.ds(l, 1), :, j * P:(j + 1) * P].rearrange("o (c p) n -> p (o c) n", p=P)).then_inc(q.wcol_ready[j % 3], 16)

        def peer_spread(sp):
            q = peer
            sp.wait_ge(q.xb_ready, NT)
            for g in range(4):
                sp.dma_start(xs[DEC * g:DEC * (g + 1), :], xb[0:DEC, 4, :]).then_inc(q.spread_x, 16)
            sp.wait_ge(q.eid_ready, NT)
            for g in range(4):
                sp.dma_start(eid_s[DEC * g:DEC * (g + 1), :], eid[0:DEC, 4 * P + DEC * g:4 * P + DEC * (g + 1)]).then_inc(q.spread_e, 16)
            sp.wait_ge(q.gate_done, NT)
            for g in range(4):
                sp.dma_start(gate_s[DEC * g:DEC * (g + 1), :], gate[0:DEC, 4 * P + DEC * g:4 * P + DEC * (g + 1)]).then_inc(q.spread_g, 16)
            sp.wait_ge(q.spread_g, 64)

        @block.sync
        def _(sp):
            sp.dma_start(x[:, 0:4, :], i.x_prompt[0].rearrange("(t p) d -> p t d", p=P)).then_inc(start_loaded, 16)
            sp.dma_start(cst[:, :], i.constants).then_inc(start_loaded, 16)
            for l in range(2):
                for r in range(2):
                    sp.dma_start(lb_rows[:, l, r:r + 1], i.hgrn_lower_bounds[l:l + 1, r * P:(r + 1) * P].rearrange("o p -> p o")).then_inc(start_loaded, 16)
            sp.wait_ge(start_set, 1)
            sp.dma_start(x[0:DEC, 4, :], i.x_sample[0]).then_inc(start_loaded, 16)
            with sp.Fori(0, DEPTH) as l:
                project_loads(sp, l)
                meet(sp, 1)
                hgrn_loads(sp, l)
                meet(sp, 2)
                gdn_loads(sp, l)
                meet(sp, 3)
                mla_loads(sp, l)
                meet(sp, 4)
                out_loads(sp, l)
                meet(sp, 5)
                peer_loads(sp, l)
                peer_spread(sp)
                meet(sp, 6)
                next_layer(sp, l)
            sp.dma_start(o.y_prompt[0].rearrange("(t p) d -> p t d", p=P), x[:, 0:4, :]).then_inc(y_out, 16)
            sp.dma_start(o.y_sample[0], x[0:DEC, 4, :]).then_inc(y_out, 16)
            sp.wait_ge(y_out, 32)

        def norm_transposes(pe, q):
            for t in range(NT):
                pe.wait_ge(q.xb_ready, t + 1)
                if t >= 2:
                    pe.wait_ge(q.h_copy_v, t - 1)
                    pe.wait_ge(q.h_copy_a, t - 1)
                for c in range(KC):
                    mm = nc.tensor.transpose(ps[:, 2 * (t % 2) + c // 4, c % 4 * P:c % 4 * P + P], xb[:, t, c * P:(c + 1) * P], ident)
                mm.then_inc(q.h_banks, 1)

        def project_tensor(pe):
            q = project
            norm_transposes(pe, q)
            pe.wait_ge(q.rows_ready, 32)
            for j in range(NJ):
                mm = nc.tensor.transpose(ps[:, 4, 7 * j:7 * j + 7], region_v[0:7, j * P:(j + 1) * P], ident[0:7, 0:7])
            mm.then_inc(q.wh_bank, 1)
            pe.wait_ge(q.h_copy_v, NT)
            pe.wait_ge(q.h_copy_a, NT)
            for j in range(16):
                pe.wait_ge(q.wcol_ready[j % 3], 16 * (j // 3 + 1))
                if j >= 2:
                    pe.wait_ge(q.col_read, j - 1)
                w = wcol[j % 3].rearrange("p (c n) -> p c n", c=KC)
                for c in range(KC):
                    nc.tensor.matmul(ps[:, j % 2, :], w[:, c, :], hT[:, c, 0:SEQ], start=(c == 0), stop=(c == KC - 1))
                    mm = nc.tensor.matmul(ps[:, 2 + j % 2, 0:DEC], w[:, c, :], hT[:, c, SEQ:TV], start=(c == 0), stop=(c == KC - 1))
                mm.then_inc(q.col_bank, 1)
                pe.wait_ge(q.col_bank, j + 1)
                pe.sem_inc(q.wcol_used, 1)
            pe.wait_ge(q.wh_ready, 1)
            for g, (_, m, _, at_) in enumerate(TM_GROUPS):
                pe.wait_ge(q.wtm_ready[g], 16)
                w = arena[:, at_:at_ + KC * m].rearrange("p (c n) -> p c n", c=KC)
                for t in range(NT):
                    k = g * NT + t
                    if k >= 4:
                        reader = q.tm_read_a if (k - 4) // NT in (0, 2) else q.tm_read_v
                        mine = [n for n in range(k - 3) if (n // NT in (0, 2)) == (reader is q.tm_read_a)]
                        pe.wait_ge(reader, len(mine))
                    for c in range(KC):
                        mm = nc.tensor.matmul(ps[:, 4 + k % 4, 0:m], hT[:, c, tok(t)], w[:, c, :], start=(c == 0), stop=(c == KC - 1))
                    mm.then_inc(q.tm_bank, 1)
                if g == 0:
                    pe.wait_ge(q.tm_bank, NT)
                    pe.sem_inc(q.tm_used, 1)
            pe.wait_ge(q.col_read, 16)
            pe.wait_ge(q.tails_in, NJ)
            for j in range(NJ):
                mm = nc.tensor.transpose(ps[0:6, j // 4, j % 4 * P:j % 4 * P + P], tails[:, j, :], ident)
            mm.then_inc(q.tail_bank, 1)

        def hgrn_tensor(pe):
            q = hgrn
            for lv in range(7):
                pe.wait_ge(q.qe_ready, lv + 1)
                pe.wait_ge(q.ke_ready, lv + 1)
                kk, qq = (zf, qh) if lv == 0 else (KE, QE)
                k3, q3 = (a.rearrange("p (r t) -> p r t", r=2) for a in (kk, qq))
                for t in range(NT):
                    k = lv * NT + t
                    if k >= 4:
                        pe.wait_ge(q.lev_read, k - 3)
                    for h in (0, 2, 1, 3):
                        R = half(h % 2)
                        mm = nc.tensor.matmul(ps[:, 2 * (k % 4) + h % 2, h // 2 * P:h // 2 * P + P], k3[R, h // 2, tok(t)],
                                              q3[R, h // 2, tok(t)], start=True, stop=True)
                    mm.then_inc(q.lev_bank, 1)
            pe.wait_ge(q.lev_read, 7 * NT)
            pe.wait_ge(q.decayed, 1)
            qe = QE.rearrange("p (r t) -> p r t", r=2)
            kd = KE.rearrange("p (r t) -> p r t", r=2)
            for t in range(NT):
                if t >= 1:
                    pe.wait_ge(q.kd_ready, t)
                for r in range(2):
                    mm = nc.tensor.transpose(ps[:, 0, r * P:(r + 1) * P], kd[:, r, tok(t)], ident)
                mm.then_inc(q.kd_bank, 1)
                if t >= 2:
                    pe.wait_ge(q.o_scaled, t - 1)
                for h in range(4):
                    nc.tensor.matmul(ps[:, 1 + t % 2, h * C:(h + 1) * C], hattn[:, t, h, :], tm[:, t, T_V + h * C:T_V + (h + 1) * C],
                                     start=(h == 0), stop=True, skip_group_check=True)
                for c in range(2):
                    pe.wait_ge(q.s_ready, 2 * t + c + 1)
                    for r in range(2):
                        mm = nc.tensor.matmul(ps[half(c), 1 + t % 2, r * P:(r + 1) * P], qe[:, r, t * P + c * C:t * P + c * C + C],
                                              hs[:, r, :], start=False, stop=True, skip_group_check=True)
                    mm.then_inc(q.o_bank, 1)
                    pe.wait_ge(q.kd_ready, t + 1)
                    for r in range(2):
                        mm = nc.tensor.matmul(ps[:, 3 + c, r * P:(r + 1) * P], kdt[half(c), t % 2, r * P:(r + 1) * P],
                                              tm[half(c), t, T_V + r * P:T_V + (r + 1) * P], start=True, stop=True)
                    mm.then_inc(q.ds_bank, 1)

        def gdn_tensor(pe):
            q = gdn
            for j in range(8):
                pe.wait_ge(q.square_ready, j + 1)
                if j >= 2:
                    pe.wait_ge(q.sum_read, j - 1)
                nc.tensor.matmul(ps[:, j % 2, :], ones, gsq[j % 2][:, 0:SEQ], start=True, stop=True)
                nc.tensor.matmul(ps[:, 2 + j % 2, 0:DEC], ones, gsq[j % 2][:, SEQ:TV], start=True, stop=True).then_inc(q.sum_bank, 1)
            pe.wait_ge(q.gate_ready, 1)
            for k, m in enumerate((upto, const("after"), const("chunk0"), const("chunk1"))):
                mm = nc.tensor.matmul(ps[:, 4, k * gate_n:(k + 1) * gate_n], m, gg, start=True, stop=True)
            mm.then_inc(q.gates_bank, 1)
            pe.wait_ge(q.qk_ready, 8)
            pe.wait_ge(q.sum_read, 8)
            pe.wait_ge(q.gates_ready, 1)
            for t in range(NT):
                def hh(h):
                    return slice(h * P, (h + 1) * P)

                pe.wait_ge(q.ug_ready, t + 1)
                if t >= 1:
                    pe.wait_ge(q.o_scaled, t)
                nc.tensor.matmul(ps[:, 0, :], ones, ug, start=True, stop=True).then_inc(q.row_bank, 1)
                for h in range(GH):
                    nc.tensor.matmul(ps[:, 1, hh(h)], conv[:, 4 + h, tok(t)], conv[:, 4 + h, tok(t)], start=True, stop=True)
                for h in range(GH):
                    mm = nc.tensor.matmul(ps[:, 2, hh(h)], conv[:, 4 + h, tok(t)], conv[:, h, tok(t)], start=True, stop=True)
                mm.then_inc(q.gram_bank, 1)
                for h in range(GH):
                    nc.tensor.transpose(ps[:, 6, hh(h)], conv[:, 4 + h, tok(t)], ident)
                for h in range(GH):
                    mm = nc.tensor.transpose(ps[:, 7, hh(h)], conv[:, 8 + h, tok(t)], ident)
                mm.then_inc(q.kv_bank, 1)
                pe.wait_ge(q.gd_ready, t + 1)
                for h in range(GH):
                    mm = nc.tensor.transpose(ps[:, 3, hh(h)], GD[:, hh(h)], ident)
                mm.then_inc(q.gdt_bank, 1)
                pe.wait_ge(q.a_ready, t + 1)
                for h in range(GH):
                    mm = nc.tensor.transpose(ps[:, 4, hh(h)], A[:, hh(h)], ident)
                mm.then_inc(q.at_bank, 1)
                pe.wait_ge(q.kv_read, t + 1)
                for lv in range(5):
                    k = 5 * t + lv
                    pe.wait_ge(q.am_ready, k + 1)
                    pe.wait_ge(q.x_ready, k + 1)
                    if lv >= 1 or t >= 1:
                        pe.wait_ge(q.y_ready, k)
                    for h in range(GH):
                        mm = nc.tensor.matmul(ps[:, 5, hh(h)], AM[lv % 2][:, hh(h)], X[:, hh(h)], start=True, stop=True)
                    mm.then_inc(q.y_bank, 1)
                    pe.wait_ge(q.y_ready, k + 1)
                    for h in range(GH):
                        nc.tensor.matmul(ps[:, 6, hh(h)], Y[:, hh(h)], XT[:, hh(h)], start=True, stop=True)
                    for h in range(GH):
                        mm = nc.tensor.matmul(ps[:, 7, hh(h)], XT[:, hh(h)], Y[:, hh(h)], start=True, stop=True)
                    mm.then_inc(q.xx_bank, 1)
                pe.wait_ge(q.t_ready, t + 1)
                for h in range(GH):
                    mm = nc.tensor.matmul(ps[:, 2, hh(h)], KB[:, hh(h)], XT[:, hh(h)], start=True, stop=True)
                mm.then_inc(q.w_bank, 1)
                for h in range(GH):
                    nc.tensor.matmul(ps[:, 3, hh(h)], XT[:, hh(h)], VB[:, hh(h)], start=(h == 0), stop=True, skip_group_check=True)
                pe.wait_ge(q.w_ready, t + 1)
                pe.wait_ge(q.qg_ready, t + 1)
                for c in range(2):
                    k = 2 * t + c
                    pe.wait_ge(q.s_ready, k + 1)
                    for h in range(GH):
                        mm = nc.tensor.matmul(ps[half(c), 3, hh(h)], NW[:, h * P + c * C:h * P + c * C + C], S[:, hh(h)],
                                              start=False, stop=True, skip_group_check=True)
                    mm.then_inc(q.vn_bank, 1)
                    for h in range(GH):
                        nc.tensor.matmul(ps[half(c), 4, hh(h)], QG[:, h * P + c * C:h * P + c * C + C], S[:, hh(h)],
                                         start=(h == 0), stop=True, skip_group_check=True)
                    pe.wait_ge(q.vn_ready, k + 1)
                    for h in range(GH):
                        mm = nc.tensor.matmul(ps[:, 5, hh(h)], KD[half(c), hh(h)], VN[half(c), hh(h)], start=True, stop=True)
                    mm.then_inc(q.ds_bank, 1)
                    for h in range(GH):
                        mm = nc.tensor.matmul(ps[half(c), 4, hh(h)], AT[half(c), h * P + c * C:h * P + c * C + C], VN[half(c), hh(h)],
                                              start=False, stop=True, skip_group_check=True)
                    mm.then_inc(q.o_bank, 1)

        def mla_tensor(pe):
            q = mla
            pe.wait_ge(q.loads, 64)
            pe.wait_ge(q.latent_ready, 1)
            for n in range(13):
                src, rows, _ = kv_tiles[n]
                if n >= 1:
                    pe.wait_ge(q.ckvT_ready, n)
                nc.tensor.transpose(ps[:, 0, 0:rows], src, ident[0:rows, 0:rows]).then_inc(q.ckvT_bank, 1)
                pe.wait_ge(q.ckvT_ready, n + 1)
                if n >= 1:
                    pe.wait_ge(q.k_ready, n)
                    pe.wait_ge(q.v_ready, n)
                nc.tensor.matmul(ps[0:rows, 1, :], ckvT[:, 0:rows], wkvb, start=True, stop=True).then_inc(q.kv_bank, 1)
                pe.wait_ge(q.k_ready, n + 1)
                if n >= 1:
                    pe.wait_ge(q.kT_ready, n)
                for h in range(4):
                    mm = nc.tensor.transpose(ps[0:96, 2, h * P:h * P + rows], K[0:rows, h, :], ident[0:rows, 0:rows])
                mm.then_inc(q.kT_bank, 1)
            for t in range(NT):
                if t >= 1:
                    pe.wait_ge(q.qaT_ready, t)
                for c in range(2):
                    mm = nc.tensor.transpose(ps[:, 3, c * P:(c + 1) * P], tm[:, t, T_C + c * P:T_C + (c + 1) * P], ident)
                mm.then_inc(q.qaT_bank, 1)
                pe.wait_ge(q.qaT_ready, t + 1)
                if t >= 1:
                    pe.wait_ge(q.q_ready, t)
                for c in range(2):
                    mm = nc.tensor.matmul(ps[:, 4, 0:384], qaT[:, c * P:(c + 1) * P], wqb[:, c, :], start=(c == 0), stop=(c == 1))
                mm.then_inc(q.q_bank, 1)
                pe.wait_ge(q.q_ready, t + 1)
                if t >= 1:
                    pe.wait_ge(q.qT_ready, t)
                for h in range(4):
                    mm = nc.tensor.transpose(ps[0:96, 5, h * P:(h + 1) * P], Qh[:, h, :], ident)
                mm.then_inc(q.qT_bank, 1)
                pe.wait_ge(q.qT_ready, t + 1)
                if t == 0:
                    pe.wait_ge(q.kT_ready, 13)
                if t < 4:
                    m = P * (t + 1)
                    for h in range(4):
                        k = 4 * t + h
                        if k >= 2:
                            pe.wait_ge(q.p_ready, k - 1)
                        nc.tensor.matmul(ps[:, 6 + k % 2, 0:m], QT[0:96, h, :], KTp[0:96, h, 0:m], start=True, stop=False, skip_group_check=True)
                        nc.tensor.matmul(ps[:, 6 + k % 2, t * P:m], const("early")[0:1, :], const("late")[0:1, :],
                                         start=False, stop=True, skip_group_check=True).then_inc(q.s_bank, 1)
                        pe.wait_ge(q.p_ready, k + 1)
                        if k >= 1:
                            pe.wait_ge(q.pT_ready, k)
                        for b in range(t + 1):
                            mm = nc.tensor.transpose(ps[:, 0, b * P:(b + 1) * P], pr[:, b * P:(b + 1) * P], ident)
                        mm.then_inc(q.pT_bank, 1)
                        pe.wait_ge(q.pT_ready, k + 1)
                        if h == 0 and t >= 1:
                            pe.wait_ge(q.o_ready, t)
                        for b in range(t + 1):
                            mm = nc.tensor.matmul(ps[:, 1, h * C:(h + 1) * C], pT[:, b * P:(b + 1) * P], Vp[:, b, h * C:(h + 1) * C],
                                                  start=(b == 0), stop=(b == t))
                    mm.then_inc(q.o_bank, 1)
                else:
                    pe.wait_ge(q.p_ready, 16)
                    for h in range(4):
                        for b in range(3):
                            a0, a1 = 512 * b, min(512 * (b + 1), PAST + DEC)
                            mm = nc.tensor.matmul(ps[32 * h:32 * h + 32, 5 + b, 0:a1 - a0], QT[0:96, h, 0:DEC], KTs[0:96, h, a0:a1],
                                                  start=True, stop=True, skip_group_check=True)
                    mm.then_inc(q.s_bank, 1)
                    pe.wait_ge(q.pn_ready, 1)
                    pe.wait_ge(q.o_ready, 4)
                    for b in range(9):
                        r = min(P, PAST + DEC - b * P)
                        mm = nc.tensor.transpose(ps[0:r, b // 4, b % 4 * P:b % 4 * P + P], pr[:, b * P:b * P + r], ident)
                    mm.then_inc(q.pT_bank, 1)
                    pe.wait_ge(q.pT_ready, 17)
                    for h in range(4):
                        for b in range(9):
                            r = min(P, PAST + DEC - b * P)
                            mm = nc.tensor.matmul(ps[0:DEC, 3, h * C:(h + 1) * C], pT[0:r, b * P + 32 * h:b * P + 32 * h + 32],
                                                  Vs[0:r, b, h * C:(h + 1) * C], start=(b == 0), stop=(b == 8))
                    mm.then_inc(q.o_bank, 1)

        def out_tensor(pe):
            q = outp
            for t in range(NT):
                if t >= 2:
                    pe.wait_ge(q.copy_v, t - 1)
                    pe.wait_ge(q.copy_a, t - 1)
                for c, col in enumerate(MIX_COLS):
                    mm = nc.tensor.transpose(ps[:, 2 * (t % 2) + c // 4, c % 4 * P:c % 4 * P + P], tm[:, t, col:col + P], ident)
                mm.then_inc(q.t_banks, 1)
                pe.wait_ge(q.copy_v, t + 1)
                pe.wait_ge(q.copy_a, t + 1)
                for k in range(2):
                    pe.wait_ge(q.w_ready[k], 16)
                    if t >= 2:
                        pe.wait_ge(q.x_ready, 2 * (t - 2) + k + 1)
                    for c in range(KC):
                        mm = nc.tensor.matmul(ps[:, 4 + 2 * (t % 2) + k, :], mT[t % 2][:, c * P:(c + 1) * P], w_out_sb[k][:, c, :],
                                              start=(c == 0), stop=(c == KC - 1))
                    mm.then_inc(q.o_bank, 1)

        def peer_tensor(pe, l):
            q = peer
            norm_transposes(pe, q)
            pe.wait_ge(q.keys_loaded, 32)
            for j in range(16):
                mm = nc.tensor.transpose(ps[:, 4 + j // 4, j % 4 * P:j % 4 * P + P], keys[:, j, :], ident)
            mm.then_inc(q.keys_bank, 1)
            pe.wait_ge(q.h_copy_v, NT)
            pe.wait_ge(q.h_copy_a, NT)

            def scores(j):
                pe.wait_ge(q.keys_ready, 1)
                pe.wait_ge(q.q_ready, j + 1)
                if j >= 2:
                    pe.wait_ge(q.top_done, j - 1)
                for t in range(4):
                    nc.tensor.matmul(ps[:, 4 + j % 2, tok(t)], qT[j % 2][:, tok(t)], keysT[:, j, :], start=True, stop=True)
                nc.tensor.matmul(ps[0:DEC, 6 + j % 2, 0:P], qT[j % 2][:, SEQ:TV], keysT[:, j, :], start=True, stop=True).then_inc(q.s_bank, 1)

            for j in range(16):
                pe.wait_ge(q.wcol_ready[j % 3], 16 * (j // 3 + 1))
                if j >= 2:
                    pe.wait_ge(q.q_ready, j - 1)
                w = wcol[j % 3].rearrange("p (c n) -> p c n", c=KC)
                for c in range(KC):
                    nc.tensor.matmul(ps[:, j % 2, :], w[:, c, :], hT[:, c, 0:SEQ], start=(c == 0), stop=(c == KC - 1))
                    mm = nc.tensor.matmul(ps[:, 2 + j % 2, 0:DEC], w[:, c, :], hT[:, c, SEQ:TV], start=(c == 0), stop=(c == KC - 1))
                mm.then_inc(q.q_bank, 1)
                if j >= 1:
                    scores(j - 1)
                pe.wait_ge(q.q_bank, j + 1)
                pe.sem_inc(q.wcol_used, 1)
            scores(15)
            pe.wait_ge(q.q_ready, 16)
            pe.wait_ge(q.top_done, 16)
            for t in range(NT):
                R, ne = (P, P) if t < 4 else (DEC, DEC)
                b = 2 * (t % 2)
                if t >= 2:
                    pe.wait_ge(q.acc_read, t - 1)
                for k in range(2):
                    nc.tensor.matmul(ps[0:R, b + k, :], zeros[:, 0:R], xb[:, 0, 0:512], start=True, stop=False, skip_group_check=True)
                with pe.Fori(0, ne // 4) as g:
                    for k in range(4):
                        pe.wait_ge(q.v_loaded[k], (g + l * GROUPS + (t * (P // 4) + 1)) * 16)
                        pe.wait_ge(q.diag_ready, g * 4 + (t * P + k + 1))
                        pe.sem_inc(q.pe_done, 1)
                        for n in range(2):
                            mm = nc.tensor.matmul(ps[0:R, b + n, :], diag[k][:, 0:R], ring[4 + k][:, n * 512:(n + 1) * 512],
                                                  start=False, stop=False, skip_group_check=True)
                        mm.then_inc(q.v_free, 1)
                for k in range(2):
                    mm = nc.tensor.matmul(ps[0:R, b + k, :], zeros[:, 0:R], xb[:, 0, 0:512], start=False, stop=True, skip_group_check=True)
                mm.then_inc(q.acc_bank, 1)

        @block.tensor
        def _(pe):
            pe.wait_ge(start_loaded, 7 * 16)
            with pe.Fori(0, DEPTH) as l:
                project_tensor(pe)
                meet(pe, 1)
                hgrn_tensor(pe)
                meet(pe, 2)
                gdn_tensor(pe)
                meet(pe, 3)
                mla_tensor(pe)
                meet(pe, 4)
                out_tensor(pe)
                meet(pe, 5)
                peer_tensor(pe, l)
                meet(pe, 6)
                next_layer(pe, l)

        V = nc.vector

        def norm_vector(v, q):
            v.wait_ge(q.rs_ready, 1)
            v.wait_ge(q.gain_ready, 16)
            for t in range(NT):
                V.scalar_tensor_tensor(xb[:, t, :], x[:, t, :], rs[:, t:t + 1], gain[:, :], ALU.mult, ALU.mult).then_inc(q.xb_ready, 1)
            for t in range(NT):
                v.wait_ge(q.h_banks, t + 1)
                V.tensor_copy(hT[:, 0:4, tok(t)], ps[:, 2 * (t % 2), :].rearrange("p (c t) -> p c t", c=4)).then_inc(q.h_copy_v, 1)

        def project_vector(v, l):
            q, done = project, Count()
            V.tensor_copy(lb, lb_all[:, bass.ds(l, 1), :].rearrange("p o n -> p (o n)"))
            V.memset(conv[:, :, TV:TP], 0.0)
            V.memset(zf.rearrange("p (r t) -> p r t", r=2)[:, :, TV:TP], 0.0)
            V.memset(qh.rearrange("p (r t) -> p r t", r=2)[:, :, TV:TP], 0.0)
            V.memset(raw[0][:, 0:3], 0.0)
            V.memset(raw[1][:, 0:3], 0.0).then_inc(q.zero_set, 1)
            norm_vector(v, q)
            v.wait_ge(q.wh_bank, 1)
            V.tensor_copy(wh, ps[:, 4, 0:84].rearrange("p (j w) -> p j w", j=NJ)).then_inc(q.wh_ready, 1)
            v.wait_ge(q.wh_ready, 1)
            v.wait_ge(q.zero_set, 1)
            for j in range(NJ):
                r, y = raw[j % 2], conv_y[j % 2]
                if j >= 2:
                    v.wait_ge(q.y_ready, j - 1)
                V.tensor_copy(r[:, 515:518], wh[:, j, 4:7]).then_inc(q.v_done, done.up())
                v.wait_ge(q.v_done, done.n)
                v.wait_ge(q.raw_ready, 2 * (j + 1))
                V.tensor_copy(tails[:, j, 0:3], r[:, 512:515])
                V.tensor_copy(tails[:, j, 3:6], r[:, 547:550]).then_inc(q.tails_in, 1)
                if j >= 2:
                    v.wait_ge(q.silu_done, j - 1)
                V.tensor_scalar(y, r[:, 0:547], wh[:, j, 0:1], None, ALU.mult).then_inc(q.v_done, done.up())
                for w in range(1, 4):
                    v.wait_ge(q.v_done, done.n)
                    ins = V.scalar_tensor_tensor(y, r[:, w:w + 547], wh[:, j, w:w + 1], y, ALU.mult, ALU.add)
                    if w < 3:
                        ins.then_inc(q.v_done, done.up())
                ins.then_inc(q.y_ready, 1)
            for g, (_, m, col, _) in enumerate(TM_GROUPS):
                if g in (0, 2):
                    continue
                for t in range(NT):
                    k = g * NT + t
                    v.wait_ge(q.tm_bank, k + 1)
                    V.tensor_copy(tm[:, t, col:col + m], ps[:, 4 + k % 4, 0:m]).then_inc(q.tm_read_v, 1)
            v.wait_ge(q.tail_bank, 1)
            V.tensor_copy(region_v[0:6, 0:QKV], ps[0:6, 0:3, :].rearrange("p b n -> p (b n)")).then_inc(q.tail_ready, 1)

        def hgrn_vector(v):
            q, done = hgrn, Count()
            V.memset(hs_init, 0.0).then_inc(q.init_zero, 1)
            V.memset(hs, 0.0).then_inc(q.v_done, done.up())
            V.memset(hattn, 0.0).then_inc(q.v_done, done.up())
            v.wait_ge(q.v_done, done.n)
            v.wait_ge(q.e1, 1)
            V.scalar_tensor_tensor(KE, zf, 0.0, E, ALU.min, ALU.subtract).then_inc(q.v_done, done.up())
            v.wait_ge(q.v_done, done.n)
            V.tensor_tensor(QE, KE, zf, ALU.subtract).then_inc(q.nlsig, 1)
            for r in range(2):
                s = slice(r * TP, (r + 1) * TP)
                ins = V.tensor_scalar(B[:, s], KE[:, s], lb[:, 2 + r:3 + r], None, ALU.add)
            ins.then_inc(q.bprime, 1)
            v.wait_ge(q.lf, 1)
            for r in range(2):
                s = slice(r * TP, (r + 1) * TP)
                ins = V.scalar_tensor_tensor(KE[:, s], B[:, s], lb[:, r:r + 1], E[:, s], ALU.max, ALU.add)
            ins.then_inc(q.v_done, done.up())
            v.wait_ge(q.v_done, done.n)
            v.wait_ge(q.k_ready, 1)
            for r in range(2):
                V.memset(KE[:, r * TP + TV:(r + 1) * TP], 0.0)
                ins = V.memset(zf[:, r * TP + TV:(r + 1) * TP], 0.0)
            ins.then_inc(q.v_done, done.up())
            v.wait_ge(q.v_done, done.n)
            for r in range(2):
                s = slice(r * TP, (r + 1) * TP)
                ins = V.tensor_tensor_scan(B[:, s], const("carry"), KE[:, s], 0.0, ALU.mult, ALU.add)
            ins.then_inc(q.scanned, 1)
            v.wait_ge(q.scanned, 1)
            v.sem_inc(q.qe_ready, 1)
            v.sem_inc(q.ke_ready, 1)

            def read_level(lv):
                mask = ident if lv == 0 else const(f"half{2 ** (lv - 1)}")
                for t in range(NT):
                    k = lv * NT + t
                    v.wait_ge(q.lev_bank, k + 1)
                    for h in range(2):
                        ins = V.copy_predicated(hattn[:, t, h::2, :], per_head(mask.bitcast(U32), 2),
                                                ps[:, 2 * (k % 4) + h, 0:256].rearrange("p (h t) -> p h t", h=2))
                    ins.then_inc(q.lev_read, 1)

            for lv in range(1, 7):
                b = 2 ** (lv - 1)
                b4 = B.rearrange("p (n w) -> p n w", w=2 * b)
                if lv >= 2:
                    v.wait_ge(q.ke_ready, lv)
                    v.wait_ge(q.qe_ready, lv)
                V.tensor_tensor(E.rearrange("p (n w) -> p n w", w=2 * b), b4, b4[:, :, b - 1:b].to_broadcast([P, TP // b, 2 * b]),
                                ALU.subtract).then_inc(q.diff, 1)
                read_level(lv - 1)
                v.wait_ge(q.ediff, lv)
                V.tensor_tensor(QE, qh, E, ALU.mult).then_inc(q.qe_ready, 1)
            read_level(6)
            v.wait_ge(q.lev_read, 7 * NT)
            c3 = B.rearrange("p (n w) -> p n w", w=C)
            V.tensor_tensor(KE.rearrange("p (n w) -> p n w", w=C), c3[:, :, C - 1:C].to_broadcast([P, 2 * TP // C, C]), c3, ALU.subtract).then_inc(q.diff, 1)
            v.wait_ge(q.eb, 1)
            V.tensor_tensor(QE, qh, E, ALU.mult).then_inc(q.v_done, done.up())
            v.wait_ge(q.ed, 1)
            V.tensor_tensor(KE, zf, KE, ALU.mult).then_inc(q.v_done, done.up())
            v.wait_ge(q.v_done, done.n)
            v.sem_inc(q.decayed, 1)
            v.sem_inc(q.s_ready, 1)
            v.wait_ge(q.ebl_ready, 1)
            v.wait_ge(q.gg_ready, 1)
            eb3 = ebl.rearrange("p (r n) -> p r n", r=2)
            for t in range(NT):
                v.wait_ge(q.kd_bank, t + 1)
                V.tensor_copy(kdt[:, t % 2, :], ps[:, 0, 0:256]).then_inc(q.kd_ready, 1)
                for c in range(2):
                    k = 2 * t + c
                    v.wait_ge(q.ds_bank, k + 1)
                    V.tensor_tensor(hds.rearrange("p (r e) -> p r e", r=2), ps[:, 3 + c, 0:256].rearrange("p (r e) -> p r e", r=2),
                                    per_head(const("diagonal"), 2), ALU.mult).then_inc(q.v_done, done.up())
                    v.wait_ge(q.v_done, done.n)
                    for r in range(2):
                        ins = V.scalar_tensor_tensor(hs[:, r, :], hs[:, r, :], eb3[:, r, k:k + 1], hds[:, r * P:(r + 1) * P], ALU.mult, ALU.add)
                    if k in (7, 9):
                        ins.then_inc(q.v_done, done.up())
                        v.wait_ge(q.v_done, done.n)
                        ins = V.tensor_copy(hs_out[:, k // 8, :, :], hs)
                        ins.then_inc(q.s_saved, 1)
                        if k == 7:
                            v.wait_ge(q.s_saved, 1)
                            v.wait_ge(q.init_ready, 64)
                            ins = V.tensor_copy(hs, hs_init.rearrange("p (r e) -> p r e", r=2))
                            ins.then_inc(q.s_ready, 1)
                    else:
                        ins.then_inc(q.s_ready, 1)
                    if k < 9:
                        v.wait_ge(q.s_ready, k + 2)
                v.wait_ge(q.osq, t + 1)
                V.tensor_reduce(ss[:, 0:4], hosq.rearrange("p (h n) -> p h n", h=4), AX.X, ALU.add).then_inc(q.oss, 1)
                v.wait_ge(q.ors, t + 1)
                V.tensor_tensor(hosq.rearrange("p (h n) -> p h n", h=4), ps[:, 1 + t % 2, 0:256].rearrange("p (h n) -> p h n", h=4),
                                heads(sr[:, 0:4], C), ALU.mult).then_inc(q.o_scaled, 1)
                v.wait_ge(q.o_scaled, t + 1)
                V.tensor_tensor(tm[:, t, T_G:T_G + 256], hosq, tm[:, t, T_G:T_G + 256], ALU.mult).then_inc(q.o_done, 1)

        def gdn_vector(v):
            q, done = gdn, Count()
            V.memset(S, 0.0).then_inc(q.v_done, done.up())
            V.memset(VN, 0.0).then_inc(q.v_done, done.up())
            ba = tm[:, :, T_BA:T_BA + 8]
            b3 = beta.rearrange("p (t h) -> p t h", t=NT)
            g3 = gg.rearrange("p (t h) -> p t h", t=NT)
            t3 = gt.rearrange("p (t h) -> p t h", t=NT)
            V.tensor_tensor(g3, ba[:, :, 4:8], per_head(gdn_par[:, 4:8], NT), ALU.add).then_inc(q.alpha, 1)
            v.wait_ge(q.bexp, 1)
            V.tensor_scalar(beta, beta, 1.0, None, ALU.add).then_inc(q.v_done, done.up())
            v.wait_ge(q.v_done, done.n)
            V.reciprocal(beta, beta).then_inc(q.v_done, done.up())
            v.wait_ge(q.soft, 1)
            v.wait_ge(q.nega, 1)
            V.scalar_tensor_tensor(gg, gg, 0.0, gt, ALU.max, ALU.add).then_inc(q.v_done, done.up())
            v.wait_ge(q.v_done, done.n)
            V.scalar_tensor_tensor(g3, g3, -1.0, per_head(gdn_par[:, 0:4], NT), ALU.mult, ALU.mult).then_inc(q.v_done, done.up())
            v.wait_ge(q.v_done, done.n)
            V.tensor_tensor(g3, g3, heads(const("valid"), GH), ALU.mult).then_inc(q.gate_ready, 1)
            for j in range(8):
                v.wait_ge(q.norm_ready, j + 1)
                ins = V.scalar_tensor_tensor(conv[:, j, 0:TV], conv[:, j, 0:TV], P ** -0.5 if j < 4 else 1.0, grs[j % 2], ALU.mult, ALU.mult)
                ins.then_inc(q.qk_ready, 1)
            v.wait_ge(q.gates_bank, 1)
            v.wait_ge(q.gexp_ready, 1)
            V.tensor_copy(gcs, ps[:, 4, 0:gate_n]).then_inc(q.v_done, done.up())
            V.tensor_tensor(begc, beta, egc, ALU.mult).then_inc(q.v_done, done.up())
            v.wait_ge(q.v_done, done.n)
            v.sem_inc(q.gates_ready, 1)
            v.sem_inc(q.s_ready, 1)

            def h3(ap):
                return ap.rearrange("p (h n) -> p h n", h=GH)

            def col(ap, t):
                return heads(ap[:, t * GH:(t + 1) * GH])

            for t in range(NT):
                v.wait_ge(q.row_bank, t + 1)
                V.tensor_tensor(h3(DT), h3(ps[:, 0, :]), col(gcs, t), ALU.subtract).then_inc(q.v_done, done.up())
                v.wait_ge(q.v_done, done.n)
                V.tensor_scalar(DT, DT, 0.0, None, ALU.min).then_inc(q.diff_ready, 1)
                v.wait_ge(q.kv_bank, t + 1)
                V.tensor_tensor(h3(KB), h3(ps[:, 6, :]), col(begc, t), ALU.mult)
                V.tensor_tensor(h3(KD), h3(ps[:, 6, :]), col(erest, t), ALU.mult)
                V.tensor_tensor(h3(VB), h3(ps[:, 7, :]), col(beta, t), ALU.mult).then_inc(q.kv_read, 1)
                v.wait_ge(q.edt_ready, t + 1)
                V.tensor_tensor(h3(DT), h3(DT), per_head(upto), ALU.mult).then_inc(q.v_done, done.up())
                v.wait_ge(q.v_done, done.n)
                v.wait_ge(q.gram_bank, t + 1)
                V.tensor_tensor(AT, ps[:, 2, :], DT, ALU.mult)
                V.tensor_tensor(GD, ps[:, 1, :], DT, ALU.mult).then_inc(q.gd_ready, 1)
                v.wait_ge(q.gdt_bank, t + 1)
                V.tensor_tensor(h3(A), h3(ps[:, 3, :]), col(beta, t), ALU.mult).then_inc(q.a_ready, 1)
                v.wait_ge(q.a_ready, t + 1)
                V.tensor_tensor(h3(X), h3(A), per_head(const("half1t")), ALU.mult)
                v.wait_ge(q.atf_ready, t + 1)
                V.tensor_tensor(h3(XT), h3(ATF), per_head(const("half1")), ALU.mult).then_inc(q.v_done, done.up())
                v.wait_ge(q.v_done, done.n)
                V.tensor_tensor(h3(X), per_head(ident), h3(X), ALU.subtract)
                V.tensor_tensor(h3(XT), per_head(ident), h3(XT), ALU.subtract).then_inc(q.x_ready, 1)
                for lv in range(5):
                    k = 5 * t + lv
                    v.wait_ge(q.xx_bank, k + 1)
                    if lv < 4:
                        V.tensor_tensor(X, X, ps[:, 7, :], ALU.subtract)
                    ins = V.tensor_tensor(XT, XT, ps[:, 6, :], ALU.subtract)
                    if lv < 4:
                        ins.then_inc(q.x_ready, 1)
                        v.wait_ge(q.x_ready, 5 * t + lv + 2)
                    else:
                        ins.then_inc(q.t_ready, 1)
                for c in range(2):
                    k = 2 * t + c
                    v.wait_ge(q.vn_bank, k + 1)
                    V.tensor_copy(VN[half(c), :], ps[half(c), 3, :]).then_inc(q.vn_ready, 1)
                    v.wait_ge(q.ds_bank, k + 1)
                    for h in range(GH):
                        hh = slice(h * P, (h + 1) * P)
                        ins = V.scalar_tensor_tensor(S[:, hh], S[:, hh], egl[:, c * gate_n + t * GH + h:c * gate_n + t * GH + h + 1],
                                                     ps[:, 5, hh], ALU.mult, ALU.add)
                    if k in (7, 9):
                        ins.then_inc(q.v_done, done.up())
                        v.wait_ge(q.v_done, done.n)
                        V.tensor_copy(gs_out[:, k // 8, :], S).then_inc(q.s_saved, 1)
                        if k == 7:
                            v.wait_ge(q.s_saved, 1)
                            v.wait_ge(q.init_ready, 16)
                            V.tensor_copy(S, gs_init).then_inc(q.s_ready, 1)
                    else:
                        ins.then_inc(q.s_ready, 1)
                    if k < 9:
                        v.wait_ge(q.s_ready, k + 2)
                v.wait_ge(q.osq, t + 1)
                V.tensor_reduce(ss[:, 0:4], h3(OSQ), AX.X, ALU.add).then_inc(q.oss, 1)
                v.wait_ge(q.ors, t + 1)
                V.tensor_tensor(h3(OSQ), h3(ps[:, 4, :]), heads(sr[:, 0:4]), ALU.mult).then_inc(q.o_scaled, 1)
                v.wait_ge(q.o_scaled, t + 1)
                v.wait_ge(q.zg_ready, t + 1)
                V.tensor_tensor(tm[:, t, 0:512], OSQ, ZG, ALU.mult).then_inc(q.o_done, 1)

        def rope(v, q, done, dst, src, cos, sin, tmp):
            x1, x2 = src
            d1, d2 = dst
            V.tensor_tensor(tmp[0], x1, cos, ALU.mult)
            V.tensor_tensor(tmp[1], x2, sin, ALU.mult)
            V.tensor_tensor(tmp[2], x1, sin, ALU.mult)
            V.tensor_tensor(tmp[3], x2, cos, ALU.mult).then_inc(q.v_done, done.up())
            v.wait_ge(q.v_done, done.n)
            V.tensor_tensor(d1, tmp[0], tmp[1], ALU.subtract)
            return V.tensor_tensor(d2, tmp[2], tmp[3], ALU.add)

        def mla_vector(v):
            q, done = mla, Count()
            v.wait_ge(q.csq, 1)
            for k, (a, m) in enumerate(((0, 256), (256, 128), (384, 32))):
                ins = V.tensor_reduce(ss[:, 5 * k:5 * k + 5], csq[:, :, a:a + m], AX.X, ALU.add)
            ins.then_inc(q.css, 1)
            v.wait_ge(q.crs, 1)
            for k, (a, m) in enumerate(((0, 256), (256, 128), (384, 32))):
                ins = V.tensor_tensor(csq[:, :, a:a + m], tm[:, :, T_C + a:T_C + a + m], heads(sr[:, 5 * k:5 * k + 5], m), ALU.mult)
            ins.then_inc(q.v_done, done.up())
            v.wait_ge(q.v_done, done.n)
            V.tensor_tensor(tm[:, :, T_C:T_C + 416], csq, per_head(lora_gain, NT), ALU.mult).then_inc(q.v_done, done.up())
            v.wait_ge(q.v_done, done.n)
            cos, sin = (const(n_).rearrange("p (t n) -> p t n", t=NT) for n_ in ("cos", "sin"))
            tmp = [rot[:, k * 80:(k + 1) * 80].rearrange("p (t n) -> p t n", t=NT) for k in range(4)]
            kp = tm[:, :, T_C + 384:T_C + 416]
            rope(v, q, done, (kp[:, :, 0:16], kp[:, :, 16:32]), (kp[:, :, 0:16], kp[:, :, 16:32]), cos, sin, tmp).then_inc(q.latent_ready, 1)
            v.wait_ge(q.latent_ready, 1)
            v.wait_ge(q.loads, 64)
            for n in range(13):
                _, rows, kpe = kv_tiles[n]
                R = slice(0, rows)
                v.wait_ge(q.ksq, n + 1)
                V.tensor_reduce(ss[R, 0:4], ksq[R, :].rearrange("p (h n) -> p h n", h=4), AX.X, ALU.add).then_inc(q.kss, 1)
                v.wait_ge(q.krs, n + 1)
                if n >= 1:
                    v.wait_ge(q.kT_bank, n)
                V.tensor_copy(K[R, :, 64:96], kpe.unsqueeze(1).to_broadcast([rows, 4, 32]))
                V.tensor_tensor(K[R, :, 0:64], ps[R, 1, :].rearrange("p (h n) -> p h n", h=4)[:, :, 0:64], heads(sr[R, 0:4], 64),
                                ALU.mult).then_inc(q.v_done, done.up())
                v.wait_ge(q.v_done, done.n)
                V.tensor_tensor(K[R, :, 0:64], K[R, :, 0:64], per_head(knope_gain[R, :]), ALU.mult).then_inc(q.k_ready, 1)
                v.wait_ge(q.kT_bank, n + 1)
                src = ps[0:96, 2, :].rearrange("p (h n) -> p h n", h=4)[:, :, R]
                if n < 4:
                    ins = V.tensor_copy(KTp[0:96, :, tok(n)], src)
                else:
                    ins = V.tensor_copy(KTs[0:96, :, (n - 4) * P:(n - 4) * P + rows], src)
                ins.then_inc(q.kT_ready, 1)
            for t in range(NT):
                v.wait_ge(q.qsq, t + 1)
                V.tensor_reduce(ss[:, 0:4], qsq.rearrange("p (h n) -> p h n", h=4)[:, :, 0:64], AX.X, ALU.add)
                V.tensor_reduce(ss[:, 4:8], qsq.rearrange("p (h n) -> p h n", h=4)[:, :, 64:96], AX.X, ALU.add).then_inc(q.qss, 1)
                v.wait_ge(q.qrs, t + 1)
                q4 = ps[:, 4, 0:384].rearrange("p (h n) -> p h n", h=4)
                qr = ksq[:, 0:128].rearrange("p (h n) -> p h n", h=4)
                V.tensor_tensor(Qh[:, :, 0:64], q4[:, :, 0:64], heads(sr[:, 0:4], 64), ALU.mult)
                V.tensor_tensor(qr, q4[:, :, 64:96], heads(sr[:, 4:8], 32), ALU.mult).then_inc(q.v_done, done.up())
                v.wait_ge(q.v_done, done.n)
                V.tensor_tensor(Qh[:, :, 0:64], Qh[:, :, 0:64], per_head(qnope_gain), ALU.mult)
                V.tensor_tensor(qr, qr, per_head(qrope_gain), ALU.mult).then_inc(q.v_done, done.up())
                v.wait_ge(q.v_done, done.n)
                tmp = [rot[:, k * 64:(k + 1) * 64].rearrange("p (h n) -> p h n", h=4) for k in range(4)]
                rope(v, q, done, (Qh[:, :, 64:80], Qh[:, :, 80:96]), (qr[:, :, 0:16], qr[:, :, 16:32]), per_head(cos[:, t, :]),
                     per_head(sin[:, t, :]), tmp).then_inc(q.q_ready, 1)
                if t < 4:
                    m = P * (t + 1)
                    for h in range(4):
                        k = 4 * t + h
                        v.wait_ge(q.s_bank, k + 1)
                        if k >= 1:
                            v.wait_ge(q.nm, k)
                        V.tensor_reduce(mx[:, 0:1], ps[:, 6 + k % 2, 0:m], AX.X, ALU.max).then_inc(q.v_done, done.up())
                        v.wait_ge(q.v_done, done.n)
                        if k >= 1:
                            v.wait_ge(q.p_ready, k)
                        V.tensor_scalar(nm[:, 0:1], mx[:, 0:1], -SCALE, None, ALU.mult).then_inc(q.nm, 1)
                    v.wait_ge(q.p_ready, 4 * t + 4)
                    V.reciprocal(rsum, sume).then_inc(q.v_done, done.up())
                    v.wait_ge(q.v_done, done.n)
                    v.wait_ge(q.o_bank, t + 1)
                    V.tensor_tensor(tm[:, t, T_C:T_C + 256].rearrange("p (h n) -> p h n", h=4),
                                    ps[:, 1, 0:256].rearrange("p (h n) -> p h n", h=4), heads(rsum, C), ALU.mult).then_inc(q.o_ready, 1)
                else:
                    v.wait_ge(q.s_bank, 17)
                    v.wait_ge(q.nm, 16)
                    scores = ps[:, 5:8, :].rearrange("p b n -> p (b n)")[:, 0:PAST + DEC]
                    V.tensor_reduce(mx[:, 0:1], scores, AX.X, ALU.max).then_inc(q.v_done, done.up())
                    v.wait_ge(q.v_done, done.n)
                    v.wait_ge(q.p_ready, 16)
                    V.tensor_scalar(nm[:, 0:1], mx[:, 0:1], -SCALE, None, ALU.mult).then_inc(q.nm, 1)
                    v.wait_ge(q.p_ready, 17)
                    V.reciprocal(rsum[:, 0:1], sume[:, 0:1]).then_inc(q.v_done, done.up())
                    v.wait_ge(q.v_done, done.n)
                    V.tensor_scalar(pr, pr, rsum[:, 0:1], None, ALU.mult).then_inc(q.pn_ready, 1)
                    v.wait_ge(q.o_bank, 5)
                    V.tensor_copy(tm[0:DEC, 4, T_C:T_C + 256], ps[0:DEC, 3, 0:256]).then_inc(q.o_ready, 1)

        def out_vector(v):
            q = outp
            for t in range(NT):
                v.wait_ge(q.t_banks, t + 1)
                if t >= 2:
                    v.wait_ge(q.o_bank, 2 * (t - 1))
                V.tensor_copy(mT[t % 2][:, 0:512], ps[:, 2 * (t % 2), :]).then_inc(q.copy_v, 1)
                if t >= 1:
                    add_out(v, t - 1)
            add_out(v, NT - 1)

        def add_out(v, t):
            q = outp
            for k in range(2):
                v.wait_ge(q.o_bank, 2 * t + k + 1)
                R = slice(0, P if t < 4 else DEC)
                V.tensor_tensor(x[R, t, k * 512:(k + 1) * 512], x[R, t, k * 512:(k + 1) * 512], ps[R, 4 + 2 * (t % 2) + k, :],
                                ALU.add).then_inc(q.x_ready, 1)

        def peer_vector(v, l):
            q, done = peer, Count()
            norm_vector(v, q)
            v.wait_ge(q.keys_bank, 1)
            V.tensor_copy(keysT, ps[:, 4:8, :].rearrange("p b (j n) -> p (b j) n", j=4)).then_inc(q.keys_ready, 1)
            for j in range(16):
                v.wait_ge(q.s_bank, j + 1)
                for t in range(NT):
                    R = slice(0, P if t < 4 else DEC)
                    s = ps[R, 4 + j % 2, tok(t)] if t < 4 else ps[R, 6 + j % 2, 0:P]
                    w = work[t % 2]
                    tv, ti = top[R, t, j // 2, j % 2, :], top_i[R, t, j // 2, j % 2, :]
                    V.max(tv[:, 0:8], s).then_inc(q.v_done, done.up())
                    v.wait_ge(q.v_done, done.n)
                    V.match_replace(w[R, :], tv[:, 0:8], s, -3e38).then_inc(q.v_done, done.up())
                    ins = V.max_index(ti[:, 0:8], tv[:, 0:8], s)
                    if t == NT - 1:
                        ins.then_inc(q.top_done, 1)
                    v.wait_ge(q.v_done, done.n)
                    V.max(tv[:, 8:16], w[R, :]).then_inc(q.v_done, done.up())
                    v.wait_ge(q.v_done, done.n)
                    V.max_index(ti[:, 8:16], tv[:, 8:16], w[R, :]).then_inc(q.v_done, done.up())
                    v.wait_ge(q.v_done, done.n)
            v.wait_ge(q.top_done, 16)
            V.tensor_copy(top_f[:, 0:4], top_i[:, 0:4])
            V.tensor_copy(top_f[0:DEC, 4], top_i[0:DEC, 4]).then_inc(q.v_done, done.up())
            v.wait_ge(q.v_done, done.n)
            for R, ts in ((slice(0, P), slice(0, 4)), (slice(0, DEC), slice(4, 5))):
                f = top_f[R, ts, :, 0, :].rearrange("p t h a -> p (t h) a")
                ins = V.tensor_scalar(f, f, float(P), None, ALU.mult)
            ins.then_inc(q.idx_ready, 1)
            v.wait_ge(q.idx_ready, 1)
            steps = 12

            def pair_sums(t):
                R = slice(0, P if t < 4 else DEC)
                if t >= 1:
                    v.wait_ge(q.sel_step, steps * EH * t)
                for src, dst in ((top, cand), (top_f, cidx)):
                    off = 0
                    for a, na, nb in PAIR_ROWS:
                        shape = [R.stop, EH, na, nb]
                        s0 = src[R, t, :, 0, a:a + na].unsqueeze(3).to_broadcast(shape)
                        s1 = src[R, t, :, 1, 0:nb].unsqueeze(2).to_broadcast(shape)
                        d = dst[R, :].rearrange("p (h n) -> p h n", h=EH)[:, :, off:off + na * nb].rearrange("p h (a b) -> p h a b", a=na)
                        ins = V.tensor_tensor(d, s0, s1, ALU.add)
                        off += na * nb
                    ins.then_inc(q.v_done, done.up())
                v.wait_ge(q.v_done, done.n)

            def settled(t, h, k):
                v.wait_ge(q.sel_step, h * steps + (t * EH * steps + k))
                v.sem_inc(q.turn_v, 1)

            def best_pairs(t, h):
                R = slice(0, P if t < 4 else DEC)
                V.tensor_copy(pairs[R, :], cand[R, bass.ds(h * VALS, VALS)]).then_inc(q.sel_step, 1)
                settled(t, h, 1)
                V.max(best[R, 0:8], pairs[R, :]).then_inc(q.sel_step, 1)
                settled(t, h, 2)
                V.match_replace(pairs_left[R, :], best[R, 0:8], pairs[R, :], -3e38).then_inc(q.sel_step, 1)
                V.max_index(sel[R, 0:8], best[R, 0:8], pairs[R, :]).then_inc(q.sel_step, 1)
                settled(t, h, 4)
                V.max(best[R, 8:16], pairs_left[R, :]).then_inc(q.sel_step, 1)
                settled(t, h, 5)
                V.max_index(sel[R, 8:16], best[R, 8:16], pairs_left[R, :]).then_inc(q.sel_step, 1)
                V.tensor_scalar(gate[R, bass.ds(h * 16 + t * P, 16)], best[R, :], best[R, 0:1], None, ALU.subtract).then_inc(q.sel_step, 1)

            def pair_experts(t, h):
                R = slice(0, P if t < 4 else DEC)
                shape = [R.stop, 16, VALS]
                settled(t, h, 7)
                V.tensor_copy(sel_f[R, :], sel[R, :]).then_inc(q.sel_step, 1)
                settled(t, h, 8)
                V.tensor_tensor(onehot[R], sel_f[R, :].unsqueeze(2).to_broadcast(shape), const("iota")[R, :].unsqueeze(1).to_broadcast(shape),
                                ALU.is_equal).then_inc(q.sel_step, 1)
                settled(t, h, 9)
                V.tensor_tensor(onehot[R], onehot[R], cidx[R, bass.ds(h * VALS, VALS)].unsqueeze(1).to_broadcast(shape),
                                ALU.mult).then_inc(q.sel_step, 1)
                settled(t, h, 10)
                V.tensor_reduce(expert[R, :], onehot[R], AX.X, ALU.add).then_inc(q.sel_step, 1)
                settled(t, h, 11)
                V.tensor_scalar(eid[R, bass.ds(h * 16 + t * P, 16)], expert[R, :], ebase[R, :], None, ALU.add).then_inc(q.sel_step, 1)

            def selected(t):
                v.wait_ge(q.sel_step, steps * EH * (t + 1))
                v.sem_inc(q.eid_ready, 1)
                v.sem_inc(q.bests, 1)

            def gates(t):
                R = slice(0, P if t < 4 else DEC)
                gt3 = gate[R, tok(t)].rearrange("p (h a) -> p h a", h=EH)
                v.wait_ge(q.gexp, t + 1)
                V.tensor_reduce(gsum[R, :], gt3, AX.X, ALU.add).then_inc(q.v_done, done.up())
                v.wait_ge(q.v_done, done.n)
                V.reciprocal(gsum[R, :], gsum[R, :]).then_inc(q.v_done, done.up())
                v.wait_ge(q.v_done, done.n)
                V.tensor_tensor(gt3, gt3, gsum[R, :].unsqueeze(2).to_broadcast([R.stop, EH, 16]), ALU.mult).then_inc(q.gate_done, 1)
                v.wait_ge(q.gate_done, t + 1)

            def expert_dots(t, group):
                rows = xb[:, t, :] if t < 4 else xs
                for k in range(4):
                    v.wait_ge(q.u_loaded[k], (group + l * GROUPS + 1) * 16)
                    V.scalar_tensor_tensor(ring[k], ring[k], 1.0, rows, ALU.mult, ALU.mult,
                                           accum_out=dots[:, bass.ds(group * 4 + k, 1)]).then_inc(q.u_free, 1)

            pair_sums(0)
            with v.Fori(0, EH) as h:
                best_pairs(0, h)
                pair_experts(0, h)
            selected(0)
            gates(0)
            v.sem_inc(q.u_free, 4)
            v.sem_inc(q.v_free, 4)
            for t in range(NT):
                if t < 4:
                    pair_sums(t + 1)
                    with v.Fori(0, EH) as h:
                        for s in range(4):
                            expert_dots(t, h * 4 + (t * (P // 4) + s))
                            if s == 0:
                                best_pairs(t + 1, h)
                            if s == 2:
                                pair_experts(t + 1, h)
                else:
                    v.wait_ge(q.spread_x, 64)
                    with v.Fori(0, DEC // 4) as g:
                        expert_dots(t, g + t * (P // 4))
                v.drain().then_inc(q.dots_ready, 1)
                if t < 4:
                    selected(t + 1)
                ne = P if t < 4 else DEC
                if t == 4:
                    v.wait_ge(q.spread_g, 64)
                v.wait_ge(q.act_ready, t + 1)
                V.tensor_tensor(wts[:, t * P:t * P + ne], act[:, 0:ne], gate[:, tok(t)] if t < 4 else gate_s, ALU.mult).then_inc(q.wts_ready, 1)
                if t < 4:
                    gates(t + 1)
                if t >= 1:
                    add_experts(v, t - 1)
            add_experts(v, NT - 1)
            v.wait_ge(q.wts_ready, NT)
            V.tensor_scalar(ebase, ebase, float(EXPERTS), None, ALU.add)

        def add_experts(v, t):
            q = peer
            R = slice(0, P if t < 4 else DEC)
            v.wait_ge(q.acc_bank, t + 1)
            b = 2 * (t % 2)
            V.tensor_tensor(x[R, t, :], x[R, t, :], ps[R, b:b + 2, :].rearrange("p b n -> p (b n)"), ALU.add).then_inc(q.acc_read, 1)

        @block.vector
        def _(v):
            V.memset(x[:, 4, :], 0.0)
            V.memset(zeros, 0.0)
            V.memset(ebase, 0.0)
            V.memset(lb_all, 0.0).then_inc(start_set, 1)
            v.wait_ge(start_set, 1)
            V.memset(lb_all[:, 0, 0:2], -1e30)
            V.memset(lb_all[:, 0, 4:6], 1e30)
            v.wait_ge(start_loaded, 7 * 16)
            V.tensor_tensor(lb_t[:, 0:2], lb_rows[:, 1, :], lb_rows[:, 0, :], ALU.subtract).then_inc(start_set, 1)
            v.wait_ge(start_set, 3)
            V.scalar_tensor_tensor(lb_all[:, 1, 0:2], lb_t[:, 0:2], 0.0, lb_t[:, 2:4], ALU.min, ALU.subtract).then_inc(start_set, 1)
            v.wait_ge(start_set, 4)
            V.tensor_tensor(lb_all[:, 1, 2:4], lb_all[:, 1, 0:2], lb_t[:, 0:2], ALU.subtract)
            V.tensor_scalar(lb_all[:, 1, 4:6], lb_all[:, 1, 0:2], -1.0, None, ALU.mult).then_inc(start_set, 1)
            v.wait_ge(start_set, 5)
            with v.Fori(0, DEPTH) as l:
                project_vector(v, l)
                meet(v, 1)
                hgrn_vector(v)
                meet(v, 2)
                gdn_vector(v)
                meet(v, 3)
                mla_vector(v)
                meet(v, 4)
                out_vector(v)
                meet(v, 5)
                peer_vector(v, l)
                meet(v, 6)
                next_layer(v, l)

        A_ = nc.scalar
        eps = const("eps")

        def inv_root(a, dst, src, m, done_sem, done, last):
            A_.activation(dst, src, ACT.Ln, bias=eps[0:dst.shape[0], :], scale=1.0 / m).then_inc(done_sem, done.up())
            a.wait_ge(done_sem, done.n)
            A_.activation(dst, dst, ACT.Exp, scale=-0.5).then_inc(last, 1)

        def softplus_tail(a, q, done, dst, src, last, bias=0.0):
            A_.activation(dst, src, ACT.Abs, bias=bias).then_inc(q.a_done, done.up())
            a.wait_ge(q.a_done, done.n)
            A_.activation(dst, dst, ACT.Exp, scale=-1.0).then_inc(q.a_done, done.up())
            a.wait_ge(q.a_done, done.n)
            return A_.activation(dst, dst, ACT.Ln, bias=1.0).then_inc(last, 1)

        def norm_scalar(a, q, done):
            for t in range(NT):
                A_.activation(ps[:, 6:8, :].rearrange("p b n -> p (b n)"), x[:, t, :], ACT.Square,
                              accum_out=sumsq[:, t:t + 1]).then_inc(q.a_done, done.up())
                a.wait_ge(q.a_done, done.n)
            inv_root(a, rs, sumsq, D, q.a_done, done, q.rs_ready)
            for t in range(NT):
                a.wait_ge(q.h_banks, t + 1)
                A_.copy(hT[:, 4:8, tok(t)], ps[:, 2 * (t % 2) + 1, :].rearrange("p (c t) -> p c t", c=4)).then_inc(q.h_copy_a, 1)

        def project_scalar(a):
            q, done = project, Count()
            norm_scalar(a, q, done)

            def silu_conv(j):
                a.wait_ge(q.y_ready, j + 1)
                A_.activation(conv[:, j, 0:SEQ], conv_y[j % 2][:, 0:SEQ], ACT.Silu)
                A_.activation(conv[:, j, SEQ:TV], conv_y[j % 2][:, 515:547], ACT.Silu).then_inc(q.silu_done, 1)

            for j in range(16):
                a.wait_ge(q.col_bank, j + 1)
                main, rest = ps[:, j % 2, :], ps[:, 2 + j % 2, 0:DEC]
                if j < NJ:
                    if j >= 2:
                        a.wait_ge(q.y_ready, j - 1)
                    A_.copy(raw[j % 2][:, 3:515], main)
                    A_.copy(raw[j % 2][:, 518:550], rest).then_inc(q.raw_ready, 2)
                    a.wait_ge(q.raw_ready, 2 * (j + 1))
                    a.sem_inc(q.col_read, 1)
                else:
                    dst = (zf if j < 14 else qh)[:, (j % 2) * TP:(j % 2) * TP + TV]
                    f = ACT.Copy if j < 14 else ACT.Silu
                    A_.activation(dst[:, 0:SEQ], main, f)
                    A_.activation(dst[:, SEQ:TV], rest, f).then_inc(q.col_read, 1)
                if 1 <= j <= NJ:
                    silu_conv(j - 1)
            for g in (0, 2):
                _, m, col, _ = TM_GROUPS[g]
                for t in range(NT):
                    k = g * NT + t
                    a.wait_ge(q.tm_bank, k + 1)
                    A_.activation(tm[:, t, col:col + m], ps[:, 4 + k % 4, 0:m], ACT.Silu).then_inc(q.tm_read_a, 1)

        def hgrn_scalar(a):
            q, done = hgrn, Count()
            softplus_tail(a, q, done, E, zf, q.e1)
            a.wait_ge(q.nlsig, 1)
            for r in range(2):
                s = slice(r * TP, (r + 1) * TP)
                ins = A_.activation(zf[:, s], QE[:, s], ACT.Exp, bias=lb[:, 2 + r:3 + r])
            ins.then_inc(q.k_ready, 1)
            a.wait_ge(q.bprime, 1)
            for r in range(2):
                s = slice(r * TP, (r + 1) * TP)
                ins = A_.activation(E[:, s], B[:, s], ACT.Abs, bias=lb[:, 4 + r:5 + r])
            ins.then_inc(q.a_done, done.up())
            a.wait_ge(q.a_done, done.n)
            A_.activation(E, E, ACT.Exp, scale=-1.0).then_inc(q.a_done, done.up())
            a.wait_ge(q.a_done, done.n)
            A_.activation(E, E, ACT.Ln, bias=1.0).then_inc(q.lf, 1)
            for lv in range(1, 7):
                a.wait_ge(q.diff, lv)
                A_.activation(E, E, ACT.Abs).then_inc(q.a_done, done.up())
                a.wait_ge(q.a_done, done.n)
                A_.activation(E, E, ACT.Exp, scale=-1.0).then_inc(q.ediff, 1)
            a.wait_ge(q.diff, 7)
            A_.activation(E, B, ACT.Exp).then_inc(q.eb, 1)
            A_.activation(ebl.rearrange("p (n w) -> p n w", w=1), B.rearrange("p (n w) -> p n w", w=C)[:, :, C - 1:C], ACT.Exp).then_inc(q.ebl_ready, 1)
            A_.activation(KE, KE, ACT.Exp).then_inc(q.ed, 1)
            for t in range(NT):
                a.wait_ge(q.o_bank, 2 * (t + 1))
                if t >= 1:
                    a.wait_ge(q.o_done, t)
                A_.activation(hosq, ps[:, 1 + t % 2, 0:256], ACT.Square).then_inc(q.osq, 1)
                a.wait_ge(q.oss, t + 1)
                inv_root(a, sr[:, 0:4], ss[:, 0:4], C, q.a_done, done, q.ors)

        def gdn_scalar(a):
            q, done = gdn, Count()
            ba = tm[:, :, T_BA:T_BA + 8]
            A_.activation(beta.rearrange("p (t h) -> p t h", t=NT), ba[:, :, 0:4], ACT.Exp, scale=-1.0).then_inc(q.bexp, 1)
            A_.activation(gdn_par[:, 0:4], gdn_par[:, 0:4], ACT.Exp).then_inc(q.nega, 1)
            a.wait_ge(q.alpha, 1)
            softplus_tail(a, q, done, gt, gg, q.soft)

            def square(j):
                if j >= 2:
                    a.wait_ge(q.sum_bank, j - 1)
                A_.activation(gsq[j % 2], conv[:, j, 0:TV], ACT.Square).then_inc(q.square_ready, 1)

            square(0)
            square(1)
            for j in range(8):
                a.wait_ge(q.sum_bank, j + 1)
                if j >= 2:
                    a.wait_ge(q.qk_ready, j - 1)
                A_.activation(grs[j % 2][:, 0:SEQ], ps[:, j % 2, :], ACT.Ln, bias=eps)
                A_.activation(grs[j % 2][:, SEQ:TV], ps[:, 2 + j % 2, 0:DEC], ACT.Ln, bias=eps).then_inc(q.sum_read, 1)
                a.wait_ge(q.sum_read, j + 1)
                A_.activation(grs[j % 2], grs[j % 2], ACT.Exp, scale=-0.5).then_inc(q.norm_ready, 1)
                if j < 6:
                    square(j + 2)
            a.wait_ge(q.gates_bank, 1)
            A_.activation(egc, ps[:, 4, 0:gate_n], ACT.Exp)
            A_.activation(erest, ps[:, 4, gate_n:2 * gate_n], ACT.Exp)
            A_.activation(egl, ps[:, 4, 2 * gate_n:4 * gate_n], ACT.Exp).then_inc(q.gexp_ready, 1)
            for t in range(NT):
                a.wait_ge(q.diff_ready, t + 1)
                A_.activation(EG, ps[:, 0, :], ACT.Exp).then_inc(q.eg_ready, 1)
                A_.activation(DT, DT, ACT.Exp).then_inc(q.edt_ready, 1)
                a.wait_ge(q.at_bank, t + 1)
                A_.copy(ATF, ps[:, 4, :]).then_inc(q.atf_ready, 1)
                for lv in range(5):
                    a.wait_ge(q.y_bank, 5 * t + lv + 1)
                    A_.copy(Y, ps[:, 5, :]).then_inc(q.y_ready, 1)
                a.wait_ge(q.w_bank, t + 1)
                A_.activation(NW, ps[:, 2, :], ACT.Copy, scale=-1.0).then_inc(q.w_ready, 1)
                a.wait_ge(q.o_bank, 2 * (t + 1))
                if t >= 1:
                    a.wait_ge(q.o_done, t)
                A_.activation(OSQ, ps[:, 4, :], ACT.Square).then_inc(q.osq, 1)
                a.wait_ge(q.oss, t + 1)
                inv_root(a, sr[:, 0:4], ss[:, 0:4], P, q.a_done, done, q.ors)

        def mla_scalar(a):
            q, done = mla, Count()
            A_.activation(csq, tm[:, :, T_C:T_C + 416], ACT.Square).then_inc(q.csq, 1)
            a.wait_ge(q.css, 1)
            for k, m in enumerate((256, 128, 32)):
                ins = A_.activation(sr[:, 5 * k:5 * k + 5], ss[:, 5 * k:5 * k + 5], ACT.Ln, bias=eps, scale=1.0 / m)
            ins.then_inc(q.a_done, done.up())
            a.wait_ge(q.a_done, done.n)
            A_.activation(sr[:, 0:15], sr[:, 0:15], ACT.Exp, scale=-0.5).then_inc(q.crs, 1)
            for n in range(13):
                rows = kv_tiles[n][1]
                R = slice(0, rows)
                a.wait_ge(q.ckvT_bank, n + 1)
                A_.copy(ckvT[:, R], ps[:, 0, R]).then_inc(q.ckvT_ready, 1)
                a.wait_ge(q.kv_bank, n + 1)
                kv = ps[R, 1, :].rearrange("p (h n) -> p h n", h=4)
                A_.activation(ksq[R, :].rearrange("p (h n) -> p h n", h=4), kv[:, :, 0:64], ACT.Square).then_inc(q.ksq, 1)
                dst = Vp[R, n, :] if n < 4 else Vs[R, n - 4, :]
                A_.copy(dst.rearrange("p (h n) -> p h n", h=4), kv[:, :, 64:128]).then_inc(q.v_ready, 1)
                a.wait_ge(q.kss, n + 1)
                inv_root(a, sr[R, 0:4], ss[R, 0:4], 64, q.a_done, done, q.krs)
            for t in range(NT):
                a.wait_ge(q.qaT_bank, t + 1)
                A_.copy(qaT, ps[:, 3, 0:256]).then_inc(q.qaT_ready, 1)
                a.wait_ge(q.q_bank, t + 1)
                A_.activation(qsq, ps[:, 4, 0:384], ACT.Square).then_inc(q.qsq, 1)
                a.wait_ge(q.qss, t + 1)
                A_.activation(sr[:, 0:4], ss[:, 0:4], ACT.Ln, bias=eps, scale=1.0 / 64)
                A_.activation(sr[:, 4:8], ss[:, 4:8], ACT.Ln, bias=eps, scale=1.0 / 32).then_inc(q.a_done, done.up())
                a.wait_ge(q.a_done, done.n)
                A_.activation(sr[:, 0:8], sr[:, 0:8], ACT.Exp, scale=-0.5).then_inc(q.qrs, 1)
                a.wait_ge(q.qT_bank, t + 1)
                A_.copy(QT[0:96], ps[0:96, 5, :].rearrange("p (h n) -> p h n", h=4)).then_inc(q.qT_ready, 1)
                if t < 4:
                    m = P * (t + 1)
                    for h in range(4):
                        k = 4 * t + h
                        a.wait_ge(q.nm, k + 1)
                        if k >= 1:
                            a.wait_ge(q.pT_bank, k)
                        A_.activation(pr[:, 0:m], ps[:, 6 + k % 2, 0:m], ACT.Exp, bias=nm[:, 0:1], scale=SCALE,
                                      accum_out=sume[:, h:h + 1]).then_inc(q.p_ready, 1)
                        a.wait_ge(q.pT_bank, k + 1)
                        A_.copy(pT[:, 0:m], ps[:, 0, 0:m]).then_inc(q.pT_ready, 1)
                else:
                    a.wait_ge(q.nm, 17)
                    scores = ps[:, 5:8, :].rearrange("p b n -> p (b n)")[:, 0:PAST + DEC]
                    A_.activation(pr, scores, ACT.Exp, bias=nm[:, 0:1], scale=SCALE, accum_out=sume[:, 0:1]).then_inc(q.p_ready, 1)
                    a.wait_ge(q.pT_bank, 17)
                    A_.copy(pT[:, 0:1024], ps[:, 0:2, :].rearrange("p b n -> p (b n)"))
                    A_.copy(pT[0:DEC, 1024:1152], ps[0:DEC, 2, 0:P]).then_inc(q.pT_ready, 1)

        def out_scalar(a):
            q = outp
            for t in range(NT):
                a.wait_ge(q.t_banks, t + 1)
                if t >= 2:
                    a.wait_ge(q.o_bank, 2 * (t - 1))
                A_.copy(mT[t % 2][:, 512:1024], ps[:, 2 * (t % 2) + 1, :]).then_inc(q.copy_a, 1)

        def peer_scalar(a):
            q, done = peer, Count()
            norm_scalar(a, q, done)
            for j in range(16):
                a.wait_ge(q.q_bank, j + 1)
                if j >= 2:
                    a.wait_ge(q.s_bank, j - 1)
                A_.copy(qT[j % 2][:, 0:SEQ], ps[:, j % 2, :])
                A_.copy(qT[j % 2][:, SEQ:TV], ps[:, 2 + j % 2, 0:DEC]).then_inc(q.q_ready, 1)
            def gate_exp(t):
                R = slice(0, P if t < 4 else DEC)
                a.wait_ge(q.bests, t + 1)
                A_.activation(gate[R, tok(t)], gate[R, tok(t)], ACT.Exp).then_inc(q.gexp, 1)

            gate_exp(0)
            for t in range(NT):
                m, ne = (P, P) if t < 4 else (DEC, DEC)
                a.wait_ge(q.dots_ready, t + 1)
                A_.activation(act[:, 0:ne], dots[:, t * P:t * P + ne], ACT.Gelu).then_inc(q.act_ready, 1)
                if t < 4:
                    gate_exp(t + 1)
                a.wait_ge(q.wts_ready, t + 1)
                place = ident if t < 4 else const("fold")
                with a.Fori(0, ne // 4) as g:
                    for k in range(4):
                        a.wait_ge(q.v_free, g * 4 + (t * P + k + 1))
                        a.sem_inc(q.a_done, 1)
                        A_.activation(diag[k][:, 0:m], place, ACT.Copy, scale=wts[:, bass.ds(g * 4 + (t * P + k), 1)]).then_inc(q.diag_ready, 1)

        @block.scalar
        def _(a):
            a.wait_ge(start_set, 2)
            A_.activation(lb_t[:, 4:6], lb_t[:, 0:2], ACT.Abs).then_inc(start_act, 1)
            a.wait_ge(start_act, 1)
            A_.activation(lb_t[:, 4:6], lb_t[:, 4:6], ACT.Exp, scale=-1.0).then_inc(start_act, 1)
            a.wait_ge(start_act, 2)
            A_.activation(lb_t[:, 2:4], lb_t[:, 4:6], ACT.Ln, bias=1.0).then_inc(start_set, 1)
            a.wait_ge(start_loaded, 7 * 16)
            with a.Fori(0, DEPTH) as l:
                project_scalar(a)
                meet(a, 1)
                hgrn_scalar(a)
                meet(a, 2)
                gdn_scalar(a)
                meet(a, 3)
                mla_scalar(a)
                meet(a, 4)
                out_scalar(a)
                meet(a, 5)
                peer_scalar(a)
                meet(a, 6)
                next_layer(a, l)

        G = nc.gpsimd

        def hgrn_pool(p):
            q = hgrn
            for t in range(NT):
                g3 = tm[:, t, T_G:T_G + 256].rearrange("p (h n) -> p h n", h=4)
                ins = G.tensor_tensor(g3, g3, per_head(hgrn_gain), ALU.mult)
            ins.then_inc(q.gg_ready, 1)
            for lv in range(1, 7):
                p.wait_ge(q.ediff, lv)
                if lv >= 2:
                    p.wait_ge(q.lev_bank, lv * NT)
                G.tensor_tensor(KE, zf, E, ALU.mult).then_inc(q.ke_ready, 1)

        def gdn_pool(p):
            q = gdn

            def h3(ap):
                return ap.rearrange("p (h n) -> p h n", h=GH)

            p.wait_ge(q.gate_ready, 1)
            p.wait_ge(q.qk_ready, 8)
            for t in range(NT):
                if t >= 1:
                    p.wait_ge(q.row_bank, t)
                G.tensor_tensor(h3(ug), per_head(upto), heads(gg[:, t * GH:(t + 1) * GH]), ALU.mult).then_inc(q.ug_ready, 1)
                p.wait_ge(q.eg_ready, t + 1)
                G.tensor_tensor(h3(QG), conv[:, 0:4, tok(t)], h3(EG), ALU.mult).then_inc(q.qg_ready, 1)
                p.wait_ge(q.atf_ready, t + 1)
                for lv in range(5):
                    k = 5 * t + lv
                    if k >= 2:
                        p.wait_ge(q.y_bank, k - 1)
                    G.tensor_tensor(h3(AM[lv % 2]), h3(ATF), per_head(const(f"half{2 << lv}")), ALU.mult).then_inc(q.am_ready, 1)
                if t >= 1:
                    p.wait_ge(q.o_done, t)
                G.tensor_tensor(h3(ZG), h3(tm[:, t, 0:512]), per_head(gdn_gain), ALU.mult).then_inc(q.zg_ready, 1)

        def peer_pool(p):
            q = peer
            tu = i.peer_expert_u.rearrange("l e d -> (l e) d")
            tv = i.peer_expert_v.rearrange("l e d -> (l e) d")

            def gathers(t, g, side, ids, free, loaded, table, ids_ready, slot0):
                numbers = eid[:, bass.ds(g * 8 + (t * P + 4 * side), 4)] if t < 4 else eid_s[:, bass.ds(g * 8 + 4 * side, 4)]
                p.wait_ge(free, g * 8 + (t * P + 4 * side + 1))
                p.sem_inc(q.p_done, 1)
                G.tensor_copy(ids[side], numbers).then_inc(ids_ready, 1)
                p.wait_ge(ids_ready, g * 2 + (t * (P // 4) + side + 1))
                p.sem_inc(q.p_done, 1)
                for k in range(4):
                    if k >= 1:
                        p.wait_ge(free, g * 8 + (t * P + 4 * side + k + 1))
                        p.sem_inc(q.p_done, 1)
                    G.indirect_dma_start(ring[slot0 + k], None, table,
                                         bass.IndirectOffsetOnAxis(ap=ids[side][:, k:k + 1], axis=0)).then_inc(loaded[k], 16)

            def gather_u(t, g):
                for side in range(2):
                    gathers(t, g, side, uidx, q.u_free, q.u_loaded, tu, q.ids_u, 0)

            def gather_v(t, g):
                for side in range(2):
                    gathers(t, g, side, vidx, q.v_free, q.v_loaded, tv, q.ids_v, 4)

            p.wait_ge(q.eid_ready, 1)
            with p.Fori(0, P // 8) as g:
                gather_u(0, g)
            for t in range(4):
                p.wait_ge(q.eid_ready, t + 2)
                if t < 3:
                    with p.Fori(0, P // 8) as g:
                        for side in range(2):
                            gathers(t, g, side, vidx, q.v_free, q.v_loaded, tv, q.ids_v, 4)
                            gathers(t + 1, g, side, uidx, q.u_free, q.u_loaded, tu, q.ids_u, 0)
                else:
                    p.wait_ge(q.spread_e, 64)
                    with p.Fori(0, DEC // 8) as g:
                        for side in range(2):
                            gathers(3, g, side, vidx, q.v_free, q.v_loaded, tv, q.ids_v, 4)
                            gathers(4, g, side, uidx, q.u_free, q.u_loaded, tu, q.ids_u, 0)
                    with p.Fori(DEC // 8, P // 8) as g:
                        gather_v(3, g)
            with p.Fori(0, DEC // 8) as g:
                gather_v(4, g)

        @block.gpsimd
        def _(p):
            p.wait_ge(start_loaded, 7 * 16)
            with p.Fori(0, DEPTH) as l:
                meet(p, 1)
                hgrn_pool(p)
                meet(p, 2)
                gdn_pool(p)
                meet(p, 3)
                meet(p, 4)
                meet(p, 5)
                peer_pool(p)
                meet(p, 6)
                next_layer(p, l)


_INS = [
    'x_prompt', 'x_sample', 'state_gdn', 'state_gdn_conv', 'state_hgrn', 'cache_mla_ckv', 'cache_mla_kpe', 'norm_mix', 'w_in',
    'conv_w', 'gdn_a_log', 'gdn_dt_bias', 'gdn_norm', 'hgrn_lower_bounds', 'hgrn_norm', 'mla_q_a_norm', 'mla_w_q_b',
    'mla_kv_a_norm', 'mla_w_kv_b', 'mla_q_norm_nope', 'mla_q_norm_rope', 'mla_k_norm_nope', 'mla_k_norm_rope', 'w_out',
    'norm_ffn', 'peer_w_query', 'peer_sub_keys', 'peer_expert_u', 'peer_expert_v']
_OUTS = [
    ('y_prompt', (1, SEQ, D)), ('y_sample', (1, DEC, D)),
    ('p_gdn', (DEPTH, 1, 4, 128, 128)), ('p_conv', (DEPTH, 1, 3, QKV)), ('p_hgrn', (DEPTH, 1, 4, 64, 64)),
    ('p_ckv', (DEPTH, 1, SEQ, 128)), ('p_kpe', (DEPTH, 1, SEQ, 32)),
    ('s_gdn', (DEPTH, 1, 4, 128, 128)), ('s_conv', (DEPTH, 1, 3, QKV)), ('s_hgrn', (DEPTH, 1, 4, 64, 64)),
    ('s_ckv', (DEPTH, 1, DEC, 128)), ('s_kpe', (DEPTH, 1, DEC, 32))]


def kernel(**inputs):
    import concourse.bacc as _bacc
    from concourse.bass_utils import run_bass_kernel_spmd as _run

    nc = _bacc.Bacc("TRN2", target_bir_lowering=False, num_devices=1)
    arrays, ins, outs = {}, {}, {}
    for name in _INS:
        a = np.ascontiguousarray(inputs[name])
        arrays[f"in_{name}"] = a
        ins[name] = nc.dram_tensor(f"in_{name}", a.shape, mybir.dt.from_np(a.dtype), kind="ExternalInput").ap()
    table, at = constants()
    arrays["constants"] = table
    ins["constants"] = nc.dram_tensor("constants", table.shape, F32, kind="ExternalInput").ap()
    for name, shape in _OUTS:
        outs[name] = nc.dram_tensor(f"out_{name}", shape, F32, kind="ExternalOutput").ap()
    build(nc, type("Inputs", (), ins), type("Outputs", (), outs), at, table.shape[1])
    r = _run(nc, [arrays], core_ids=[0])
    return tuple(r.results[0][f"out_{name}"] for name, _ in _OUTS)
```

```python
from contextlib import ExitStack

import numpy as np

import concourse.bass as bass
from concourse import mybir

ALU = mybir.AluOpType
ACT = mybir.ActivationFunctionType
AX = mybir.AxisListType
F32 = mybir.dt.float32
U32 = mybir.dt.uint32

P = 128
DEPTH, D, SEQ, DEC, PAST = 2, 1024, 512, 32, 1024
NT = SEQ // P + 1
TP = NT * P
TV = SEQ + DEC
KC = D // P
EPS = 1e-6
C = 64
GH = 4
QKV = 1536
NJ = QKV // P
PIN = 3496
VALS = 50
EH = 8
EXPERTS = 16384
SCALE = 96 ** -0.5
GROUPS = (4 * P + DEC) // 4

W_Z, W_BA, W_BF, W_BI, W_BQ, W_BG, W_C = 1536, 2048, 2056, 2312, 2568, 2824, 3080
T_Z, T_V, T_G, T_C, T_BA, TM = 0, 512, 768, 1024, 1440, 1448
CH_COLS = [j * P for j in range(NJ)] + [W_BF, W_BF + P, W_BQ, W_BQ + P]
TM_GROUPS = [(W_Z, 512, T_Z, 0), (W_BI, 256, T_V, 4096), (W_BG, 256, T_G, 6144), (W_C, 416, T_C, 0),
             (W_BA, 8, T_BA, 8192)]
MIX_COLS = [0, 128, 256, 384, 768, 896, 1024, 1152]
PAIR_ROWS = [(0, 1, 16), (1, 1, 8), (2, 1, 5), (3, 1, 4), (4, 1, 3), (5, 3, 2), (8, 8, 1)]


def constants():
    s, t = np.arange(P)[:, None], np.arange(P)[None, :]
    same = (s // C) == (t // C)
    parts = {
        "ident": s == t, "ones": np.ones((P, P)), "upto": same & (s <= t), "after": same & (s > t),
        "chunk0": (s < C) & (t >= 0), "chunk1": (s >= C) & (t >= 0), "diagonal": same,
    }
    for b in (1, 2, 4, 8, 16, 32):
        parts[f"half{b}"] = (s // (2 * b) == t // (2 * b)) & (s % (2 * b) < b) & (t % (2 * b) >= b)
    parts["half1t"] = parts["half1"].T
    parts["carry"] = (np.arange(TP)[None, :] % C != 0) & (s >= 0)
    inv = (np.float32(10000.0) ** (-np.arange(16, dtype=np.float32) / np.float32(16))).astype(np.float32)
    pos = np.arange(P)[:, None] + P * np.arange(NT)[None, :]
    pos[:, NT - 1] = PAST + np.arange(P)
    ang = (pos.astype(np.float32)[:, :, None] * inv).astype(np.float32)
    parts["cos"], parts["sin"] = np.cos(ang).reshape(P, -1), np.sin(ang).reshape(P, -1)
    valid = np.ones((P, NT))
    valid[DEC:, NT - 1] = 0
    parts["valid"] = valid
    parts["eps"] = np.full((P, 1), EPS)
    parts["early"] = (t < C) & (s >= 0)
    parts["late"] = np.where(t >= C, -1e30, 0.0) * (s >= 0)
    parts["fold"] = s % DEC == np.arange(DEC)[None, :]
    parts["iota"] = np.arange(VALS)[None, :] * np.ones((P, 1))
    at, off = {}, 0
    for k, v in parts.items():
        at[k] = (off, v.shape[1])
        off += v.shape[1]
    return np.concatenate([v.astype(np.float32) for v in parts.values()], axis=1), at


class Count:

    def __init__(self):
        self.n = 0

    def up(self):
        self.n += 1
        return 1


def build(nc, i, o, at, ncols):
    with ExitStack() as ctx:
        def sb(name, cols, dt=F32):
            return ctx.enter_context(nc.sbuf_tensor(name, [P, cols], dt))

        sems = []

        def sem(name, cleared=True):
            s = ctx.enter_context(nc.semaphore(name))
            if cleared:
                sems.append(s)
            return s

        ps = ctx.enter_context(nc.psum_tensor("ps", [P, 8, 512], F32))
        x = sb("x", NT * D)[:, :].rearrange("p (t d) -> p t d", t=NT)
        region_h = sb("region_h", 5120)
        region_t = sb("region_t", NT * TM)
        region_c = sb("region_c", 8192)
        region_w = sb("region_w", 3072)
        arena = sb("arena", 12288)
        cst = sb("cst", ncols)
        gain = sb("gain", D)
        region_v = sb("region_v", 2304)
        raw = [sb(f"raw{k}", 550) for k in range(2)]
        small = sb("small", 1500)

        used = [0]

        def piece(n):
            used[0] += n
            assert used[0] <= 1500
            return small[:, used[0] - n:used[0]]

        def const(name):
            a, n = at[name]
            return cst[:, a:a + n]

        ident, ones, upto = const("ident"), const("ones"), const("upto")
        hT = region_h[:, :].rearrange("p (c t) -> p c t", c=KC)
        tm = region_t[:, :].rearrange("p (t n) -> p t n", t=NT)
        xb = region_t[:, 0:NT * D].rearrange("p (t n) -> p t n", t=NT)
        conv = region_c[:, 0:NJ * TP].rearrange("p (j t) -> p j t", j=NJ)
        wcol = [region_w[:, k * D:(k + 1) * D] for k in range(3)]
        zf = arena[:, 9728:11008]
        qh = arena[:, 11008:12288]
        conv_y = [arena[:, 8256 + k * 547:8256 + (k + 1) * 547] for k in range(2)]

        sumsq, rs = piece(NT), piece(NT)
        wh = piece(NJ * 7).rearrange("p (j w) -> p j w", j=NJ)
        tails = piece(NJ * 6).rearrange("p (j w) -> p j w", j=NJ)
        lb_rows = piece(4).rearrange("p (l r) -> p l r", l=2)
        lb_all = piece(12).rearrange("p (l r) -> p l r", l=2)
        lb = piece(6)
        lb_t = piece(8)
        gdn_par = piece(8)
        gdn_gain, hgrn_gain = piece(128), piece(64)
        lora_gain = piece(416)
        knope_gain, qnope_gain, qrope_gain = piece(64), piece(64), piece(32)
        ebase = piece(1)
        gate_n = NT * GH
        beta, gg, gcs, egc, begc, erest = (piece(gate_n) for _ in range(6))
        egl = piece(2 * gate_n)
        gt = piece(gate_n)
        ebl = piece(20)
        ss = piece(16)
        sr = piece(16)
        mx, nm, sume, rsum = piece(4), piece(4), piece(4), piece(4)

        shared = [ctx.enter_context(nc.semaphore(f"shared{k}")) for k in range(64)]

        def named(text):
            names = text.split()
            assert len(names) <= len(shared)
            return type("Phase", (), dict(zip(names, shared)))

        start_loaded = ctx.enter_context(nc.semaphore("start_loaded"))
        start_set = ctx.enter_context(nc.semaphore("start_set"))
        met = ctx.enter_context(nc.semaphore("phase_met"))
        start_act = ctx.enter_context(nc.semaphore("start_act"))
        layer_arrive = ctx.enter_context(nc.semaphore("layer_arrive"))
        layer_cleared = ctx.enter_context(nc.semaphore("layer_cleared"))
        u_loaded = [ctx.enter_context(nc.semaphore(f"u_loaded{k}")) for k in range(4)]
        v_loaded = [ctx.enter_context(nc.semaphore(f"v_loaded{k}")) for k in range(4)]
        passed = ctx.enter_context(nc.semaphore("passed"))
        turn = ctx.enter_context(nc.semaphore("turn"))
        y_out = ctx.enter_context(nc.semaphore("y_out"))

        def meet(eng, k):
            if eng.engine == nc.sync.engine:
                eng.wait_ge(met, 5 * k - 1)
                for s in shared:
                    eng.sem_clear(s)
                eng.sem_inc(met, 1)
            else:
                eng.drain().then_inc(met, 1)
            eng.wait_ge(met, 5 * k)
            eng.sem_inc(passed, 1)

        def next_layer(eng, l):
            if eng.engine == nc.sync.engine:
                eng.wait_ge(layer_arrive, l * 4 + 4)
                eng.sem_inc(turn, 1)
                eng.sem_clear(met)
                eng.sem_clear(turn)
                eng.sem_inc(layer_cleared, 1)
            else:
                eng.sem_inc(layer_arrive, 1)
                eng.wait_ge(layer_cleared, l + 1)
                eng.sem_inc(passed, 1)

        def tok(t):
            return slice(t * P, (t + 1) * P)

        def half(c):
            return slice(c * C, (c + 1) * C)

        def heads(ap, m=P):
            return ap.unsqueeze(2).to_broadcast([ap.shape[0], ap.shape[1], m])

        def per_head(ap, h=GH):
            return ap.unsqueeze(1).to_broadcast([ap.shape[0], h, ap.shape[1]])

        def span(region, start, cols):
            return region[:, start:start + cols]

        zeros = piece(P)
        sr2 = piece(16)
        B, E, QE, KE = (span(arena, k * 1280, 1280) for k in range(4))
        hattn = span(arena, 5120, 2560).rearrange("p (t h s) -> p t h s", t=NT, h=4)
        hs = span(arena, 7680, 256).rearrange("p (r e) -> p r e", r=2)
        hs_init = span(arena, 7936, 256)
        hs_out = span(arena, 8192, 512).rearrange("p (k r e) -> p k r e", k=2, r=2)
        hds = span(arena, 8704, 256)
        kdt = span(region_v, 0, 512).rearrange("p (k n) -> p k n", k=2)
        hosq = span(region_v, 512, 256)
        hgg = span(region_v, 768, 256)
        (DT, EG, QG, AT, GD, A, ATF, AM0, AM1, X, XT, Y, VB, KB, KD, NW, VN, S, OSQ, ZG, ug, gs_init) = (
            span(arena, k * 512, 512) for k in range(22))
        AM = [AM0, AM1]
        AT, KD, QG = [AT, span(region_w, 1088, 512)], [KD, span(region_w, 1600, 512)], [QG, span(region_w, 2112, 512)]
        gs_out = span(region_v, 0, 1024).rearrange("p (k n) -> p k n", k=2)
        gsq = [span(region_v, 1024, 544), span(region_v, 1024 + 544, 544)]
        grs = [span(region_w, 0, 544), span(region_w, 544, 544)]
        wqb = span(arena, 0, 768).rearrange("p (c n) -> p c n", c=2)
        wkvb = span(arena, 768, 512)
        past_c = span(arena, 1280, 1024).rearrange("p (t n) -> p t n", t=8)
        past_k = span(arena, 2304, 256).rearrange("p (t n) -> p t n", t=8)
        pr = span(arena, 4224, 1056)
        pT = span(arena, 5280, 1152)
        csq = span(arena, 6432, 2080).rearrange("p (t n) -> p t n", t=NT)
        rot = span(arena, 8512, 512)
        mla_sq = span(arena, 9024, 768)
        mla_qr = span(arena, 9792, 256)
        mla_mx, mla_nm = span(arena, 10048, 17), span(arena, 10080, 17)
        mla_sum, mla_rsum = span(arena, 10112, 17), span(arena, 10144, 17)
        mla_ss, mla_sr = span(arena, 10176, 16), span(arena, 10192, 16)
        mla_rows = [span(region_c, k * 768, 768) for k in range(2)]
        latT = span(region_c, 1536, 23 * P)
        QT = span(region_c, 4480, NT * 512).rearrange("p (t h n) -> p t h n", t=NT, h=4)
        KTp = span(region_w, 0, 2048).rearrange("p (h n) -> p h n", h=4)
        Vp = span(region_w, 2048, 1024).rearrange("p (t n) -> p t n", t=4)
        KTs = span(region_h, 0, 4 * 1056).rearrange("p (h n) -> p h n", h=4)
        Vs = span(region_v, 0, 2304).rearrange("p (t n) -> p t n", t=9)
        latents = ([tm[:, t, T_C + 256:T_C + 384] for t in range(4)] + [past_c[:, t, :] for t in range(8)]
                   + [tm[:, t, T_C + c * P:T_C + (c + 1) * P] for t in range(NT) for c in range(2)]
                   + [tm[0:DEC, 4, T_C + 256:T_C + 384]])
        Q_LAT, OWN_LAT = 12, 22
        KEY_ITEMS = 7
        mla_items = ([("key", (2 * g, 2 * g + 1)) for g in range(6)] + [("key", (12,))]
                     + [("query", (0, 1)), ("query", (2, 3)), ("query", (4,))])
        A_BANK = [1 + 2 * (k % 2) for k in range(10)]
        B_BANK = [(5, 6) if k % 2 == 0 else (7, 0) for k in range(10)]

        w_out_sb = [span(arena, k * 4096, 4096).rearrange("p (c n) -> p c n", c=KC) for k in range(2)]
        mT = [span(region_c, k * 1024, 1024) for k in range(2)]
        keys = span(arena, 0, 2048).rearrange("p (j n) -> p j n", j=16)
        keysT = span(arena, 2048, 2048).rearrange("p (j n) -> p j n", j=16)
        qT = [span(arena, 4096, 544), span(arena, 4640, 544)]
        top = span(arena, 5184, 1280).rearrange("p (t h s a) -> p t h s a", t=NT, h=EH, s=2)
        top_i = span(arena, 6464, 1280).bitcast(U32).rearrange("p (t h s a) -> p t h s a", t=NT, h=EH, s=2)
        top_f = span(arena, 7744, 1280).rearrange("p (t h s a) -> p t h s a", t=NT, h=EH, s=2)
        work = [span(arena, 9024, 128), span(arena, 9152, 128)]
        pairs, pairs_left = span(arena, 0, VALS), span(arena, 64, VALS)
        best = span(arena, 128, 16)
        sel = span(arena, 144, 16).bitcast(U32)
        sel_f, expert = span(arena, 160, 16), span(arena, 176, 16)
        onehot = span(arena, 192, 16 * VALS).rearrange("p (a n) -> p a n", a=16)
        eid_s = span(arena, 1024, DEC).bitcast(U32)
        gate_s = span(arena, 1024 + DEC, DEC)
        xs = gain[:, :]
        cand = span(arena, 9280, EH * VALS)
        cidx = span(arena, 9680, EH * VALS)
        eid = span(arena, 10464, NT * P).bitcast(U32)
        gate = span(arena, 11104, NT * P)
        diag = [span(arena, 11744 + k * P, P) for k in range(4)]
        dots = span(region_v, 0, NT * P)
        wts = span(region_v, 640, NT * P)
        act = span(region_v, 1280, P)
        uidx = [span(region_v, 1408 + 8 * k, 4).bitcast(U32) for k in range(2)]
        vidx = [span(region_v, 1412 + 8 * k, 4).bitcast(U32) for k in range(2)]
        gsum = span(region_v, 1424, EH)
        ring = [span(region_c, k * D, D) for k in range(8)]

        project = named("gain_ready sumsq_ready rs_ready xb_ready h_banks h_copy_v h_copy_a params_ready rows_ready wcol_used "
                        "wc0 wc1 wc2 tm_used wt0 wt1 wt2 wt3 wt4 wh_bank wh_ready col_bank col_read tm_bank tm_read_a tm_read_v "
                        "tails_in tail_bank tail_ready tail_out raw_ready y_ready silu_done v_done a_done zero_set")
        project.wcol_ready = [project.wc0, project.wc1, project.wc2]
        project.wtm_ready = [project.wt0, project.wt1, project.wt2, project.wt3, project.wt4]
        hgrn = named("init_zero init_ready s_saved state_out qe_ready ke_ready lev_bank lev_read decayed kd_bank kd_ready o_scaled "
                     "s_ready o_bank ds_bank v_done a_done e1 lsig nlsig k_ready bprime ad lf scanned diff ediff eb ed mult_ready "
                     "osq oss ors gg_ready ebl_ready p_done o_done")
        gdn = named("init_ready s_saved state_out square_ready sum_bank sum_read gate_ready gates_bank gates_ready qk_ready ug_ready "
                    "row_bank gram_bank kv_bank gd_ready gdt_bank a_ready at_bank kv_read am_ready x_ready y_ready y_bank xx_bank "
                    "t_ready w_bank w_ready qg_ready s_ready vn_bank vn_ready ds_bank o_bank o_scaled v_done a_done norm_ready "
                    "soft gexp_ready eg_ready diff_ready edt_ready dtm_ready atf_ready osq oss ors zg_ready bexp alpha nega o_done")
        mla = named("loads latent_ready latent_out csq css crs lat_bank lat_ready a_bank sq ssum rs rows_ready v_ready t_bank "
                    "kT_ready qT_ready s_bank mx nm p_ready pT_bank pT_ready av_done o_bank o_ready pn_ready v_done a_done rsums")
        outp = named("w0 w1 copy_v copy_a t_banks x_ready o_bank")
        outp.w_ready = [outp.w0, outp.w1]
        peer = named("gain_ready sumsq_ready rs_ready xb_ready h_banks h_copy_v h_copy_a wcol_used wc0 wc1 wc2 keys_loaded "
                     "keys_bank keys_ready q_ready s_bank top_done q_bank acc_read diag_ready v_free acc_bank u_free "
                     "v_done a_done pair_ready pair_used eid_ready dots_ready act_ready wts_ready diag_free bests gexp "
                     "p_done pe_done ids_u ids_v spread_x spread_e spread_g gate_done sel_step turn_v")
        peer.wcol_ready = [peer.wc0, peer.wc1, peer.wc2]
        peer.u_loaded, peer.v_loaded = u_loaded, v_loaded
        block = ctx.enter_context(nc.Block())
        def norm_loads(sp, q, l, weights):
            sp.dma_start(gain[:, :], weights[bass.ds(l, 1), :].to_broadcast([P, D])).then_inc(q.gain_ready, 16)

        def project_loads(sp, l):
            q = project
            norm_loads(sp, q, l, i.norm_mix)
            sp.dma_start(region_v[0:4, 0:QKV], i.conv_w[bass.ds(l, 1), :, :].rearrange("o w n -> (o w) n")).then_inc(q.rows_ready, 16)
            sp.dma_start(region_v[4:7, 0:QKV], i.state_gdn_conv[bass.ds(l, 1), 0, :, :].rearrange("o w n -> (o w) n")).then_inc(q.rows_ready, 16)
            small_loads = [
                (gdn_par[:, 0:4], i.gdn_a_log, GH), (gdn_par[:, 4:8], i.gdn_dt_bias, GH), (gdn_gain, i.gdn_norm, P),
                (hgrn_gain, i.hgrn_norm, C), (lora_gain[:, 0:256], i.mla_q_a_norm, 256),
                (lora_gain[:, 256:384], i.mla_kv_a_norm, 128), (lora_gain[:, 384:416], i.mla_k_norm_rope, 32),
                (knope_gain, i.mla_k_norm_nope, C), (qnope_gain, i.mla_q_norm_nope, C), (qrope_gain, i.mla_q_norm_rope, 32)]
            for dst, src, m in small_loads:
                sp.dma_start(dst, src[bass.ds(l, 1), :].to_broadcast([P, m])).then_inc(q.params_ready, 16)
            for j, col in enumerate(CH_COLS):
                if j >= 3:
                    sp.wait_ge(q.wcol_used, j - 2)
                sp.dma_start(wcol[j % 3].rearrange("p (c n) -> p c n", c=KC),
                             i.w_in[bass.ds(l, 1), :, col:col + P].rearrange("o (c p) n -> p (o c) n", p=P)).then_inc(q.wcol_ready[j % 3], 16)
            for g, (col, m, _, at_) in enumerate(TM_GROUPS):
                if g == 3:
                    sp.wait_ge(q.tm_used, 1)
                sp.dma_start(arena[:, at_:at_ + KC * m].rearrange("p (c n) -> p c n", c=KC),
                             i.w_in[bass.ds(l, 1), :, col:col + m].rearrange("o (c p) n -> p (o c) n", p=P)).then_inc(q.wtm_ready[g], 16)
            sp.wait_ge(q.tail_ready, 1)
            sp.dma_start(o.p_conv[bass.ds(l, 1), 0, :, :].rearrange("o w n -> (o w) n"), region_v[0:3, 0:QKV]).then_inc(q.tail_out, 16)
            sp.dma_start(o.s_conv[bass.ds(l, 1), 0, :, :].rearrange("o w n -> (o w) n"), region_v[3:6, 0:QKV]).then_inc(q.tail_out, 16)
            sp.wait_ge(q.params_ready, 16 * len(small_loads))
            sp.wait_ge(q.tail_out, 32)

        def hgrn_loads(sp, l):
            q = hgrn
            sp.wait_ge(q.init_zero, 1)
            for h in range(4):
                sp.dma_start(hs_init[half(h % 2), h // 2 * P + h % 2 * C:h // 2 * P + h % 2 * C + C],
                             i.state_hgrn[bass.ds(l, 1), 0, h, :, :].rearrange("o a b -> (o a) b")).then_inc(q.init_ready, 16)
            for k, (dst, at_) in enumerate(((o.p_hgrn, 1), (o.s_hgrn, 2))):
                sp.wait_ge(q.s_saved, at_)
                for h in range(4):
                    sp.dma_start(dst[bass.ds(l, 1), 0, h, :, :].rearrange("o a b -> (o a) b"),
                                 hs_out[half(h % 2), k, h // 2, h % 2 * C:h % 2 * C + C]).then_inc(q.state_out, 16)
            sp.wait_ge(q.state_out, 8 * 16)

        def gdn_loads(sp, l):
            q = gdn
            sp.dma_start(gs_init[:, :].rearrange("p (h e) -> p h e", h=GH),
                         i.state_gdn[bass.ds(l, 1), 0, :, :, :].rearrange("o h a b -> a (o h) b")).then_inc(q.init_ready, 16)
            for k, dst in enumerate((o.p_gdn, o.s_gdn)):
                sp.wait_ge(q.s_saved, k + 1)
                sp.dma_start(dst[bass.ds(l, 1), 0, :, :, :].rearrange("o h a b -> a (o h) b"),
                             gs_out[:, k, :].rearrange("p (h e) -> p h e", h=GH)).then_inc(q.state_out, 16)
            sp.wait_ge(q.state_out, 32)

        def mla_loads(sp, l):
            q = mla
            sp.dma_start(wqb[:, :, :], i.mla_w_q_b[bass.ds(l, 1), :, :].rearrange("o (c p) n -> p (o c) n", p=P)).then_inc(q.loads, 16)
            sp.dma_start(wkvb, i.mla_w_kv_b[bass.ds(l, 1), :, :].rearrange("o p n -> p (o n)")).then_inc(q.loads, 16)
            sp.dma_start(past_c[:, :, :], i.cache_mla_ckv[bass.ds(l, 1), 0, :, :].rearrange("o (t p) n -> p (o t) n", p=P)).then_inc(q.loads, 16)
            sp.dma_start(past_k[:, :, :], i.cache_mla_kpe[bass.ds(l, 1), 0, :, :].rearrange("o (t p) n -> p (o t) n", p=P)).then_inc(q.loads, 16)
            sp.wait_ge(q.latent_ready, 1)
            sp.dma_start(o.p_ckv[bass.ds(l, 1), 0, :, :].rearrange("o (t p) n -> p (o t) n", p=P), tm[:, 0:4, T_C + 256:T_C + 384]).then_inc(q.latent_out, 16)
            sp.dma_start(o.p_kpe[bass.ds(l, 1), 0, :, :].rearrange("o (t p) n -> p (o t) n", p=P), tm[:, 0:4, T_C + 384:T_C + 416]).then_inc(q.latent_out, 16)
            sp.dma_start(o.s_ckv[bass.ds(l, 1), 0, :, :].rearrange("o p n -> p (o n)"), tm[0:DEC, 4, T_C + 256:T_C + 384]).then_inc(q.latent_out, 16)
            sp.dma_start(o.s_kpe[bass.ds(l, 1), 0, :, :].rearrange("o p n -> p (o n)"), tm[0:DEC, 4, T_C + 384:T_C + 416]).then_inc(q.latent_out, 16)
            sp.wait_ge(q.latent_out, 64)

        def out_loads(sp, l):
            q = outp
            for k in range(2):
                sp.dma_start(w_out_sb[k], i.w_out[bass.ds(l, 1), :, k * 512:(k + 1) * 512].rearrange("o (c p) n -> p (o c) n", p=P)).then_inc(q.w_ready[k], 16)

        def peer_loads(sp, l):
            q = peer
            norm_loads(sp, q, l, i.norm_ffn)
            for k in range(2):
                sp.dma_start(keys[:, 8 * k:8 * k + 8, :], i.peer_sub_keys[bass.ds(l, 1), 4 * k:4 * k + 4, :, :, :].rearrange("o h s n d -> n (o h s) d")).then_inc(q.keys_loaded, 16)
            for j in range(16):
                if j >= 3:
                    sp.wait_ge(q.wcol_used, j - 2)
                sp.dma_start(wcol[j % 3].rearrange("p (c n) -> p c n", c=KC),
                             i.peer_w_query[bass.ds(l, 1), :, j * P:(j + 1) * P].rearrange("o (c p) n -> p (o c) n", p=P)).then_inc(q.wcol_ready[j % 3], 16)

        def peer_spread(sp):
            q = peer
            sp.wait_ge(q.xb_ready, NT)
            for g in range(4):
                sp.dma_start(xs[DEC * g:DEC * (g + 1), :], xb[0:DEC, 4, :]).then_inc(q.spread_x, 16)
            sp.wait_ge(q.eid_ready, NT)
            for g in range(4):
                sp.dma_start(eid_s[DEC * g:DEC * (g + 1), :], eid[0:DEC, 4 * P + DEC * g:4 * P + DEC * (g + 1)]).then_inc(q.spread_e, 16)
            sp.wait_ge(q.gate_done, NT)
            for g in range(4):
                sp.dma_start(gate_s[DEC * g:DEC * (g + 1), :], gate[0:DEC, 4 * P + DEC * g:4 * P + DEC * (g + 1)]).then_inc(q.spread_g, 16)
            sp.wait_ge(q.spread_g, 64)

        @block.sync
        def _(sp):
            sp.dma_start(x[:, 0:4, :], i.x_prompt[0].rearrange("(t p) d -> p t d", p=P)).then_inc(start_loaded, 16)
            sp.dma_start(cst[:, :], i.constants).then_inc(start_loaded, 16)
            for l in range(2):
                for r in range(2):
                    sp.dma_start(lb_rows[:, l, r:r + 1], i.hgrn_lower_bounds[l:l + 1, r * P:(r + 1) * P].rearrange("o p -> p o")).then_inc(start_loaded, 16)
            sp.wait_ge(start_set, 1)
            sp.dma_start(x[0:DEC, 4, :], i.x_sample[0]).then_inc(start_loaded, 16)
            with sp.Fori(0, DEPTH) as l:
                project_loads(sp, l)
                meet(sp, 1)
                hgrn_loads(sp, l)
                meet(sp, 2)
                gdn_loads(sp, l)
                meet(sp, 3)
                mla_loads(sp, l)
                meet(sp, 4)
                out_loads(sp, l)
                meet(sp, 5)
                peer_loads(sp, l)
                peer_spread(sp)
                meet(sp, 6)
                next_layer(sp, l)
            sp.dma_start(o.y_prompt[0].rearrange("(t p) d -> p t d", p=P), x[:, 0:4, :]).then_inc(y_out, 16)
            sp.dma_start(o.y_sample[0], x[0:DEC, 4, :]).then_inc(y_out, 16)
            sp.wait_ge(y_out, 32)

        def norm_transposes(pe, q):
            for t in range(NT):
                pe.wait_ge(q.xb_ready, t + 1)
                if t >= 2:
                    pe.wait_ge(q.h_copy_v, t - 1)
                    pe.wait_ge(q.h_copy_a, t - 1)
                for c in range(KC):
                    mm = nc.tensor.transpose(ps[:, 2 * (t % 2) + c // 4, c % 4 * P:c % 4 * P + P], xb[:, t, c * P:(c + 1) * P], ident)
                mm.then_inc(q.h_banks, 1)

        def project_tensor(pe):
            q = project
            norm_transposes(pe, q)
            pe.wait_ge(q.rows_ready, 32)
            for j in range(NJ):
                mm = nc.tensor.transpose(ps[:, 4, 7 * j:7 * j + 7], region_v[0:7, j * P:(j + 1) * P], ident[0:7, 0:7])
            mm.then_inc(q.wh_bank, 1)
            pe.wait_ge(q.h_copy_v, NT)
            pe.wait_ge(q.h_copy_a, NT)
            for j in range(16):
                pe.wait_ge(q.wcol_ready[j % 3], 16 * (j // 3 + 1))
                if j >= 2:
                    pe.wait_ge(q.col_read, j - 1)
                w = wcol[j % 3].rearrange("p (c n) -> p c n", c=KC)
                for c in range(KC):
                    nc.tensor.matmul(ps[:, j % 2, :], w[:, c, :], hT[:, c, 0:SEQ], start=(c == 0), stop=(c == KC - 1))
                    mm = nc.tensor.matmul(ps[:, 2 + j % 2, 0:DEC], w[:, c, :], hT[:, c, SEQ:TV], start=(c == 0), stop=(c == KC - 1))
                mm.then_inc(q.col_bank, 1)
                pe.wait_ge(q.col_bank, j + 1)
                pe.sem_inc(q.wcol_used, 1)
            pe.wait_ge(q.wh_ready, 1)
            for g, (_, m, _, at_) in enumerate(TM_GROUPS):
                pe.wait_ge(q.wtm_ready[g], 16)
                w = arena[:, at_:at_ + KC * m].rearrange("p (c n) -> p c n", c=KC)
                for t in range(NT):
                    k = g * NT + t
                    if k >= 4:
                        reader = q.tm_read_a if (k - 4) // NT in (0, 2) else q.tm_read_v
                        mine = [n for n in range(k - 3) if (n // NT in (0, 2)) == (reader is q.tm_read_a)]
                        pe.wait_ge(reader, len(mine))
                    for c in range(KC):
                        mm = nc.tensor.matmul(ps[:, 4 + k % 4, 0:m], hT[:, c, tok(t)], w[:, c, :], start=(c == 0), stop=(c == KC - 1))
                    mm.then_inc(q.tm_bank, 1)
                if g == 0:
                    pe.wait_ge(q.tm_bank, NT)
                    pe.sem_inc(q.tm_used, 1)
            pe.wait_ge(q.col_read, 16)
            pe.wait_ge(q.tails_in, NJ)
            for j in range(NJ):
                mm = nc.tensor.transpose(ps[0:6, j // 4, j % 4 * P:j % 4 * P + P], tails[:, j, :], ident)
            mm.then_inc(q.tail_bank, 1)

        def hgrn_tensor(pe):
            q = hgrn
            for lv in range(7):
                pe.wait_ge(q.qe_ready, lv + 1)
                pe.wait_ge(q.ke_ready, lv + 1)
                kk, qq = (zf, qh) if lv == 0 else (KE, QE)
                k3, q3 = (a.rearrange("p (r t) -> p r t", r=2) for a in (kk, qq))
                for t in range(NT):
                    k = lv * NT + t
                    if k >= 4:
                        pe.wait_ge(q.lev_read, k - 3)
                    for h in (0, 2, 1, 3):
                        R = half(h % 2)
                        mm = nc.tensor.matmul(ps[:, 2 * (k % 4) + h % 2, h // 2 * P:h // 2 * P + P], k3[R, h // 2, tok(t)],
                                              q3[R, h // 2, tok(t)], start=True, stop=True)
                    mm.then_inc(q.lev_bank, 1)
            pe.wait_ge(q.lev_read, 7 * NT)
            pe.wait_ge(q.decayed, 1)
            qe = QE.rearrange("p (r t) -> p r t", r=2)
            kd = KE.rearrange("p (r t) -> p r t", r=2)
            for t in range(NT):
                if t >= 1:
                    pe.wait_ge(q.kd_ready, t)
                for r in range(2):
                    mm = nc.tensor.transpose(ps[:, 0, r * P:(r + 1) * P], kd[:, r, tok(t)], ident)
                mm.then_inc(q.kd_bank, 1)
                if t >= 2:
                    pe.wait_ge(q.o_scaled, t - 1)
                for h in range(4):
                    nc.tensor.matmul(ps[:, 1 + t % 2, h * C:(h + 1) * C], hattn[:, t, h, :], tm[:, t, T_V + h * C:T_V + (h + 1) * C],
                                     start=(h == 0), stop=True, skip_group_check=True)
                for c in range(2):
                    pe.wait_ge(q.s_ready, 2 * t + c + 1)
                    for r in range(2):
                        mm = nc.tensor.matmul(ps[half(c), 1 + t % 2, r * P:(r + 1) * P], qe[:, r, t * P + c * C:t * P + c * C + C],
                                              hs[:, r, :], start=False, stop=True, skip_group_check=True)
                    mm.then_inc(q.o_bank, 1)
                    pe.wait_ge(q.kd_ready, t + 1)
                    for r in range(2):
                        mm = nc.tensor.matmul(ps[:, 3 + c, r * P:(r + 1) * P], kdt[half(c), t % 2, r * P:(r + 1) * P],
                                              tm[half(c), t, T_V + r * P:T_V + (r + 1) * P], start=True, stop=True)
                    mm.then_inc(q.ds_bank, 1)

        def gdn_tensor(pe):
            q = gdn
            for j in range(8):
                pe.wait_ge(q.square_ready, j + 1)
                if j >= 2:
                    pe.wait_ge(q.sum_read, j - 1)
                nc.tensor.matmul(ps[:, j % 2, :], ones, gsq[j % 2][:, 0:SEQ], start=True, stop=True)
                nc.tensor.matmul(ps[:, 2 + j % 2, 0:DEC], ones, gsq[j % 2][:, SEQ:TV], start=True, stop=True).then_inc(q.sum_bank, 1)
            pe.wait_ge(q.gate_ready, 1)
            for k, m in enumerate((upto, const("after"), const("chunk0"), const("chunk1"))):
                mm = nc.tensor.matmul(ps[:, 4, k * gate_n:(k + 1) * gate_n], m, gg, start=True, stop=True)
            mm.then_inc(q.gates_bank, 1)
            pe.wait_ge(q.qk_ready, 8)
            pe.wait_ge(q.sum_read, 8)
            pe.wait_ge(q.gates_ready, 1)

            def hh(h):
                return slice(h * P, (h + 1) * P)

            def products(t):
                pe.wait_ge(q.ug_ready, t + 1)
                nc.tensor.matmul(ps[:, 0, :], ones, ug, start=True, stop=True).then_inc(q.row_bank, 1)
                for h in range(GH):
                    nc.tensor.matmul(ps[:, 1, hh(h)], conv[:, 4 + h, tok(t)], conv[:, 4 + h, tok(t)], start=True, stop=True)
                for h in range(GH):
                    mm = nc.tensor.matmul(ps[:, 2, hh(h)], conv[:, 4 + h, tok(t)], conv[:, h, tok(t)], start=True, stop=True)
                mm.then_inc(q.gram_bank, 1)
                for h in range(GH):
                    nc.tensor.transpose(ps[:, 6, hh(h)], conv[:, 4 + h, tok(t)], ident)
                for h in range(GH):
                    mm = nc.tensor.transpose(ps[:, 7, hh(h)], conv[:, 8 + h, tok(t)], ident)
                mm.then_inc(q.kv_bank, 1)

            def turn_gram(t):
                pe.wait_ge(q.gd_ready, t + 1)
                for h in range(GH):
                    mm = nc.tensor.transpose(ps[:, 0, hh(h)], GD[:, hh(h)], ident)
                mm.then_inc(q.gdt_bank, 1)

            def turn_a(t):
                pe.wait_ge(q.a_ready, t + 1)
                for h in range(GH):
                    mm = nc.tensor.transpose(ps[:, 1, hh(h)], A[:, hh(h)], ident)
                mm.then_inc(q.at_bank, 1)

            def invert(t):
                pe.wait_ge(q.kv_read, t + 1)
                for lv in range(5):
                    k = 5 * t + lv
                    pe.wait_ge(q.am_ready, k + 1)
                    pe.wait_ge(q.x_ready, k + 1)
                    if lv >= 1 or t >= 1:
                        pe.wait_ge(q.y_ready, k)
                    for h in range(GH):
                        mm = nc.tensor.matmul(ps[:, 2, hh(h)], AM[lv % 2][:, hh(h)], X[:, hh(h)], start=True, stop=True)
                    mm.then_inc(q.y_bank, 1)
                    pe.wait_ge(q.y_ready, k + 1)
                    for h in range(GH):
                        nc.tensor.matmul(ps[:, 6, hh(h)], Y[:, hh(h)], XT[:, hh(h)], start=True, stop=True)
                    for h in range(GH):
                        mm = nc.tensor.matmul(ps[:, 7, hh(h)], XT[:, hh(h)], Y[:, hh(h)], start=True, stop=True)
                    mm.then_inc(q.xx_bank, 1)

            def open_chunk(t, c):
                k = 2 * t + c
                pe.wait_ge(q.s_ready, k + 1)
                for h in range(GH):
                    mm = nc.tensor.matmul(ps[half(c), 3, hh(h)], NW[:, h * P + c * C:h * P + c * C + C], S[:, hh(h)],
                                          start=False, stop=True, skip_group_check=True)
                mm.then_inc(q.vn_bank, 1)
                if c == 0 and t >= 1:
                    pe.wait_ge(q.o_scaled, t)
                for h in range(GH):
                    nc.tensor.matmul(ps[half(c), 4, hh(h)], QG[t % 2][:, h * P + c * C:h * P + c * C + C], S[:, hh(h)],
                                     start=(h == 0), stop=True, skip_group_check=True)

            def close_chunk(t, c):
                pe.wait_ge(q.vn_ready, 2 * t + c + 1)
                for h in range(GH):
                    mm = nc.tensor.matmul(ps[:, 5, hh(h)], KD[t % 2][half(c), hh(h)], VN[half(c), hh(h)], start=True, stop=True)
                mm.then_inc(q.ds_bank, 1)
                for h in range(GH):
                    mm = nc.tensor.matmul(ps[half(c), 4, hh(h)], AT[t % 2][half(c), h * P + c * C:h * P + c * C + C], VN[half(c), hh(h)],
                                          start=False, stop=True, skip_group_check=True)
                mm.then_inc(q.o_bank, 1)

            products(0)
            turn_gram(0)
            turn_a(0)
            invert(0)
            for t in range(NT):
                more = t + 1 < NT
                pe.wait_ge(q.t_ready, t + 1)
                for h in range(GH):
                    mm = nc.tensor.matmul(ps[:, 2, hh(h)], KB[:, hh(h)], XT[:, hh(h)], start=True, stop=True)
                mm.then_inc(q.w_bank, 1)
                for h in range(GH):
                    nc.tensor.matmul(ps[:, 3, hh(h)], XT[:, hh(h)], VB[:, hh(h)], start=(h == 0), stop=True, skip_group_check=True)
                pe.wait_ge(q.w_ready, t + 1)
                pe.wait_ge(q.qg_ready, t + 1)
                open_chunk(t, 0)
                if more:
                    products(t + 1)
                close_chunk(t, 0)
                if more:
                    turn_gram(t + 1)
                open_chunk(t, 1)
                if more:
                    turn_a(t + 1)
                close_chunk(t, 1)
                if more:
                    invert(t + 1)

        def mla_tensor(pe):
            q = mla
            pe.wait_ge(q.loads, 64)
            pe.wait_ge(q.latent_ready, 1)
            for b in range(6):
                if b >= 2:
                    pe.wait_ge(q.lat_ready, b - 1)
                for j in range(4 * b, min(4 * b + 4, OWN_LAT + 1)):
                    rows = latents[j].shape[0]
                    mm = nc.tensor.transpose(ps[:, 7 * (b % 2), j % 4 * P:j % 4 * P + rows], latents[j], ident[0:rows, 0:rows])
                mm.then_inc(q.lat_bank, 1)

            def make(i):
                kind, tiles = mla_items[i]
                if i >= 2:
                    pe.wait_ge(q.rows_ready, i - 1)
                    pe.wait_ge(q.v_ready, min(i - 1, KEY_ITEMS))
                for u, n in enumerate(tiles):
                    bank = A_BANK[i] + u
                    if kind == "key":
                        j, rows = (n, P) if n < 12 else (OWN_LAT, DEC)
                        pe.wait_ge(q.lat_ready, j // 4 + 1)
                        mm = nc.tensor.matmul(ps[0:rows, bank, :], latT[:, j * P:j * P + rows], wkvb, start=True, stop=True)
                    else:
                        for c in range(2):
                            j = Q_LAT + 2 * n + c
                            pe.wait_ge(q.lat_ready, j // 4 + 1)
                            mm = nc.tensor.matmul(ps[:, bank, 0:384], latT[:, j * P:(j + 1) * P], wqb[:, c, :], start=(c == 0), stop=(c == 1))
                mm.then_inc(q.a_bank, 1)

            def turn(i):
                _, tiles = mla_items[i]
                pe.wait_ge(q.rows_ready, i + 1)
                if i == 1:
                    pe.wait_ge(q.lat_ready, 6)
                if i >= 2:
                    pe.wait_ge(q.kT_ready, min(i - 1, KEY_ITEMS))
                    if i - 1 > KEY_ITEMS:
                        pe.wait_ge(q.qT_ready, i - 1 - KEY_ITEMS)
                rows = DEC if tiles == (12,) else P
                for u in range(len(tiles)):
                    for h in range(4):
                        mm = nc.tensor.transpose(ps[0:96, B_BANK[i][u], h * P:h * P + rows],
                                                 mla_rows[i % 2][0:rows, (4 * u + h) * 96:(4 * u + h + 1) * 96], ident[0:rows, 0:rows])
                mm.then_inc(q.t_bank, 1)

            make(0)
            for i in range(10):
                if i < 9:
                    make(i + 1)
                turn(i)

            def scores(k):
                t, h = divmod(k, 4)
                m = P * (t + 1)
                if k >= 4:
                    pe.wait_ge(q.p_ready, k - 3)
                nc.tensor.matmul(ps[:, 4 + k % 4, 0:m], QT[0:96, t, h, :], KTp[0:96, h, 0:m], start=True, stop=False, skip_group_check=True)
                nc.tensor.matmul(ps[:, 4 + k % 4, t * P:m], const("early")[0:1, :], const("late")[0:1, :],
                                 start=False, stop=True, skip_group_check=True).then_inc(q.s_bank, 1)

            def weigh(k):
                t, h = divmod(k, 4)
                pe.wait_ge(q.pT_ready, k + 1)
                if h == 0 and t >= 2:
                    pe.wait_ge(q.o_ready, t - 1)
                for b in range(t + 1):
                    c0 = 512 * (k % 2) + b * P
                    mm = nc.tensor.matmul(ps[:, 2 + t % 2, h * C:(h + 1) * C], pT[:, c0:c0 + P], Vp[:, b, h * C:(h + 1) * C],
                                          start=(b == 0), stop=(b == t))
                mm.then_inc(q.av_done, 1)

            pe.wait_ge(q.kT_ready, KEY_ITEMS)
            pe.wait_ge(q.qT_ready, 3)
            for k in range(3):
                scores(k)
            for k in range(16):
                if k + 3 < 16:
                    scores(k + 3)
                pe.wait_ge(q.p_ready, k + 1)
                if k >= 2:
                    pe.wait_ge(q.pT_ready, k - 1)
                for b in range(k // 4 + 1):
                    c0 = 512 * (k % 2) + b * P
                    mm = nc.tensor.transpose(ps[:, k % 2, b * P:(b + 1) * P], pr[:, c0:c0 + P], ident)
                mm.then_inc(q.pT_bank, 1)
                if k >= 1:
                    weigh(k - 1)
            for h in range(4):
                for b in range(3):
                    a0, a1 = 512 * b, min(512 * (b + 1), PAST + DEC)
                    mm = nc.tensor.matmul(ps[32 * h:32 * h + 32, 5 + b, 0:a1 - a0], QT[0:96, 4, h, 0:DEC], KTs[0:96, h, a0:a1],
                                          start=True, stop=True, skip_group_check=True)
            mm.then_inc(q.s_bank, 1)
            weigh(15)
            pe.wait_ge(q.pn_ready, 1)
            pe.wait_ge(q.o_ready, 4)
            for b in range(9):
                r = min(P, PAST + DEC - b * P)
                mm = nc.tensor.transpose(ps[0:r, b // 4, b % 4 * P:b % 4 * P + P], pr[:, b * P:b * P + r], ident)
            mm.then_inc(q.pT_bank, 1)
            pe.wait_ge(q.pT_ready, 17)
            for h in range(4):
                for b in range(9):
                    r = min(P, PAST + DEC - b * P)
                    mm = nc.tensor.matmul(ps[0:DEC, 3, h * C:(h + 1) * C], pT[0:r, b * P + 32 * h:b * P + 32 * h + 32],
                                          Vs[0:r, b, h * C:(h + 1) * C], start=(b == 0), stop=(b == 8))
            mm.then_inc(q.o_bank, 1)

        def out_tensor(pe):
            q = outp
            for t in range(NT):
                if t >= 2:
                    pe.wait_ge(q.copy_v, t - 1)
                    pe.wait_ge(q.copy_a, t - 1)
                for c, col in enumerate(MIX_COLS):
                    mm = nc.tensor.transpose(ps[:, 2 * (t % 2) + c // 4, c % 4 * P:c % 4 * P + P], tm[:, t, col:col + P], ident)
                mm.then_inc(q.t_banks, 1)
                pe.wait_ge(q.copy_v, t + 1)
                pe.wait_ge(q.copy_a, t + 1)
                for k in range(2):
                    pe.wait_ge(q.w_ready[k], 16)
                    if t >= 2:
                        pe.wait_ge(q.x_ready, 2 * (t - 2) + k + 1)
                    for c in range(KC):
                        mm = nc.tensor.matmul(ps[:, 4 + 2 * (t % 2) + k, :], mT[t % 2][:, c * P:(c + 1) * P], w_out_sb[k][:, c, :],
                                              start=(c == 0), stop=(c == KC - 1))
                    mm.then_inc(q.o_bank, 1)

        def peer_tensor(pe, l):
            q = peer
            norm_transposes(pe, q)
            pe.wait_ge(q.keys_loaded, 32)
            for j in range(16):
                mm = nc.tensor.transpose(ps[:, 4 + j // 4, j % 4 * P:j % 4 * P + P], keys[:, j, :], ident)
            mm.then_inc(q.keys_bank, 1)
            pe.wait_ge(q.h_copy_v, NT)
            pe.wait_ge(q.h_copy_a, NT)

            def scores(j):
                pe.wait_ge(q.keys_ready, 1)
                pe.wait_ge(q.q_ready, j + 1)
                if j >= 2:
                    pe.wait_ge(q.top_done, j - 1)
                for t in range(4):
                    nc.tensor.matmul(ps[:, 4 + j % 2, tok(t)], qT[j % 2][:, tok(t)], keysT[:, j, :], start=True, stop=True)
                nc.tensor.matmul(ps[0:DEC, 6 + j % 2, 0:P], qT[j % 2][:, SEQ:TV], keysT[:, j, :], start=True, stop=True).then_inc(q.s_bank, 1)

            for j in range(16):
                pe.wait_ge(q.wcol_ready[j % 3], 16 * (j // 3 + 1))
                if j >= 2:
                    pe.wait_ge(q.q_ready, j - 1)
                w = wcol[j % 3].rearrange("p (c n) -> p c n", c=KC)
                for c in range(KC):
                    nc.tensor.matmul(ps[:, j % 2, :], w[:, c, :], hT[:, c, 0:SEQ], start=(c == 0), stop=(c == KC - 1))
                    mm = nc.tensor.matmul(ps[:, 2 + j % 2, 0:DEC], w[:, c, :], hT[:, c, SEQ:TV], start=(c == 0), stop=(c == KC - 1))
                mm.then_inc(q.q_bank, 1)
                if j >= 1:
                    scores(j - 1)
                pe.wait_ge(q.q_bank, j + 1)
                pe.sem_inc(q.wcol_used, 1)
            scores(15)
            pe.wait_ge(q.q_ready, 16)
            pe.wait_ge(q.top_done, 16)
            for t in range(NT):
                R, ne = (P, P) if t < 4 else (DEC, DEC)
                b = 2 * (t % 2)
                if t >= 2:
                    pe.wait_ge(q.acc_read, t - 1)
                for k in range(2):
                    nc.tensor.matmul(ps[0:R, b + k, :], zeros[:, 0:R], xb[:, 0, 0:512], start=True, stop=False, skip_group_check=True)
                with pe.Fori(0, ne // 4) as g:
                    for k in range(4):
                        pe.wait_ge(q.v_loaded[k], (g + l * GROUPS + (t * (P // 4) + 1)) * 16)
                        pe.wait_ge(q.diag_ready, g * 4 + (t * P + k + 1))
                        pe.sem_inc(q.pe_done, 1)
                        for n in range(2):
                            mm = nc.tensor.matmul(ps[0:R, b + n, :], diag[k][:, 0:R], ring[4 + k][:, n * 512:(n + 1) * 512],
                                                  start=False, stop=False, skip_group_check=True)
                        mm.then_inc(q.v_free, 1)
                for k in range(2):
                    mm = nc.tensor.matmul(ps[0:R, b + k, :], zeros[:, 0:R], xb[:, 0, 0:512], start=False, stop=True, skip_group_check=True)
                mm.then_inc(q.acc_bank, 1)

        @block.tensor
        def _(pe):
            pe.wait_ge(start_loaded, 7 * 16)
            with pe.Fori(0, DEPTH) as l:
                project_tensor(pe)
                meet(pe, 1)
                hgrn_tensor(pe)
                meet(pe, 2)
                gdn_tensor(pe)
                meet(pe, 3)
                mla_tensor(pe)
                meet(pe, 4)
                out_tensor(pe)
                meet(pe, 5)
                peer_tensor(pe, l)
                meet(pe, 6)
                next_layer(pe, l)

        V = nc.vector

        def norm_vector(v, q):
            v.wait_ge(q.rs_ready, 1)
            v.wait_ge(q.gain_ready, 16)
            for t in range(NT):
                V.scalar_tensor_tensor(xb[:, t, :], x[:, t, :], rs[:, t:t + 1], gain[:, :], ALU.mult, ALU.mult).then_inc(q.xb_ready, 1)
            for t in range(NT):
                v.wait_ge(q.h_banks, t + 1)
                V.tensor_copy(hT[:, 0:4, tok(t)], ps[:, 2 * (t % 2), :].rearrange("p (c t) -> p c t", c=4)).then_inc(q.h_copy_v, 1)

        def project_vector(v, l):
            q, done = project, Count()
            V.tensor_copy(lb, lb_all[:, bass.ds(l, 1), :].rearrange("p o n -> p (o n)"))
            V.memset(conv[:, :, TV:TP], 0.0)
            V.memset(zf.rearrange("p (r t) -> p r t", r=2)[:, :, TV:TP], 0.0)
            V.memset(qh.rearrange("p (r t) -> p r t", r=2)[:, :, TV:TP], 0.0)
            V.memset(raw[0][:, 0:3], 0.0)
            V.memset(raw[1][:, 0:3], 0.0).then_inc(q.zero_set, 1)
            norm_vector(v, q)
            v.wait_ge(q.wh_bank, 1)
            V.tensor_copy(wh, ps[:, 4, 0:84].rearrange("p (j w) -> p j w", j=NJ)).then_inc(q.wh_ready, 1)
            v.wait_ge(q.wh_ready, 1)
            v.wait_ge(q.zero_set, 1)
            for j in range(NJ):
                r, y = raw[j % 2], conv_y[j % 2]
                if j >= 2:
                    v.wait_ge(q.y_ready, j - 1)
                V.tensor_copy(r[:, 515:518], wh[:, j, 4:7]).then_inc(q.v_done, done.up())
                v.wait_ge(q.v_done, done.n)
                v.wait_ge(q.raw_ready, 2 * (j + 1))
                V.tensor_copy(tails[:, j, 0:3], r[:, 512:515])
                V.tensor_copy(tails[:, j, 3:6], r[:, 547:550]).then_inc(q.tails_in, 1)
                if j >= 2:
                    v.wait_ge(q.silu_done, j - 1)
                V.tensor_scalar(y, r[:, 0:547], wh[:, j, 0:1], None, ALU.mult).then_inc(q.v_done, done.up())
                for w in range(1, 4):
                    v.wait_ge(q.v_done, done.n)
                    ins = V.scalar_tensor_tensor(y, r[:, w:w + 547], wh[:, j, w:w + 1], y, ALU.mult, ALU.add)
                    if w < 3:
                        ins.then_inc(q.v_done, done.up())
                ins.then_inc(q.y_ready, 1)
            for g, (_, m, col, _) in enumerate(TM_GROUPS):
                if g in (0, 2):
                    continue
                for t in range(NT):
                    k = g * NT + t
                    v.wait_ge(q.tm_bank, k + 1)
                    V.tensor_copy(tm[:, t, col:col + m], ps[:, 4 + k % 4, 0:m]).then_inc(q.tm_read_v, 1)
            v.wait_ge(q.tail_bank, 1)
            V.tensor_copy(region_v[0:6, 0:QKV], ps[0:6, 0:3, :].rearrange("p b n -> p (b n)")).then_inc(q.tail_ready, 1)

        def hgrn_vector(v):
            q, done = hgrn, Count()
            V.memset(hs_init, 0.0).then_inc(q.init_zero, 1)
            V.memset(hs, 0.0).then_inc(q.v_done, done.up())
            V.memset(hattn, 0.0).then_inc(q.v_done, done.up())
            v.wait_ge(q.v_done, done.n)
            v.wait_ge(q.e1, 1)
            V.scalar_tensor_tensor(KE, zf, 0.0, E, ALU.min, ALU.subtract).then_inc(q.v_done, done.up())
            v.wait_ge(q.v_done, done.n)
            V.tensor_tensor(QE, KE, zf, ALU.subtract).then_inc(q.nlsig, 1)
            for r in range(2):
                s = slice(r * TP, (r + 1) * TP)
                ins = V.tensor_scalar(B[:, s], KE[:, s], lb[:, 2 + r:3 + r], None, ALU.add)
            ins.then_inc(q.bprime, 1)
            v.wait_ge(q.lf, 1)
            for r in range(2):
                s = slice(r * TP, (r + 1) * TP)
                ins = V.scalar_tensor_tensor(KE[:, s], B[:, s], lb[:, r:r + 1], E[:, s], ALU.max, ALU.add)
            ins.then_inc(q.v_done, done.up())
            v.wait_ge(q.v_done, done.n)
            v.wait_ge(q.k_ready, 1)
            for r in range(2):
                V.memset(KE[:, r * TP + TV:(r + 1) * TP], 0.0)
                ins = V.memset(zf[:, r * TP + TV:(r + 1) * TP], 0.0)
            ins.then_inc(q.v_done, done.up())
            v.wait_ge(q.v_done, done.n)
            for r in range(2):
                s = slice(r * TP, (r + 1) * TP)
                ins = V.tensor_tensor_scan(B[:, s], const("carry"), KE[:, s], 0.0, ALU.mult, ALU.add)
            ins.then_inc(q.scanned, 1)
            v.wait_ge(q.scanned, 1)
            v.sem_inc(q.qe_ready, 1)
            v.sem_inc(q.ke_ready, 1)

            def read_level(lv):
                mask = ident if lv == 0 else const(f"half{2 ** (lv - 1)}")
                for t in range(NT):
                    k = lv * NT + t
                    v.wait_ge(q.lev_bank, k + 1)
                    for h in range(2):
                        ins = V.copy_predicated(hattn[:, t, h::2, :], per_head(mask.bitcast(U32), 2),
                                                ps[:, 2 * (k % 4) + h, 0:256].rearrange("p (h t) -> p h t", h=2))
                    ins.then_inc(q.lev_read, 1)

            for lv in range(1, 7):
                b = 2 ** (lv - 1)
                b4 = B.rearrange("p (n w) -> p n w", w=2 * b)
                if lv >= 2:
                    v.wait_ge(q.ke_ready, lv)
                    v.wait_ge(q.qe_ready, lv)
                V.tensor_tensor(E.rearrange("p (n w) -> p n w", w=2 * b), b4, b4[:, :, b - 1:b].to_broadcast([P, TP // b, 2 * b]),
                                ALU.subtract).then_inc(q.diff, 1)
                read_level(lv - 1)
                v.wait_ge(q.ediff, lv)
                V.tensor_tensor(QE, qh, E, ALU.mult).then_inc(q.qe_ready, 1)
            read_level(6)
            v.wait_ge(q.lev_read, 7 * NT)
            c3 = B.rearrange("p (n w) -> p n w", w=C)
            V.tensor_tensor(KE.rearrange("p (n w) -> p n w", w=C), c3[:, :, C - 1:C].to_broadcast([P, 2 * TP // C, C]), c3, ALU.subtract).then_inc(q.diff, 1)
            v.wait_ge(q.eb, 1)
            V.tensor_tensor(QE, qh, E, ALU.mult).then_inc(q.v_done, done.up())
            v.wait_ge(q.ed, 1)
            V.tensor_tensor(KE, zf, KE, ALU.mult).then_inc(q.v_done, done.up())
            v.wait_ge(q.v_done, done.n)
            v.sem_inc(q.decayed, 1)
            v.sem_inc(q.s_ready, 1)
            v.wait_ge(q.ebl_ready, 1)
            v.wait_ge(q.gg_ready, 1)
            eb3 = ebl.rearrange("p (r n) -> p r n", r=2)
            for t in range(NT):
                v.wait_ge(q.kd_bank, t + 1)
                V.tensor_copy(kdt[:, t % 2, :], ps[:, 0, 0:256]).then_inc(q.kd_ready, 1)
                for c in range(2):
                    k = 2 * t + c
                    v.wait_ge(q.ds_bank, k + 1)
                    V.tensor_tensor(hds.rearrange("p (r e) -> p r e", r=2), ps[:, 3 + c, 0:256].rearrange("p (r e) -> p r e", r=2),
                                    per_head(const("diagonal"), 2), ALU.mult).then_inc(q.v_done, done.up())
                    v.wait_ge(q.v_done, done.n)
                    for r in range(2):
                        ins = V.scalar_tensor_tensor(hs[:, r, :], hs[:, r, :], eb3[:, r, k:k + 1], hds[:, r * P:(r + 1) * P], ALU.mult, ALU.add)
                    if k in (7, 9):
                        ins.then_inc(q.v_done, done.up())
                        v.wait_ge(q.v_done, done.n)
                        ins = V.tensor_copy(hs_out[:, k // 8, :, :], hs)
                        ins.then_inc(q.s_saved, 1)
                        if k == 7:
                            v.wait_ge(q.s_saved, 1)
                            v.wait_ge(q.init_ready, 64)
                            ins = V.tensor_copy(hs, hs_init.rearrange("p (r e) -> p r e", r=2))
                            ins.then_inc(q.s_ready, 1)
                    else:
                        ins.then_inc(q.s_ready, 1)
                    if k < 9:
                        v.wait_ge(q.s_ready, k + 2)
                v.wait_ge(q.osq, t + 1)
                V.tensor_reduce(ss[:, 0:4], hosq.rearrange("p (h n) -> p h n", h=4), AX.X, ALU.add).then_inc(q.oss, 1)
                v.wait_ge(q.ors, t + 1)
                V.tensor_tensor(hosq.rearrange("p (h n) -> p h n", h=4), ps[:, 1 + t % 2, 0:256].rearrange("p (h n) -> p h n", h=4),
                                heads(sr[:, 0:4], C), ALU.mult).then_inc(q.o_scaled, 1)
                v.wait_ge(q.o_scaled, t + 1)
                V.tensor_tensor(tm[:, t, T_G:T_G + 256], hosq, tm[:, t, T_G:T_G + 256], ALU.mult).then_inc(q.o_done, 1)

        def gdn_vector(v):
            q, done = gdn, Count()
            V.memset(S, 0.0).then_inc(q.v_done, done.up())
            V.memset(VN, 0.0).then_inc(q.v_done, done.up())
            ba = tm[:, :, T_BA:T_BA + 8]
            b3 = beta.rearrange("p (t h) -> p t h", t=NT)
            g3 = gg.rearrange("p (t h) -> p t h", t=NT)
            t3 = gt.rearrange("p (t h) -> p t h", t=NT)
            V.tensor_tensor(g3, ba[:, :, 4:8], per_head(gdn_par[:, 4:8], NT), ALU.add).then_inc(q.alpha, 1)
            v.wait_ge(q.bexp, 1)
            V.tensor_scalar(beta, beta, 1.0, None, ALU.add).then_inc(q.v_done, done.up())
            v.wait_ge(q.v_done, done.n)
            V.reciprocal(beta, beta).then_inc(q.v_done, done.up())
            v.wait_ge(q.soft, 1)
            v.wait_ge(q.nega, 1)
            V.scalar_tensor_tensor(gg, gg, 0.0, gt, ALU.max, ALU.add).then_inc(q.v_done, done.up())
            v.wait_ge(q.v_done, done.n)
            V.scalar_tensor_tensor(g3, g3, -1.0, per_head(gdn_par[:, 0:4], NT), ALU.mult, ALU.mult).then_inc(q.v_done, done.up())
            v.wait_ge(q.v_done, done.n)
            V.tensor_tensor(g3, g3, heads(const("valid"), GH), ALU.mult).then_inc(q.gate_ready, 1)
            for j in range(8):
                v.wait_ge(q.norm_ready, j + 1)
                ins = V.scalar_tensor_tensor(conv[:, j, 0:TV], conv[:, j, 0:TV], P ** -0.5 if j < 4 else 1.0, grs[j % 2], ALU.mult, ALU.mult)
                ins.then_inc(q.qk_ready, 1)
            v.wait_ge(q.gates_bank, 1)
            v.wait_ge(q.gexp_ready, 1)
            V.tensor_copy(gcs, ps[:, 4, 0:gate_n]).then_inc(q.v_done, done.up())
            V.tensor_tensor(begc, beta, egc, ALU.mult).then_inc(q.v_done, done.up())
            v.wait_ge(q.v_done, done.n)
            v.sem_inc(q.gates_ready, 1)
            v.sem_inc(q.s_ready, 1)

            def h3(ap):
                return ap.rearrange("p (h n) -> p h n", h=GH)

            def col(ap, t):
                return heads(ap[:, t * GH:(t + 1) * GH])

            def log_decay(t):
                v.wait_ge(q.row_bank, t + 1)
                V.tensor_tensor(h3(DT), h3(ps[:, 0, :]), col(gcs, t), ALU.subtract).then_inc(q.v_done, done.up())
                v.wait_ge(q.v_done, done.n)
                V.tensor_scalar(DT, DT, 0.0, None, ALU.min).then_inc(q.diff_ready, 1)

            def decayed(t):
                v.wait_ge(q.kv_bank, t + 1)
                V.tensor_tensor(h3(KB), h3(ps[:, 6, :]), col(begc, t), ALU.mult)
                V.tensor_tensor(h3(KD[t % 2]), h3(ps[:, 6, :]), col(erest, t), ALU.mult)
                V.tensor_tensor(h3(VB), h3(ps[:, 7, :]), col(beta, t), ALU.mult).then_inc(q.kv_read, 1)
                v.wait_ge(q.edt_ready, t + 1)
                V.tensor_tensor(h3(DT), h3(DT), per_head(upto), ALU.mult).then_inc(q.v_done, done.up())
                v.wait_ge(q.v_done, done.n)
                v.wait_ge(q.gram_bank, t + 1)
                V.tensor_tensor(AT[t % 2], ps[:, 2, :], DT, ALU.mult)
                V.tensor_tensor(GD, ps[:, 1, :], DT, ALU.mult).then_inc(q.gd_ready, 1)

            def first_inverse(t):
                v.wait_ge(q.gdt_bank, t + 1)
                V.tensor_tensor(h3(A), h3(ps[:, 0, :]), col(beta, t), ALU.mult).then_inc(q.a_ready, 1)
                v.wait_ge(q.a_ready, t + 1)
                V.tensor_tensor(h3(X), h3(A), per_head(const("half1t")), ALU.mult)
                v.wait_ge(q.atf_ready, t + 1)
                V.tensor_tensor(h3(XT), h3(ATF), per_head(const("half1")), ALU.mult).then_inc(q.v_done, done.up())
                v.wait_ge(q.v_done, done.n)
                V.tensor_tensor(h3(X), per_head(ident), h3(X), ALU.subtract)
                V.tensor_tensor(h3(XT), per_head(ident), h3(XT), ALU.subtract).then_inc(q.x_ready, 1)

            def level(t, lv):
                v.wait_ge(q.xx_bank, 5 * t + lv + 1)
                if lv < 4:
                    V.tensor_tensor(X, X, ps[:, 7, :], ALU.subtract)
                ins = V.tensor_tensor(XT, XT, ps[:, 6, :], ALU.subtract)
                if lv < 4:
                    ins.then_inc(q.x_ready, 1)
                    v.wait_ge(q.x_ready, 5 * t + lv + 2)
                else:
                    ins.then_inc(q.t_ready, 1)

            def new_values(k):
                c = k % 2
                v.wait_ge(q.vn_bank, k + 1)
                V.tensor_copy(VN[half(c), :], ps[half(c), 3, :]).then_inc(q.vn_ready, 1)

            def new_state(k):
                t, c = divmod(k, 2)
                v.wait_ge(q.ds_bank, k + 1)
                v.wait_ge(q.s_ready, k + 1)
                for h in range(GH):
                    hh = slice(h * P, (h + 1) * P)
                    ins = V.scalar_tensor_tensor(S[:, hh], S[:, hh], egl[:, c * gate_n + t * GH + h:c * gate_n + t * GH + h + 1],
                                                 ps[:, 5, hh], ALU.mult, ALU.add)
                if k in (7, 9):
                    ins.then_inc(q.v_done, done.up())
                    v.wait_ge(q.v_done, done.n)
                    V.tensor_copy(gs_out[:, k // 8, :], S).then_inc(q.s_saved, 1)
                    if k == 7:
                        v.wait_ge(q.s_saved, 1)
                        v.wait_ge(q.init_ready, 16)
                        V.tensor_copy(S, gs_init).then_inc(q.s_ready, 1)
                else:
                    ins.then_inc(q.s_ready, 1)

            def output(t, step):
                if step == 0:
                    v.wait_ge(q.osq, t + 1)
                    V.tensor_reduce(ss[:, 0:4], h3(OSQ), AX.X, ALU.add).then_inc(q.oss, 1)
                elif step == 1:
                    v.wait_ge(q.ors, t + 1)
                    V.tensor_tensor(h3(OSQ), h3(ps[:, 4, :]), heads(sr[:, 0:4]), ALU.mult).then_inc(q.o_scaled, 1)
                else:
                    v.wait_ge(q.o_scaled, t + 1)
                    v.wait_ge(q.zg_ready, t + 1)
                    V.tensor_tensor(tm[:, t, 0:512], OSQ, ZG, ALU.mult).then_inc(q.o_done, 1)

            log_decay(0)
            decayed(0)
            first_inverse(0)
            for lv in range(5):
                level(0, lv)
            for t in range(NT):
                more = t + 1 < NT
                new_values(2 * t)
                if more:
                    log_decay(t + 1)
                new_state(2 * t)
                if more:
                    decayed(t + 1)
                new_values(2 * t + 1)
                if more:
                    first_inverse(t + 1)
                new_state(2 * t + 1)
                for lv in range(5):
                    if more:
                        level(t + 1, lv)
                    if lv < 3:
                        output(t, lv)

        def rope(v, q, done, dst, src, cos, sin, tmp):
            x1, x2 = src
            d1, d2 = dst
            V.tensor_tensor(tmp[0], x1, cos, ALU.mult)
            V.tensor_tensor(tmp[1], x2, sin, ALU.mult)
            V.tensor_tensor(tmp[2], x1, sin, ALU.mult)
            V.tensor_tensor(tmp[3], x2, cos, ALU.mult).then_inc(q.v_done, done.up())
            v.wait_ge(q.v_done, done.n)
            V.tensor_tensor(d1, tmp[0], tmp[1], ALU.subtract)
            return V.tensor_tensor(d2, tmp[2], tmp[3], ALU.add)

        def mla_vector(v):
            q, done = mla, Count()
            v.wait_ge(q.csq, 1)
            for k, (a, m) in enumerate(((0, 256), (256, 128), (384, 32))):
                ins = V.tensor_reduce(ss[:, 5 * k:5 * k + 5], csq[:, :, a:a + m], AX.X, ALU.add)
            ins.then_inc(q.css, 1)
            v.wait_ge(q.crs, 1)
            for k, (a, m) in enumerate(((0, 256), (256, 128), (384, 32))):
                ins = V.tensor_tensor(csq[:, :, a:a + m], tm[:, :, T_C + a:T_C + a + m], heads(sr[:, 5 * k:5 * k + 5], m), ALU.mult)
            ins.then_inc(q.v_done, done.up())
            v.wait_ge(q.v_done, done.n)
            V.tensor_tensor(tm[:, :, T_C:T_C + 416], csq, per_head(lora_gain, NT), ALU.mult).then_inc(q.v_done, done.up())
            v.wait_ge(q.v_done, done.n)
            cos, sin = (const(n_).rearrange("p (t n) -> p t n", t=NT) for n_ in ("cos", "sin"))
            tmp = [rot[:, k * 80:(k + 1) * 80].rearrange("p (t n) -> p t n", t=NT) for k in range(4)]
            kp = tm[:, :, T_C + 384:T_C + 416]
            rope(v, q, done, (kp[:, :, 0:16], kp[:, :, 16:32]), (kp[:, :, 0:16], kp[:, :, 16:32]), cos, sin, tmp).then_inc(q.latent_ready, 1)
            v.wait_ge(q.latent_ready, 1)
            v.wait_ge(q.loads, 64)
            for i, (kind, tiles) in enumerate(mla_items):
                U, R = len(tiles), slice(0, DEC if tiles == (12,) else P)
                rows_i = mla_rows[i % 2][R, 0:384 * U]
                r4 = rows_i.rearrange("p (u h n) -> p u h n", u=U, h=4)
                rh = rows_i.rearrange("p (k n) -> p k n", n=96)
                bank = ps[R, A_BANK[i]:A_BANK[i] + U, :]
                inv = [mla_sr[R, k * 4 * U:(k + 1) * 4 * U].rearrange("p (u h) -> p u h", u=U).unsqueeze(3) for k in range(2)]
                v.wait_ge(q.sq, i + 1)
                if kind == "key":
                    V.tensor_reduce(mla_ss[R, 0:4 * U], mla_sq[R, 0:256 * U].rearrange("p (k n) -> p k n", n=C), AX.X, ALU.add).then_inc(q.ssum, 1)
                else:
                    s3 = mla_sq[R, 0:384 * U].rearrange("p (k n) -> p k n", n=96)
                    V.tensor_reduce(mla_ss[R, 0:4 * U], s3[:, :, 0:64], AX.X, ALU.add)
                    V.tensor_reduce(mla_ss[R, 4 * U:8 * U], s3[:, :, 64:96], AX.X, ALU.add).then_inc(q.ssum, 1)
                v.wait_ge(q.rs, i + 1)
                if i >= 2:
                    v.wait_ge(q.t_bank, i - 1)
                if kind == "key":
                    if tiles == (12,):
                        kpe = tm[R, 4:5, T_C + 384:T_C + 416]
                    elif i < 2:
                        kpe = tm[:, 2 * i:2 * i + 2, T_C + 384:T_C + 416]
                    else:
                        kpe = past_k[:, 2 * i - 4:2 * i - 2, :]
                    V.tensor_copy(r4[:, :, :, 64:96], kpe.unsqueeze(2).to_broadcast([R.stop, U, 4, 32]))
                    b4 = bank.rearrange("p u (h n) -> p u h n", h=4)
                    V.tensor_tensor(r4[:, :, :, 0:64], b4[:, :, :, 0:64], inv[0].to_broadcast([R.stop, U, 4, 64]), ALU.mult).then_inc(q.v_done, done.up())
                    v.wait_ge(q.v_done, done.n)
                    V.tensor_tensor(rh[:, :, 0:64], rh[:, :, 0:64], per_head(knope_gain[R, :], 4 * U), ALU.mult).then_inc(q.rows_ready, 1)
                else:
                    b4 = bank[:, :, 0:384].rearrange("p u (h n) -> p u h n", h=4)
                    qr = mla_qr[:, 0:128 * U]
                    qr4, qrh = qr.rearrange("p (u h n) -> p u h n", u=U, h=4), qr.rearrange("p (k n) -> p k n", n=32)
                    V.tensor_tensor(r4[:, :, :, 0:64], b4[:, :, :, 0:64], inv[0].to_broadcast([P, U, 4, 64]), ALU.mult)
                    V.tensor_tensor(qr4, b4[:, :, :, 64:96], inv[1].to_broadcast([P, U, 4, 32]), ALU.mult).then_inc(q.v_done, done.up())
                    v.wait_ge(q.v_done, done.n)
                    V.tensor_tensor(rh[:, :, 0:64], rh[:, :, 0:64], per_head(qnope_gain, 4 * U), ALU.mult)
                    V.tensor_tensor(qrh, qrh, per_head(qrope_gain, 4 * U), ALU.mult).then_inc(q.v_done, done.up())
                    v.wait_ge(q.v_done, done.n)
                    tmp = [rot[:, k * 64 * U:(k + 1) * 64 * U].rearrange("p (u h n) -> p u h n", u=U, h=4) for k in range(4)]
                    cs = [w[:, tiles[0]:tiles[0] + U, :].unsqueeze(2).to_broadcast([P, U, 4, 16]) for w in (cos, sin)]
                    rope(v, q, done, (r4[:, :, :, 64:80], r4[:, :, :, 80:96]), (qr4[:, :, :, 0:16], qr4[:, :, :, 16:32]), cs[0], cs[1],
                         tmp).then_inc(q.rows_ready, 1)
                if 1 <= i <= KEY_ITEMS:
                    keep_keys(v, i - 1)

            def finish(t):
                v.wait_ge(q.p_ready, 4 * t + 4)
                V.reciprocal(mla_rsum[:, 4 * t:4 * t + 4], mla_sum[:, 4 * t:4 * t + 4]).then_inc(q.v_done, done.up())
                v.wait_ge(q.v_done, done.n)
                v.wait_ge(q.av_done, 4 * t + 4)
                V.tensor_tensor(tm[:, t, T_C:T_C + 256].rearrange("p (h n) -> p h n", h=4),
                                ps[:, 2 + t % 2, 0:256].rearrange("p (h n) -> p h n", h=4), heads(mla_rsum[:, 4 * t:4 * t + 4], C),
                                ALU.mult).then_inc(q.o_ready, 1)

            for k in range(17):
                v.wait_ge(q.s_bank, k + 1)
                s = ps[:, 4 + k % 4, 0:P * (k // 4 + 1)] if k < 16 else ps[:, 5:8, :].rearrange("p b n -> p (b n)")[:, 0:PAST + DEC]
                V.tensor_reduce(mla_mx[:, k:k + 1], s, AX.X, ALU.max).then_inc(q.mx, 1)
                v.wait_ge(q.mx, k + 1)
                V.tensor_scalar(mla_nm[:, k:k + 1], mla_mx[:, k:k + 1], -SCALE, None, ALU.mult).then_inc(q.nm, 1)
                if k % 4 == 1 and k >= 5:
                    finish(k // 4 - 1)
            finish(3)
            v.wait_ge(q.p_ready, 17)
            V.reciprocal(mla_rsum[:, 16:17], mla_sum[:, 16:17]).then_inc(q.v_done, done.up())
            v.wait_ge(q.v_done, done.n)
            V.tensor_scalar(pr, pr, mla_rsum[:, 16:17], None, ALU.mult).then_inc(q.pn_ready, 1)
            v.wait_ge(q.o_bank, 1)
            V.tensor_copy(tm[0:DEC, 4, T_C:T_C + 256], ps[0:DEC, 3, 0:256]).then_inc(q.o_ready, 1)

        def keep_keys(v, i):
            v.wait_ge(mla.t_bank, i + 1)
            tiles = mla_items[i][1]
            for u, n in enumerate(tiles):
                rows = P if n < 12 else DEC
                src = ps[0:96, B_BANK[i][u], :].rearrange("p (h n) -> p h n", h=4)[:, :, 0:rows]
                if n < 4:
                    ins = V.tensor_copy(KTp[0:96, :, tok(n)], src)
                else:
                    ins = V.tensor_copy(KTs[0:96, :, (n - 4) * P:(n - 4) * P + rows], src)
            ins.then_inc(mla.kT_ready, 1)

        def out_vector(v):
            q = outp
            for t in range(NT):
                v.wait_ge(q.t_banks, t + 1)
                if t >= 2:
                    v.wait_ge(q.o_bank, 2 * (t - 1))
                V.tensor_copy(mT[t % 2][:, 0:512], ps[:, 2 * (t % 2), :]).then_inc(q.copy_v, 1)
                if t >= 1:
                    add_out(v, t - 1)
            add_out(v, NT - 1)

        def add_out(v, t):
            q = outp
            for k in range(2):
                v.wait_ge(q.o_bank, 2 * t + k + 1)
                R = slice(0, P if t < 4 else DEC)
                V.tensor_tensor(x[R, t, k * 512:(k + 1) * 512], x[R, t, k * 512:(k + 1) * 512], ps[R, 4 + 2 * (t % 2) + k, :],
                                ALU.add).then_inc(q.x_ready, 1)

        def peer_vector(v, l):
            q, done = peer, Count()
            norm_vector(v, q)
            v.wait_ge(q.keys_bank, 1)
            V.tensor_copy(keysT, ps[:, 4:8, :].rearrange("p b (j n) -> p (b j) n", j=4)).then_inc(q.keys_ready, 1)
            def best_keys(j):
                v.wait_ge(q.s_bank, j + 1)
                for t in range(NT):
                    R = slice(0, P if t < 4 else DEC)
                    s = ps[R, 4 + j % 2, tok(t)] if t < 4 else ps[R, 6 + j % 2, 0:P]
                    w = work[t % 2]
                    tv, ti = top[R, t, j // 2, j % 2, :], top_i[R, t, j // 2, j % 2, :]
                    V.max(tv[:, 0:8], s).then_inc(q.v_done, done.up())
                    v.wait_ge(q.v_done, done.n)
                    V.match_replace(w[R, :], tv[:, 0:8], s, -3e38).then_inc(q.v_done, done.up())
                    ins = V.max_index(ti[:, 0:8], tv[:, 0:8], s)
                    if t == NT - 1:
                        ins.then_inc(q.top_done, 1)
                    v.wait_ge(q.v_done, done.n)
                    V.max(tv[:, 8:16], w[R, :]).then_inc(q.v_done, done.up())
                    v.wait_ge(q.v_done, done.n)
                    V.max_index(ti[:, 8:16], tv[:, 8:16], w[R, :]).then_inc(q.v_done, done.up())
                    v.wait_ge(q.v_done, done.n)

            steps = 12

            def numbers(ts, hs):
                for R, tt in ((slice(0, P), [t for t in ts if t < 4]), (slice(0, DEC), [t for t in ts if t == 4])):
                    if tt:
                        tt = slice(tt[0], tt[-1] + 1)
                        V.tensor_copy(top_f[R, tt, hs], top_i[R, tt, hs]).then_inc(q.v_done, done.up())
                        v.wait_ge(q.v_done, done.n)
                        f = top_f[R, tt, hs, 0, :]
                        V.tensor_scalar(f, f, float(P), None, ALU.mult).then_inc(q.v_done, done.up())
                v.wait_ge(q.v_done, done.n)

            def pair_sums(t, h0=0, h1=EH):
                R = slice(0, P if t < 4 else DEC)
                if t >= 1:
                    v.wait_ge(q.sel_step, steps * EH * t)
                for src, dst in ((top, cand), (top_f, cidx)):
                    off = 0
                    for a, na, nb in PAIR_ROWS:
                        shape = [R.stop, h1 - h0, na, nb]
                        s0 = src[R, t, h0:h1, 0, a:a + na].unsqueeze(3).to_broadcast(shape)
                        s1 = src[R, t, h0:h1, 1, 0:nb].unsqueeze(2).to_broadcast(shape)
                        d = dst[R, :].rearrange("p (h n) -> p h n", h=EH)[:, h0:h1, off:off + na * nb].rearrange("p h (a b) -> p h a b", a=na)
                        ins = V.tensor_tensor(d, s0, s1, ALU.add)
                        off += na * nb
                    ins.then_inc(q.v_done, done.up())
                v.wait_ge(q.v_done, done.n)

            def settled(t, h, k):
                v.wait_ge(q.sel_step, h * steps + (t * EH * steps + k))
                v.sem_inc(q.turn_v, 1)

            def best_pairs(t, h):
                R = slice(0, P if t < 4 else DEC)
                V.tensor_copy(pairs[R, :], cand[R, bass.ds(h * VALS, VALS)]).then_inc(q.sel_step, 1)
                settled(t, h, 1)
                V.max(best[R, 0:8], pairs[R, :]).then_inc(q.sel_step, 1)
                settled(t, h, 2)
                V.match_replace(pairs_left[R, :], best[R, 0:8], pairs[R, :], -3e38).then_inc(q.sel_step, 1)
                V.max_index(sel[R, 0:8], best[R, 0:8], pairs[R, :]).then_inc(q.sel_step, 1)
                settled(t, h, 4)
                V.max(best[R, 8:16], pairs_left[R, :]).then_inc(q.sel_step, 1)
                settled(t, h, 5)
                V.max_index(sel[R, 8:16], best[R, 8:16], pairs_left[R, :]).then_inc(q.sel_step, 1)
                V.tensor_scalar(gate[R, bass.ds(h * 16 + t * P, 16)], best[R, :], best[R, 0:1], None, ALU.subtract).then_inc(q.sel_step, 1)

            def pair_experts(t, h):
                R = slice(0, P if t < 4 else DEC)
                shape = [R.stop, 16, VALS]
                settled(t, h, 7)
                V.tensor_copy(sel_f[R, :], sel[R, :]).then_inc(q.sel_step, 1)
                settled(t, h, 8)
                V.tensor_tensor(onehot[R], sel_f[R, :].unsqueeze(2).to_broadcast(shape), const("iota")[R, :].unsqueeze(1).to_broadcast(shape),
                                ALU.is_equal).then_inc(q.sel_step, 1)
                settled(t, h, 9)
                V.tensor_tensor(onehot[R], onehot[R], cidx[R, bass.ds(h * VALS, VALS)].unsqueeze(1).to_broadcast(shape),
                                ALU.mult).then_inc(q.sel_step, 1)
                settled(t, h, 10)
                V.tensor_reduce(expert[R, :], onehot[R], AX.X, ALU.add).then_inc(q.sel_step, 1)
                settled(t, h, 11)
                V.tensor_scalar(eid[R, bass.ds(h * 16 + t * P, 16)], expert[R, :], ebase[R, :], None, ALU.add).then_inc(q.sel_step, 1)

            def selected(t):
                v.wait_ge(q.sel_step, steps * EH * (t + 1))
                v.sem_inc(q.eid_ready, 1)
                v.sem_inc(q.bests, 1)

            def gates(t):
                R = slice(0, P if t < 4 else DEC)
                gt3 = gate[R, tok(t)].rearrange("p (h a) -> p h a", h=EH)
                v.wait_ge(q.gexp, t + 1)
                V.tensor_reduce(gsum[R, :], gt3, AX.X, ALU.add).then_inc(q.v_done, done.up())
                v.wait_ge(q.v_done, done.n)
                V.reciprocal(gsum[R, :], gsum[R, :]).then_inc(q.v_done, done.up())
                v.wait_ge(q.v_done, done.n)
                V.tensor_tensor(gt3, gt3, gsum[R, :].unsqueeze(2).to_broadcast([R.stop, EH, 16]), ALU.mult).then_inc(q.gate_done, 1)
                v.wait_ge(q.gate_done, t + 1)

            def expert_dots(t, group):
                rows = xb[:, t, :] if t < 4 else xs
                for k in range(4):
                    v.wait_ge(q.u_loaded[k], (group + l * GROUPS + 1) * 16)
                    V.scalar_tensor_tensor(ring[k], ring[k], 1.0, rows, ALU.mult, ALU.mult,
                                           accum_out=dots[:, bass.ds(group * 4 + k, 1)]).then_inc(q.u_free, 1)

            for h in range(EH):
                for s in range(2):
                    best_keys(2 * h + s)
                numbers([0], slice(h, h + 1))
                pair_sums(0, h, h + 1)
                best_pairs(0, h)
                pair_experts(0, h)
            selected(0)
            gates(0)
            v.sem_inc(q.u_free, 4)
            v.sem_inc(q.v_free, 4)
            numbers([1, 2, 3, 4], slice(0, EH))
            for t in range(NT):
                if t < 4:
                    pair_sums(t + 1)
                    with v.Fori(0, EH) as h:
                        for s in range(4):
                            expert_dots(t, h * 4 + (t * (P // 4) + s))
                            if s == 0:
                                best_pairs(t + 1, h)
                            if s == 2:
                                pair_experts(t + 1, h)
                else:
                    v.wait_ge(q.spread_x, 64)
                    with v.Fori(0, DEC // 4) as g:
                        expert_dots(t, g + t * (P // 4))
                v.drain().then_inc(q.dots_ready, 1)
                if t < 4:
                    selected(t + 1)
                ne = P if t < 4 else DEC
                if t == 4:
                    v.wait_ge(q.spread_g, 64)
                v.wait_ge(q.act_ready, t + 1)
                V.tensor_tensor(wts[:, t * P:t * P + ne], act[:, 0:ne], gate[:, tok(t)] if t < 4 else gate_s, ALU.mult).then_inc(q.wts_ready, 1)
                if t < 4:
                    gates(t + 1)
                if t >= 1:
                    add_experts(v, t - 1)
            add_experts(v, NT - 1)
            v.wait_ge(q.wts_ready, NT)
            V.tensor_scalar(ebase, ebase, float(EXPERTS), None, ALU.add)

        def add_experts(v, t):
            q = peer
            R = slice(0, P if t < 4 else DEC)
            v.wait_ge(q.acc_bank, t + 1)
            b = 2 * (t % 2)
            V.tensor_tensor(x[R, t, :], x[R, t, :], ps[R, b:b + 2, :].rearrange("p b n -> p (b n)"), ALU.add).then_inc(q.acc_read, 1)

        @block.vector
        def _(v):
            V.memset(x[:, 4, :], 0.0)
            V.memset(zeros, 0.0)
            V.memset(ebase, 0.0)
            V.memset(lb_all, 0.0).then_inc(start_set, 1)
            v.wait_ge(start_set, 1)
            V.memset(lb_all[:, 0, 0:2], -1e30)
            V.memset(lb_all[:, 0, 4:6], 1e30)
            v.wait_ge(start_loaded, 7 * 16)
            V.tensor_tensor(lb_t[:, 0:2], lb_rows[:, 1, :], lb_rows[:, 0, :], ALU.subtract).then_inc(start_set, 1)
            v.wait_ge(start_set, 3)
            V.scalar_tensor_tensor(lb_all[:, 1, 0:2], lb_t[:, 0:2], 0.0, lb_t[:, 2:4], ALU.min, ALU.subtract).then_inc(start_set, 1)
            v.wait_ge(start_set, 4)
            V.tensor_tensor(lb_all[:, 1, 2:4], lb_all[:, 1, 0:2], lb_t[:, 0:2], ALU.subtract)
            V.tensor_scalar(lb_all[:, 1, 4:6], lb_all[:, 1, 0:2], -1.0, None, ALU.mult).then_inc(start_set, 1)
            v.wait_ge(start_set, 5)
            with v.Fori(0, DEPTH) as l:
                project_vector(v, l)
                meet(v, 1)
                hgrn_vector(v)
                meet(v, 2)
                gdn_vector(v)
                meet(v, 3)
                mla_vector(v)
                meet(v, 4)
                out_vector(v)
                meet(v, 5)
                peer_vector(v, l)
                meet(v, 6)
                next_layer(v, l)

        A_ = nc.scalar
        eps = const("eps")

        def inv_root(a, dst, src, m, done_sem, done, last):
            A_.activation(dst, src, ACT.Ln, bias=eps[0:dst.shape[0], :], scale=1.0 / m).then_inc(done_sem, done.up())
            a.wait_ge(done_sem, done.n)
            A_.activation(dst, dst, ACT.Exp, scale=-0.5).then_inc(last, 1)

        def softplus_tail(a, q, done, dst, src, last, bias=0.0):
            A_.activation(dst, src, ACT.Abs, bias=bias).then_inc(q.a_done, done.up())
            a.wait_ge(q.a_done, done.n)
            A_.activation(dst, dst, ACT.Exp, scale=-1.0).then_inc(q.a_done, done.up())
            a.wait_ge(q.a_done, done.n)
            return A_.activation(dst, dst, ACT.Ln, bias=1.0).then_inc(last, 1)

        def norm_scalar(a, q, done):
            for t in range(NT):
                A_.activation(ps[:, 6:8, :].rearrange("p b n -> p (b n)"), x[:, t, :], ACT.Square,
                              accum_out=sumsq[:, t:t + 1]).then_inc(q.a_done, done.up())
                a.wait_ge(q.a_done, done.n)
            inv_root(a, rs, sumsq, D, q.a_done, done, q.rs_ready)
            for t in range(NT):
                a.wait_ge(q.h_banks, t + 1)
                A_.copy(hT[:, 4:8, tok(t)], ps[:, 2 * (t % 2) + 1, :].rearrange("p (c t) -> p c t", c=4)).then_inc(q.h_copy_a, 1)

        def project_scalar(a):
            q, done = project, Count()
            norm_scalar(a, q, done)

            def silu_conv(j):
                a.wait_ge(q.y_ready, j + 1)
                A_.activation(conv[:, j, 0:SEQ], conv_y[j % 2][:, 0:SEQ], ACT.Silu)
                A_.activation(conv[:, j, SEQ:TV], conv_y[j % 2][:, 515:547], ACT.Silu).then_inc(q.silu_done, 1)

            for j in range(16):
                a.wait_ge(q.col_bank, j + 1)
                main, rest = ps[:, j % 2, :], ps[:, 2 + j % 2, 0:DEC]
                if j < NJ:
                    if j >= 2:
                        a.wait_ge(q.y_ready, j - 1)
                    A_.copy(raw[j % 2][:, 3:515], main)
                    A_.copy(raw[j % 2][:, 518:550], rest).then_inc(q.raw_ready, 2)
                    a.wait_ge(q.raw_ready, 2 * (j + 1))
                    a.sem_inc(q.col_read, 1)
                else:
                    dst = (zf if j < 14 else qh)[:, (j % 2) * TP:(j % 2) * TP + TV]
                    f = ACT.Copy if j < 14 else ACT.Silu
                    A_.activation(dst[:, 0:SEQ], main, f)
                    A_.activation(dst[:, SEQ:TV], rest, f).then_inc(q.col_read, 1)
                if 1 <= j <= NJ:
                    silu_conv(j - 1)
            for g in (0, 2):
                _, m, col, _ = TM_GROUPS[g]
                for t in range(NT):
                    k = g * NT + t
                    a.wait_ge(q.tm_bank, k + 1)
                    A_.activation(tm[:, t, col:col + m], ps[:, 4 + k % 4, 0:m], ACT.Silu).then_inc(q.tm_read_a, 1)

        def hgrn_scalar(a):
            q, done = hgrn, Count()
            softplus_tail(a, q, done, E, zf, q.e1)
            a.wait_ge(q.nlsig, 1)
            for r in range(2):
                s = slice(r * TP, (r + 1) * TP)
                ins = A_.activation(zf[:, s], QE[:, s], ACT.Exp, bias=lb[:, 2 + r:3 + r])
            ins.then_inc(q.k_ready, 1)
            a.wait_ge(q.bprime, 1)
            for r in range(2):
                s = slice(r * TP, (r + 1) * TP)
                ins = A_.activation(E[:, s], B[:, s], ACT.Abs, bias=lb[:, 4 + r:5 + r])
            ins.then_inc(q.a_done, done.up())
            a.wait_ge(q.a_done, done.n)
            A_.activation(E, E, ACT.Exp, scale=-1.0).then_inc(q.a_done, done.up())
            a.wait_ge(q.a_done, done.n)
            A_.activation(E, E, ACT.Ln, bias=1.0).then_inc(q.lf, 1)
            for lv in range(1, 7):
                a.wait_ge(q.diff, lv)
                A_.activation(E, E, ACT.Abs).then_inc(q.a_done, done.up())
                a.wait_ge(q.a_done, done.n)
                A_.activation(E, E, ACT.Exp, scale=-1.0).then_inc(q.ediff, 1)
            a.wait_ge(q.diff, 7)
            A_.activation(E, B, ACT.Exp).then_inc(q.eb, 1)
            A_.activation(ebl.rearrange("p (n w) -> p n w", w=1), B.rearrange("p (n w) -> p n w", w=C)[:, :, C - 1:C], ACT.Exp).then_inc(q.ebl_ready, 1)
            A_.activation(KE, KE, ACT.Exp).then_inc(q.ed, 1)
            for t in range(NT):
                a.wait_ge(q.o_bank, 2 * (t + 1))
                if t >= 1:
                    a.wait_ge(q.o_done, t)
                A_.activation(hosq, ps[:, 1 + t % 2, 0:256], ACT.Square).then_inc(q.osq, 1)
                a.wait_ge(q.oss, t + 1)
                inv_root(a, sr[:, 0:4], ss[:, 0:4], C, q.a_done, done, q.ors)

        def gdn_scalar(a):
            q, done = gdn, Count()
            ba = tm[:, :, T_BA:T_BA + 8]
            A_.activation(beta.rearrange("p (t h) -> p t h", t=NT), ba[:, :, 0:4], ACT.Exp, scale=-1.0).then_inc(q.bexp, 1)
            A_.activation(gdn_par[:, 0:4], gdn_par[:, 0:4], ACT.Exp).then_inc(q.nega, 1)
            a.wait_ge(q.alpha, 1)
            softplus_tail(a, q, done, gt, gg, q.soft)

            def square(j):
                if j >= 2:
                    a.wait_ge(q.sum_bank, j - 1)
                A_.activation(gsq[j % 2], conv[:, j, 0:TV], ACT.Square).then_inc(q.square_ready, 1)

            square(0)
            square(1)
            for j in range(8):
                a.wait_ge(q.sum_bank, j + 1)
                if j >= 2:
                    a.wait_ge(q.qk_ready, j - 1)
                A_.activation(grs[j % 2][:, 0:SEQ], ps[:, j % 2, :], ACT.Ln, bias=eps)
                A_.activation(grs[j % 2][:, SEQ:TV], ps[:, 2 + j % 2, 0:DEC], ACT.Ln, bias=eps).then_inc(q.sum_read, 1)
                a.wait_ge(q.sum_read, j + 1)
                A_.activation(grs[j % 2], grs[j % 2], ACT.Exp, scale=-0.5).then_inc(q.norm_ready, 1)
                if j < 6:
                    square(j + 2)
            a.wait_ge(q.gates_bank, 1)
            A_.activation(egc, ps[:, 4, 0:gate_n], ACT.Exp)
            A_.activation(erest, ps[:, 4, gate_n:2 * gate_n], ACT.Exp)
            A_.activation(egl, ps[:, 4, 2 * gate_n:4 * gate_n], ACT.Exp).then_inc(q.gexp_ready, 1)

            def decays(t):
                a.wait_ge(q.diff_ready, t + 1)
                A_.activation(EG, ps[:, 0, :], ACT.Exp).then_inc(q.eg_ready, 1)
                A_.activation(DT, DT, ACT.Exp).then_inc(q.edt_ready, 1)
                a.wait_ge(q.at_bank, t + 1)
                A_.copy(ATF, ps[:, 1, :]).then_inc(q.atf_ready, 1)

            def level(t, lv):
                a.wait_ge(q.y_bank, 5 * t + lv + 1)
                A_.copy(Y, ps[:, 2, :]).then_inc(q.y_ready, 1)

            decays(0)
            for lv in range(5):
                level(0, lv)
            for t in range(NT):
                more = t + 1 < NT
                a.wait_ge(q.w_bank, t + 1)
                A_.activation(NW, ps[:, 2, :], ACT.Copy, scale=-1.0).then_inc(q.w_ready, 1)
                if more:
                    decays(t + 1)
                a.wait_ge(q.o_bank, 2 * (t + 1))
                if t >= 1:
                    a.wait_ge(q.o_done, t)
                A_.activation(OSQ, ps[:, 4, :], ACT.Square).then_inc(q.osq, 1)
                if more:
                    level(t + 1, 0)
                a.wait_ge(q.oss, t + 1)
                inv_root(a, sr[:, 0:4], ss[:, 0:4], P, q.a_done, done, q.ors)
                if more:
                    for lv in range(1, 5):
                        level(t + 1, lv)

        def mla_scalar(a):
            q, done = mla, Count()
            A_.activation(csq, tm[:, :, T_C:T_C + 416], ACT.Square).then_inc(q.csq, 1)
            a.wait_ge(q.css, 1)
            for k, m in enumerate((256, 128, 32)):
                ins = A_.activation(sr[:, 5 * k:5 * k + 5], ss[:, 5 * k:5 * k + 5], ACT.Ln, bias=eps, scale=1.0 / m)
            ins.then_inc(q.a_done, done.up())
            a.wait_ge(q.a_done, done.n)
            A_.activation(sr[:, 0:15], sr[:, 0:15], ACT.Exp, scale=-0.5).then_inc(q.crs, 1)
            for b in range(6):
                a.wait_ge(q.lat_bank, b + 1)
                m = 512 if b < 5 else 2 * P + DEC
                A_.copy(latT[:, b * 512:b * 512 + m], ps[:, 7 * (b % 2), 0:m]).then_inc(q.lat_ready, 1)
            for i, (kind, tiles) in enumerate(mla_items):
                U, R = len(tiles), slice(0, DEC if tiles == (12,) else P)
                bank = ps[R, A_BANK[i]:A_BANK[i] + U, :]
                a.wait_ge(q.a_bank, i + 1)
                if kind == "key":
                    kv = bank.rearrange("p u (h n) -> p u h n", h=4)
                    sq = mla_sq[R, 0:256 * U].rearrange("p (u h n) -> p u h n", u=U, h=4)
                    A_.activation(sq, kv[:, :, :, 0:64], ACT.Square).then_inc(q.sq, 1)
                    n = tiles[0]
                    dst = Vp[R, n:n + U, :] if n < 4 else Vs[R, n - 4:n - 4 + U, :]
                    A_.copy(dst.rearrange("p u (h n) -> p u h n", h=4), kv[:, :, :, 64:128]).then_inc(q.v_ready, 1)
                    a.wait_ge(q.ssum, i + 1)
                    inv_root(a, mla_sr[R, 0:4 * U], mla_ss[R, 0:4 * U], 64, q.a_done, done, q.rs)
                else:
                    A_.activation(mla_sq[:, 0:384 * U].rearrange("p (u n) -> p u n", u=U), bank[:, :, 0:384], ACT.Square).then_inc(q.sq, 1)
                    a.wait_ge(q.ssum, i + 1)
                    A_.activation(mla_sr[:, 0:4 * U], mla_ss[:, 0:4 * U], ACT.Ln, bias=eps, scale=1.0 / 64)
                    A_.activation(mla_sr[:, 4 * U:8 * U], mla_ss[:, 4 * U:8 * U], ACT.Ln, bias=eps, scale=1.0 / 32).then_inc(q.a_done, done.up())
                    a.wait_ge(q.a_done, done.n)
                    A_.activation(mla_sr[:, 0:8 * U], mla_sr[:, 0:8 * U], ACT.Exp, scale=-0.5).then_inc(q.rs, 1)
                    if i > KEY_ITEMS:
                        keep_queries(a, i - 1)
            keep_queries(a, 9)

            def turn_probs(k):
                a.wait_ge(q.pT_bank, k + 1)
                if k >= 2:
                    a.wait_ge(q.av_done, k - 1)
                m, c0 = P * (k // 4 + 1), 512 * (k % 2)
                A_.copy(pT[:, c0:c0 + m], ps[:, k % 2, 0:m]).then_inc(q.pT_ready, 1)

            for k in range(16):
                a.wait_ge(q.nm, k + 1)
                m, c0 = P * (k // 4 + 1), 512 * (k % 2)
                A_.activation(pr[:, c0:c0 + m], ps[:, 4 + k % 4, 0:m], ACT.Exp, bias=mla_nm[:, k:k + 1], scale=SCALE,
                              accum_out=mla_sum[:, k:k + 1]).then_inc(q.p_ready, 1)
                if k >= 1:
                    turn_probs(k - 1)
            turn_probs(15)
            a.wait_ge(q.nm, 17)
            scores = ps[:, 5:8, :].rearrange("p b n -> p (b n)")[:, 0:PAST + DEC]
            A_.activation(pr, scores, ACT.Exp, bias=mla_nm[:, 16:17], scale=SCALE, accum_out=mla_sum[:, 16:17]).then_inc(q.p_ready, 1)
            a.wait_ge(q.pT_bank, 17)
            a.wait_ge(q.av_done, 16)
            A_.copy(pT[:, 0:1024], ps[:, 0:2, :].rearrange("p b n -> p (b n)"))
            A_.copy(pT[0:DEC, 1024:1152], ps[0:DEC, 2, 0:P]).then_inc(q.pT_ready, 1)

        def keep_queries(a, i):
            a.wait_ge(mla.t_bank, i + 1)
            tiles = mla_items[i][1]
            for u, t in enumerate(tiles):
                ins = A_.copy(QT[0:96, t], ps[0:96, B_BANK[i][u], :].rearrange("p (h n) -> p h n", h=4))
            ins.then_inc(mla.qT_ready, 1)

        def out_scalar(a):
            q = outp
            for t in range(NT):
                a.wait_ge(q.t_banks, t + 1)
                if t >= 2:
                    a.wait_ge(q.o_bank, 2 * (t - 1))
                A_.copy(mT[t % 2][:, 512:1024], ps[:, 2 * (t % 2) + 1, :]).then_inc(q.copy_a, 1)

        def peer_scalar(a):
            q, done = peer, Count()
            norm_scalar(a, q, done)
            for j in range(16):
                a.wait_ge(q.q_bank, j + 1)
                if j >= 2:
                    a.wait_ge(q.s_bank, j - 1)
                A_.copy(qT[j % 2][:, 0:SEQ], ps[:, j % 2, :])
                A_.copy(qT[j % 2][:, SEQ:TV], ps[:, 2 + j % 2, 0:DEC]).then_inc(q.q_ready, 1)
            def gate_exp(t):
                R = slice(0, P if t < 4 else DEC)
                a.wait_ge(q.bests, t + 1)
                A_.activation(gate[R, tok(t)], gate[R, tok(t)], ACT.Exp).then_inc(q.gexp, 1)

            gate_exp(0)
            for t in range(NT):
                m, ne = (P, P) if t < 4 else (DEC, DEC)
                a.wait_ge(q.dots_ready, t + 1)
                A_.activation(act[:, 0:ne], dots[:, t * P:t * P + ne], ACT.Gelu).then_inc(q.act_ready, 1)
                if t < 4:
                    gate_exp(t + 1)
                a.wait_ge(q.wts_ready, t + 1)
                place = ident if t < 4 else const("fold")
                with a.Fori(0, ne // 4) as g:
                    for k in range(4):
                        a.wait_ge(q.v_free, g * 4 + (t * P + k + 1))
                        a.sem_inc(q.a_done, 1)
                        A_.activation(diag[k][:, 0:m], place, ACT.Copy, scale=wts[:, bass.ds(g * 4 + (t * P + k), 1)]).then_inc(q.diag_ready, 1)

        @block.scalar
        def _(a):
            a.wait_ge(start_set, 2)
            A_.activation(lb_t[:, 4:6], lb_t[:, 0:2], ACT.Abs).then_inc(start_act, 1)
            a.wait_ge(start_act, 1)
            A_.activation(lb_t[:, 4:6], lb_t[:, 4:6], ACT.Exp, scale=-1.0).then_inc(start_act, 1)
            a.wait_ge(start_act, 2)
            A_.activation(lb_t[:, 2:4], lb_t[:, 4:6], ACT.Ln, bias=1.0).then_inc(start_set, 1)
            a.wait_ge(start_loaded, 7 * 16)
            with a.Fori(0, DEPTH) as l:
                project_scalar(a)
                meet(a, 1)
                hgrn_scalar(a)
                meet(a, 2)
                gdn_scalar(a)
                meet(a, 3)
                mla_scalar(a)
                meet(a, 4)
                out_scalar(a)
                meet(a, 5)
                peer_scalar(a)
                meet(a, 6)
                next_layer(a, l)

        G = nc.gpsimd

        def hgrn_pool(p):
            q = hgrn
            for t in range(NT):
                g3 = tm[:, t, T_G:T_G + 256].rearrange("p (h n) -> p h n", h=4)
                ins = G.tensor_tensor(g3, g3, per_head(hgrn_gain), ALU.mult)
            ins.then_inc(q.gg_ready, 1)
            for lv in range(1, 7):
                p.wait_ge(q.ediff, lv)
                if lv >= 2:
                    p.wait_ge(q.lev_bank, lv * NT)
                G.tensor_tensor(KE, zf, E, ALU.mult).then_inc(q.ke_ready, 1)

        def gdn_pool(p):
            q = gdn

            def h3(ap):
                return ap.rearrange("p (h n) -> p h n", h=GH)

            p.wait_ge(q.gate_ready, 1)
            p.wait_ge(q.qk_ready, 8)
            for t in range(NT):
                if t >= 1:
                    p.wait_ge(q.row_bank, t)
                G.tensor_tensor(h3(ug), per_head(upto), heads(gg[:, t * GH:(t + 1) * GH]), ALU.mult).then_inc(q.ug_ready, 1)
                p.wait_ge(q.eg_ready, t + 1)
                G.tensor_tensor(h3(QG[t % 2]), conv[:, 0:4, tok(t)], h3(EG), ALU.mult).then_inc(q.qg_ready, 1)
                p.wait_ge(q.atf_ready, t + 1)
                for lv in range(5):
                    k = 5 * t + lv
                    if k >= 2:
                        p.wait_ge(q.y_bank, k - 1)
                    G.tensor_tensor(h3(AM[lv % 2]), h3(ATF), per_head(const(f"half{2 << lv}")), ALU.mult).then_inc(q.am_ready, 1)
                if t >= 1:
                    p.wait_ge(q.o_done, t)
                G.tensor_tensor(h3(ZG), h3(tm[:, t, 0:512]), per_head(gdn_gain), ALU.mult).then_inc(q.zg_ready, 1)

        def peer_pool(p):
            q = peer
            tu = i.peer_expert_u.rearrange("l e d -> (l e) d")
            tv = i.peer_expert_v.rearrange("l e d -> (l e) d")

            def gathers(t, g, side, ids, free, loaded, table, ids_ready, slot0):
                numbers = eid[:, bass.ds(g * 8 + (t * P + 4 * side), 4)] if t < 4 else eid_s[:, bass.ds(g * 8 + 4 * side, 4)]
                p.wait_ge(free, g * 8 + (t * P + 4 * side + 1))
                p.sem_inc(q.p_done, 1)
                G.tensor_copy(ids[side], numbers).then_inc(ids_ready, 1)
                p.wait_ge(ids_ready, g * 2 + (t * (P // 4) + side + 1))
                p.sem_inc(q.p_done, 1)
                for k in range(4):
                    if k >= 1:
                        p.wait_ge(free, g * 8 + (t * P + 4 * side + k + 1))
                        p.sem_inc(q.p_done, 1)
                    G.indirect_dma_start(ring[slot0 + k], None, table,
                                         bass.IndirectOffsetOnAxis(ap=ids[side][:, k:k + 1], axis=0)).then_inc(loaded[k], 16)

            def gather_u(t, g):
                for side in range(2):
                    gathers(t, g, side, uidx, q.u_free, q.u_loaded, tu, q.ids_u, 0)

            def gather_v(t, g):
                for side in range(2):
                    gathers(t, g, side, vidx, q.v_free, q.v_loaded, tv, q.ids_v, 4)

            p.wait_ge(q.eid_ready, 1)
            with p.Fori(0, P // 8) as g:
                gather_u(0, g)
            for t in range(4):
                p.wait_ge(q.eid_ready, t + 2)
                if t < 3:
                    with p.Fori(0, P // 8) as g:
                        for side in range(2):
                            gathers(t, g, side, vidx, q.v_free, q.v_loaded, tv, q.ids_v, 4)
                            gathers(t + 1, g, side, uidx, q.u_free, q.u_loaded, tu, q.ids_u, 0)
                else:
                    p.wait_ge(q.spread_e, 64)
                    with p.Fori(0, DEC // 8) as g:
                        for side in range(2):
                            gathers(3, g, side, vidx, q.v_free, q.v_loaded, tv, q.ids_v, 4)
                            gathers(4, g, side, uidx, q.u_free, q.u_loaded, tu, q.ids_u, 0)
                    with p.Fori(DEC // 8, P // 8) as g:
                        gather_v(3, g)
            with p.Fori(0, DEC // 8) as g:
                gather_v(4, g)

        @block.gpsimd
        def _(p):
            p.wait_ge(start_loaded, 7 * 16)
            with p.Fori(0, DEPTH) as l:
                meet(p, 1)
                hgrn_pool(p)
                meet(p, 2)
                gdn_pool(p)
                meet(p, 3)
                meet(p, 4)
                meet(p, 5)
                peer_pool(p)
                meet(p, 6)
                next_layer(p, l)


_INS = [
    'x_prompt', 'x_sample', 'state_gdn', 'state_gdn_conv', 'state_hgrn', 'cache_mla_ckv', 'cache_mla_kpe', 'norm_mix', 'w_in',
    'conv_w', 'gdn_a_log', 'gdn_dt_bias', 'gdn_norm', 'hgrn_lower_bounds', 'hgrn_norm', 'mla_q_a_norm', 'mla_w_q_b',
    'mla_kv_a_norm', 'mla_w_kv_b', 'mla_q_norm_nope', 'mla_q_norm_rope', 'mla_k_norm_nope', 'mla_k_norm_rope', 'w_out',
    'norm_ffn', 'peer_w_query', 'peer_sub_keys', 'peer_expert_u', 'peer_expert_v']
_OUTS = [
    ('y_prompt', (1, SEQ, D)), ('y_sample', (1, DEC, D)),
    ('p_gdn', (DEPTH, 1, 4, 128, 128)), ('p_conv', (DEPTH, 1, 3, QKV)), ('p_hgrn', (DEPTH, 1, 4, 64, 64)),
    ('p_ckv', (DEPTH, 1, SEQ, 128)), ('p_kpe', (DEPTH, 1, SEQ, 32)),
    ('s_gdn', (DEPTH, 1, 4, 128, 128)), ('s_conv', (DEPTH, 1, 3, QKV)), ('s_hgrn', (DEPTH, 1, 4, 64, 64)),
    ('s_ckv', (DEPTH, 1, DEC, 128)), ('s_kpe', (DEPTH, 1, DEC, 32))]


def kernel(**inputs):
    import concourse.bacc as _bacc
    from concourse.bass_utils import run_bass_kernel_spmd as _run

    nc = _bacc.Bacc("TRN2", target_bir_lowering=False, num_devices=1)
    arrays, ins, outs = {}, {}, {}
    for name in _INS:
        a = np.ascontiguousarray(inputs[name])
        arrays[f"in_{name}"] = a
        ins[name] = nc.dram_tensor(f"in_{name}", a.shape, mybir.dt.from_np(a.dtype), kind="ExternalInput").ap()
    table, at = constants()
    arrays["constants"] = table
    ins["constants"] = nc.dram_tensor("constants", table.shape, F32, kind="ExternalInput").ap()
    for name, shape in _OUTS:
        outs[name] = nc.dram_tensor(f"out_{name}", shape, F32, kind="ExternalOutput").ap()
    build(nc, type("Inputs", (), ins), type("Outputs", (), outs), at, table.shape[1])
    r = _run(nc, [arrays], core_ids=[0])
    return tuple(r.results[0][f"out_{name}"] for name, _ in _OUTS)
```
